# Optimizing a Trainium2 kernel written in Bass

```python
import math
import jax
import jax.numpy as jnp
from jax import lax
import numpy as np

D_MODEL = 1024
BATCH = 1
SEQ = 512
DEPTH = 2

N_MIXERS = 2
GDN_HEADS = 8
GDN_DK = 128
GDN_DV = 128
GDN_CONV = 4
GDN_CHUNK = 64
GDN_IN = 2 * GDN_HEADS * GDN_DK + 2 * GDN_HEADS * GDN_DV + 2 * GDN_HEADS
DSA_HEADS = 16
DSA_QK_DIM = 64
DSA_V_DIM = 64
DSA_Q_LORA = 256
DSA_KV_LORA = 256
IDX_HEADS = 8
IDX_DIM = 64
TOPK_MAX = 256
Q_BLOCK = 128
DSA_IN = DSA_Q_LORA + DSA_KV_LORA + IDX_DIM + IDX_HEADS
FFN_HIDDEN = -(-8 * D_MODEL // (3 * 256)) * 256
NORM_EPS = 1e-6
L2_EPS = 1e-6

kernel_name = "hybrid_gdn_dsa_sandwich_adaln_trunk"

def rms_norm(x, g):
    xf = x.astype(jnp.float32)
    y = xf * lax.rsqrt(jnp.mean(xf * xf, axis=-1, keepdims=True) + NORM_EPS)
    return y.astype(x.dtype) * g

def layer_norm(x, g, b):
    xf = x.astype(jnp.float32)
    mu = jnp.mean(xf, axis=-1, keepdims=True)
    var = jnp.mean(jnp.square(xf - mu), axis=-1, keepdims=True)
    return ((xf - mu) * lax.rsqrt(var + NORM_EPS)).astype(x.dtype) * g + b

def l2_normalize(x):
    return x * lax.rsqrt(jnp.sum(x * x, axis=-1, keepdims=True) + L2_EPS)

def causal_dwconv(u, w):
    K, C = w.shape
    return lax.conv_general_dilated(
        u.astype(jnp.float32), w.astype(jnp.float32)[:, None, :],
        window_strides=(1,), padding=[(K - 1, 0)],
        dimension_numbers=('NWC', 'WIO', 'NWC'), feature_group_count=C)

def chunk_gated_delta_rule(q, k, v, g, beta):
    B, S, H, DK = q.shape
    DV = v.shape[-1]
    C = GDN_CHUNK
    N = S // C

    def chunks(t):
        t = t.reshape(B, N, C, H, *t.shape[3:])
        return jnp.moveaxis(t, (1, 3), (0, 2))

    q, k, v, g, beta = chunks(q), chunks(k), chunks(v), chunks(g), chunks(beta)
    G = jnp.cumsum(g, axis=-1)
    pos = jnp.arange(C)
    lower = pos[:, None] >= pos[None, :]
    strict = pos[:, None] > pos[None, :]
    decay = jnp.exp(jnp.where(lower, G[..., :, None] - G[..., None, :], -jnp.inf))
    kb = k * beta[..., None]
    L = jnp.where(strict, jnp.einsum('nbhid,nbhjd->nbhij', kb, k) * decay, 0.0)
    A = L + jnp.eye(C, dtype=L.dtype)
    u = lax.linalg.triangular_solve(A, v * beta[..., None], left_side=True, lower=True)
    w = lax.linalg.triangular_solve(A, kb * jnp.exp(G)[..., None], left_side=True, lower=True)
    attn = jnp.einsum('nbhid,nbhjd->nbhij', q, k) * decay
    g_last = G[..., -1]
    q_g = q * jnp.exp(G)[..., None]
    k_g = k * jnp.exp(g_last[..., None] - G)[..., None]

    def step(state, xs):
        u_c, w_c, qg_c, kg_c, attn_c, gl_c = xs
        v_new = u_c - jnp.einsum('bhck,bhkv->bhcv', w_c, state)
        o_c = (jnp.einsum('bhck,bhkv->bhcv', qg_c, state)
               + jnp.einsum('bhij,bhjv->bhiv', attn_c, v_new))
        state = (state * jnp.exp(gl_c)[..., None, None]
                 + jnp.einsum('bhck,bhcv->bhkv', kg_c, v_new))
        return state, o_c

    state0 = jnp.zeros((B, H, DK, DV), jnp.float32)
    _, o = lax.scan(step, state0, (u, w, q_g, k_g, attn, g_last))
    return jnp.moveaxis(o, (0, 2), (1, 3)).reshape(B, S, H, DV)

def gdn_mixer(h, w_in, conv_w, a_log, dt_bias, norm_g, w_out):
    B, S, _ = h.shape
    H = GDN_HEADS
    HK = GDN_HEADS * GDN_DK
    HV = GDN_HEADS * GDN_DV
    proj = h @ w_in
    qkv, z, b_raw, a_raw = jnp.split(proj, [2 * HK + HV, 2 * HK + 2 * HV, 2 * HK + 2 * HV + H], axis=-1)
    qkv = jax.nn.silu(causal_dwconv(qkv, conv_w))
    q, k, v = jnp.split(qkv, [HK, 2 * HK], axis=-1)
    q = l2_normalize(q.reshape(B, S, H, GDN_DK)) * (GDN_DK ** -0.5)
    k = l2_normalize(k.reshape(B, S, H, GDN_DK))
    v = v.reshape(B, S, H, GDN_DV)
    beta = jax.nn.sigmoid(b_raw.astype(jnp.float32))
    g = -jnp.exp(a_log.astype(jnp.float32)) * jax.nn.softplus(
        a_raw.astype(jnp.float32) + dt_bias.astype(jnp.float32))
    o = chunk_gated_delta_rule(q, k, v, g, beta)
    o = rms_norm(o, norm_g) * jax.nn.silu(z.reshape(B, S, H, GDN_DV).astype(jnp.float32))
    return o.reshape(B, S, HV).astype(h.dtype) @ w_out

def dsa_mixer(h, w_in, q_norm_g, kv_norm_g, w_uq, w_uk, w_uv, w_qidx, kidx_ln_g, kidx_ln_b, w_out):
    B, S, _ = h.shape
    topk = min(TOPK_MAX, S // 4)
    proj = h @ w_in
    c_q, c_kv, k_idx, w_idx = jnp.split(
        proj, [DSA_Q_LORA, DSA_Q_LORA + DSA_KV_LORA, DSA_Q_LORA + DSA_KV_LORA + IDX_DIM], axis=-1)
    c_q = rms_norm(c_q, q_norm_g)
    c_kv = rms_norm(c_kv, kv_norm_g)
    q = (c_q @ w_uq).reshape(B, S, DSA_HEADS, DSA_QK_DIM)
    q_idx = (c_q @ w_qidx).reshape(B, S, IDX_HEADS, IDX_DIM)
    k_idx = layer_norm(k_idx, kidx_ln_g, kidx_ln_b)
    w_idx = w_idx * ((IDX_HEADS ** -0.5) * (IDX_DIM ** -0.5))
    nb = S // Q_BLOCK

    def blocks(t):
        return jnp.swapaxes(t.reshape(B, nb, Q_BLOCK, *t.shape[2:]), 0, 1)

    starts = jnp.arange(nb, dtype=jnp.int32) * Q_BLOCK
    key_pos = jnp.arange(S, dtype=jnp.int32)

    def attend_block(args):
        q_b, qi_b, wi_b, t0 = args
        t = t0 + jnp.arange(Q_BLOCK, dtype=jnp.int32)
        logits = jnp.einsum('bqhd,bsd->bqhs', qi_b, k_idx).astype(jnp.float32)
        score = jnp.einsum('bqh,bqhs->bqs', wi_b.astype(jnp.float32), jax.nn.relu(logits))
        score = jnp.where(key_pos[None, None, :] <= t[None, :, None], score, -jnp.inf)
        _, idx = lax.top_k(score, topk)
        valid = idx <= t[None, :, None]
        kv_sel = jax.vmap(lambda kv, i: kv[i])(c_kv, idx)
        q_lat = jnp.einsum('bqhd,hdc->bqhc', q_b, w_uk)
        s = jnp.einsum('bqhc,bqkc->bqhk', q_lat, kv_sel).astype(jnp.float32) * (DSA_QK_DIM ** -0.5)
        s = jnp.where(valid[:, :, None, :], s, -jnp.inf)
        p = jax.nn.softmax(s, axis=-1).astype(kv_sel.dtype)
        o_lat = jnp.einsum('bqhk,bqkc->bqhc', p, kv_sel)
        o = jnp.einsum('bqhc,hcv->bqhv', o_lat, w_uv)
        return o.reshape(B, Q_BLOCK, DSA_HEADS * DSA_V_DIM)

    o = lax.map(attend_block, (blocks(q), blocks(q_idx), blocks(w_idx), starts))
    o = jnp.swapaxes(o, 0, 1).reshape(B, S, DSA_HEADS * DSA_V_DIM)
    return o @ w_out

def swiglu(h, w_in, w_out):
    gate, up = jnp.split(h @ w_in, 2, axis=-1)
    return (jax.nn.silu(gate) * up) @ w_out

def _normal(key, shape, fan_in, gain=1.0):
    return jax.random.normal(key, shape, jnp.float32) * (gain * fan_in ** -0.5)

def setup_inputs(seed: int = 0) -> dict:
    key = jax.random.key(seed)
    ks = jax.random.split(key, 23)
    D = D_MODEL
    n_gdn = (DEPTH + N_MIXERS - 1) // N_MIXERS
    n_dsa = DEPTH // N_MIXERS
    HK = GDN_HEADS * GDN_DK
    HV = GDN_HEADS * GDN_DV
    nrm = lambda k, s: jax.random.normal(k, s, jnp.float32)
    x = nrm(ks[0], (BATCH, SEQ, D))
    c = nrm(ks[1], (BATCH, D))
    ada_w = _normal(ks[2], (DEPTH, D, 6 * D), D, 0.5)
    ada_b = 0.02 * nrm(ks[3], (DEPTH, 6 * D))
    norm_g = 1.0 + 0.05 * nrm(ks[4], (DEPTH, 4, D))
    ffn_w_in = _normal(ks[5], (DEPTH, D, 2 * FFN_HIDDEN), D)
    ffn_w_out = _normal(ks[6], (DEPTH, FFN_HIDDEN, D), FFN_HIDDEN)
    gdn_w_in = _normal(ks[7], (n_gdn, D, GDN_IN), D)
    gdn_conv_w = _normal(ks[8], (n_gdn, GDN_CONV, 2 * HK + HV), GDN_CONV)
    gdn_a_log = jnp.log(jax.random.uniform(ks[9], (n_gdn, GDN_HEADS), jnp.float32, 1.0, 16.0))
    dt = jnp.exp(jax.random.uniform(ks[10], (n_gdn, GDN_HEADS), jnp.float32,
                                    math.log(1e-3), math.log(1e-1)))
    gdn_dt_bias = dt + jnp.log(-jnp.expm1(-dt))
    gdn_norm_g = 1.0 + 0.05 * nrm(ks[11], (n_gdn, GDN_DV))
    gdn_w_out = _normal(ks[12], (n_gdn, HV, D), HV)
    dsa_w_in = _normal(ks[13], (n_dsa, D, DSA_IN), D)
    dsa_q_norm_g = 1.0 + 0.05 * nrm(ks[14], (n_dsa, DSA_Q_LORA))
    dsa_kv_norm_g = 1.0 + 0.05 * nrm(ks[15], (n_dsa, DSA_KV_LORA))
    dsa_w_uq = _normal(ks[16], (n_dsa, DSA_Q_LORA, DSA_HEADS * DSA_QK_DIM), DSA_Q_LORA)
    dsa_w_uk = _normal(ks[17], (n_dsa, DSA_HEADS, DSA_QK_DIM, DSA_KV_LORA), DSA_KV_LORA)
    dsa_w_uv = _normal(ks[18], (n_dsa, DSA_HEADS, DSA_KV_LORA, DSA_V_DIM), DSA_KV_LORA)
    dsa_w_qidx = _normal(ks[19], (n_dsa, DSA_Q_LORA, IDX_HEADS * IDX_DIM), DSA_Q_LORA)
    dsa_kidx_ln_g = 1.0 + 0.05 * nrm(ks[20], (n_dsa, IDX_DIM))
    dsa_kidx_ln_b = 0.02 * nrm(ks[21], (n_dsa, IDX_DIM))
    dsa_w_out = _normal(ks[22], (n_dsa, DSA_HEADS * DSA_V_DIM, D), DSA_HEADS * DSA_V_DIM)
    return {"x": x, "c": c, "ada_w": ada_w, "ada_b": ada_b, "norm_g": norm_g,
            "ffn_w_in": ffn_w_in, "ffn_w_out": ffn_w_out,
            "gdn_w_in": gdn_w_in, "gdn_conv_w": gdn_conv_w, "gdn_a_log": gdn_a_log,
            "gdn_dt_bias": gdn_dt_bias, "gdn_norm_g": gdn_norm_g, "gdn_w_out": gdn_w_out,
            "dsa_w_in": dsa_w_in, "dsa_q_norm_g": dsa_q_norm_g, "dsa_kv_norm_g": dsa_kv_norm_g,
            "dsa_w_uq": dsa_w_uq, "dsa_w_uk": dsa_w_uk, "dsa_w_uv": dsa_w_uv,
            "dsa_w_qidx": dsa_w_qidx, "dsa_kidx_ln_g": dsa_kidx_ln_g,
            "dsa_kidx_ln_b": dsa_kidx_ln_b, "dsa_w_out": dsa_w_out}

def reference(x, c, ada_w, ada_b, norm_g, ffn_w_in, ffn_w_out,
              gdn_w_in, gdn_conv_w, gdn_a_log, gdn_dt_bias, gdn_norm_g, gdn_w_out,
              dsa_w_in, dsa_q_norm_g, dsa_kv_norm_g, dsa_w_uq, dsa_w_uk, dsa_w_uv,
              dsa_w_qidx, dsa_kidx_ln_g, dsa_kidx_ln_b, dsa_w_out):
    c_act = jax.nn.silu(c)
    for layer in range(DEPTH):
        mod = c_act @ ada_w[layer] + ada_b[layer]
        sh_m, sc_m, ga_m, sh_f, sc_f, ga_f = [m[:, None, :] for m in jnp.split(mod, 6, axis=-1)]
        h = rms_norm(x, norm_g[layer, 0]) * (1.0 + sc_m) + sh_m
        j = layer // N_MIXERS
        if layer % N_MIXERS == 0:
            y = gdn_mixer(h, gdn_w_in[j], gdn_conv_w[j], gdn_a_log[j], gdn_dt_bias[j],
                          gdn_norm_g[j], gdn_w_out[j])
        else:
            y = dsa_mixer(h, dsa_w_in[j], dsa_q_norm_g[j], dsa_kv_norm_g[j], dsa_w_uq[j],
                          dsa_w_uk[j], dsa_w_uv[j], dsa_w_qidx[j], dsa_kidx_ln_g[j],
                          dsa_kidx_ln_b[j], dsa_w_out[j])
        x = x + (1.0 + ga_m) * rms_norm(y, norm_g[layer, 1])
        h = rms_norm(x, norm_g[layer, 2]) * (1.0 + sc_f) + sh_f
        y = swiglu(h, ffn_w_in[layer], ffn_w_out[layer])
        x = x + (1.0 + ga_f) * rms_norm(y, norm_g[layer, 3])
    return x


_drawn_inputs = setup_inputs


def setup_inputs(seed=0):
    import zlib

    import numpy as np

    out = dict(_drawn_inputs(seed))
    spreads = {}
    factors = {'dsa_kidx_ln_b': 3.846}
    for name, (base, spread) in spreads.items():
        noise = np.random.default_rng([zlib.crc32(name.encode()), seed]).standard_normal(out[name].shape)
        drawn = base * np.exp(spread * noise) if base else spread * noise
        out[name] = jnp.asarray(drawn.astype(out[name].dtype))
    for name, factor in factors.items():
        out[name] = (out[name] * factor).astype(out[name].dtype)
    return out
```

```python
from contextlib import ExitStack

import concourse.bass as bass
from concourse import mybir

F32 = mybir.dt.float32
F32R = mybir.dt.float32r
ALU = mybir.AluOpType
ACT = mybir.ActivationFunctionType
AX_X = mybir.AxisListType.X

P = 128
BIG = 1.0e30
TAKEN = -3.0e38
EPS = 1e-6


class Chain:

    def __init__(self, eng, sem):
        self.eng, self.sem, self.n, self.turns = eng, sem, 0, None

    def inc(self, ins):
        ins.then_inc(self.sem, 1)
        self.n += 1

    def wait(self):
        self.eng.wait_ge(self.sem, self.n if self.turns is None else self.turns + self.n)

    def __call__(self, ins):
        self.inc(ins)
        self.wait()


def repeat(eng, n, body, chain=None, first=0):
    start = chain.n if chain else 0
    body(first)
    per = chain.n - start if chain else 0
    rest = n - first - 1
    if rest < 3:
        for i in range(first + 1, n):
            body(i)
        return
    with eng.Fori(first + 1, n) as i:
        if chain:
            chain.turns = i * per - (first + 1) * per
        body(i)
    if chain:
        assert chain.n == start + 2 * per, (chain.n, start, per)
        chain.turns = None
        chain.n = start + per * (rest + 1)


def over_heads(square, n=4):
    return square.unsqueeze(1).to_broadcast([P, n, square.shape[-1]])


def along(cols, m=P):
    return cols.unsqueeze(2).to_broadcast([P, cols.shape[-1], m])


def build_trunk(nc, x, c, ada_w, ada_b, norm_g, ffn_w_in, ffn_w_out,
                gdn_w_in, gdn_conv_w, gdn_a_log, gdn_dt_bias, gdn_norm_g, gdn_w_out,
                dsa_w_in, dsa_q_norm_g, dsa_kv_norm_g, dsa_w_uq, dsa_w_uk, dsa_w_uv,
                dsa_w_qidx, dsa_kidx_ln_g, dsa_kidx_ln_b, dsa_w_out, out, stop=9):
    _, S, D = x.shape
    DC = D // P
    NB = S // P
    FC = ffn_w_out.shape[1] // P
    H = gdn_a_log.shape[1]
    CONV = gdn_conv_w.shape[1]
    QKV = gdn_conv_w.shape[2] // P
    HG = 4
    NG = H // HG
    LEVELS = 7
    AH, DH, LAT = dsa_w_uk.shape[1:]
    LC = LAT // P
    IH = dsa_w_qidx.shape[2] // DH
    SMALL = DH + IH
    TOPK = min(256, S // 4)
    PARTS = [8, 8, 6]
    assert S == 512 and D == 1024 and H == 8 and QKV == 24 and sum(PARTS) == FC
    assert LAT == 256 and DH == 64 and AH == 16 and IH == 8 and TOPK == P

    Q_GDN_IN = 0
    N_GDN_IN = (QKV + H) // 4
    Q_GDN_OUT = Q_GDN_IN + N_GDN_IN
    Q_FFN = [Q_GDN_OUT + 2, 0]
    N_FFN = sum(p // 2 + 2 for p in PARTS)
    Q_DSA = Q_FFN[0] + N_FFN
    Q_DSA_OUT = Q_DSA + 3
    Q_FFN[1] = Q_DSA_OUT + 2
    N_QUADS = Q_FFN[1] + N_FFN

    with ExitStack() as ctx:
        place = [(nc.sbuf_base + 31) // 32 * 32]

        def fixed(name, shape, dt=F32, at=None):
            size = 4
            for n in shape[1:]:
                size *= n
            size = (size + 31) // 32 * 32
            if at is None:
                at = place[0]
                place[0] += size
                assert place[0] <= nc.sbuf_usable_end, name
            t = nc.alloc_sbuf_tensor_at(name, shape, dt, offset=at)
            return t

        class Region:
            def __init__(self, at):
                self.at = at

            def __call__(self, name, shape, dt=F32):
                size = 4
                for n in shape[1:]:
                    size *= n
                t = fixed(name, shape, dt, at=self.at)
                self.at += (size + 31) // 32 * 32
                assert self.at <= nc.sbuf_usable_end, name
                return t

        ident = fixed("ident", [P, P])
        ones = fixed("ones", [P, P])
        upto = fixed("upto", [P, P])
        mask_l = fixed("mask_l", [P, P])
        mask_t = fixed("mask_t", [P, P])
        first_l = fixed("first_l", [P, P])
        first_t = fixed("first_t", [P, P])
        level_t = fixed("level_t", [P, LEVELS, P])
        causal = fixed("causal", [P, P])
        ln_gb = fixed("ln_gb", [P, 2, DH])
        half = fixed("half", [P, 64])
        VEC = DC + 8 * DC + 1 + 2 * LC
        vec_t = fixed("vec_t", [P, VEC])
        gnorm = vec_t[:, 9 * DC:9 * DC + 1]
        qn_g = vec_t[:, 9 * DC + 1:VEC].rearrange("p (a k) -> p a k", a=2)
        bias_t = fixed("bias_t", [P, 96])
        conv_t = fixed("conv_t", [P, CONV, QKV])
        mod = fixed("mod", [P, 96])
        c_act = fixed("c_act", [P, DC])
        coef = fixed("coef", [P, 2, 4, DC])
        raw = [fixed(f"raw{i}", [P, 8, 256]) for i in range(2)]
        w_hi = fixed("w_hi", [P, 4, 1024], F32R)
        w_lo = fixed("w_lo", [P, 4, 1024], F32R)
        x_t = fixed("x_t", [P, DC, S])
        small_at = place[0]
        diag = fixed("diag", [P, NB, P])
        tmp = fixed("tmp", [P, 3, S])
        var = fixed("var", [P, 32])
        rinv = fixed("rinv", [P, 32])
        ada_acc = fixed("ada_acc", [P, 512])
        h_base = place[0]
        h_hi = fixed("h_hi", [P, DC, S], F32R)
        h_lo = fixed("h_lo", [P, DC, S], F32R)
        ada_base = place[0]
        ada_in = [fixed(f"ada_in{i}", [P, 4, 512]) for i in range(2)]
        phase = place[0]

        pre = Region(phase)
        x_tok = pre("x_tok", [P, NB, D])
        row_vec = pre("row_vec", [VEC, P])
        row_bias = pre("row_bias", [96, P])
        row_conv = pre("row_conv", [96, P])

        gdn = Region(phase)
        qkv_at = gdn.at
        qkv = gdn("qkv", [P, QKV, S])
        z_t = gdn("z_t", [P, H, S])
        state = gdn("state", [P, H, P])
        ba_at = gdn.at
        ba_raw = gdn("ba_raw", [P, DC, 2 * H])
        ba_hi = gdn("ba_hi", [P, DC, 2 * H], F32R)
        ba_lo = gdn("ba_lo", [P, DC, 2 * H], F32R)
        ba = gdn("ba", [P, NB, 2 * H])
        beta = gdn("beta", [P, NB, H])
        gate = gdn("gate", [P, NB, H])
        gtmp = gdn("gtmp", [P, 2, NB, H])
        dt_b = gdn("dt_b", [P, 2, H])
        gsum = gdn("gsum", [P, 3, NB, H])
        gexp = fixed("gexp", [P, 3, NB, H], at=ba_at)
        l2 = gtmp[:, :, :, :].rearrange("p a b c -> p (a b c)").rearrange("p (a b) -> p a b", a=NB)
        l2r = gdn("l2r", [P, NB, 2 * H])
        q_f = gdn("q_f", [P, NB, H])
        qg_f = gdn("qg_f", [P, NB, H])
        kb_f = gdn("kb_f", [P, NB, H])
        kl_f = gdn("kl_f", [P, NB, H])
        conv_u = [gdn(f"conv_u{i}", [P, S + 8]) for i in range(2)]
        conv_a = [tmp[:, i, :] for i in range(2)]
        y_gdn = fixed("y_gdn", [P, DC, S], at=qkv_at + 16384)
        sq_gdn = fixed("sq_gdn", [P, DC, S], at=qkv_at + 32768)
        room = ([h_base + 2048 * i for i in range(16)] + [ada_base + 2048 * i for i in range(8)]
                + [small_at + 2048 * i for i in range(4)])
        slot_names = "A B C D E F G H I J K M N O".split()
        slots = [{n: fixed(f"m{g}{n}", [P, HG, P], at=room.pop(0)) for n in slot_names}
                 for g in range(NG)]

        ffn = Region(phase)
        g_hi = ffn("g_hi", [P, 8, S], F32R)
        g_lo = ffn("g_lo", [P, 8, S], F32R)
        y_ffn = ffn("y_ffn", [P, DC, S])
        silu_g = ffn("silu_g", [P, 2, S])
        gated = ffn("gated", [P, 2, S])
        sq_ffn = ffn("sq_ffn", [P, DC, S])

        dsa = Region(phase)
        o_tok_at = dsa.at
        uk_hi = dsa("uk_hi", [P, LC, 1024], F32R)
        uk_lo = dsa("uk_lo", [P, LC, 1024], F32R)
        cq_hi = dsa("cq_hi", [P, LC, S], F32R)
        cq_lo = dsa("cq_lo", [P, LC, S], F32R)
        ckv_hi = dsa("ckv_hi", [P, LC, S], F32R)
        ckv_lo = dsa("ckv_lo", [P, LC, S], F32R)
        q_at = dsa.at
        q_t = dsa("q_t", [P, 8, S])
        k_at = dsa.at
        k_t = dsa("k_t", [P, 8, S])
        kx = dsa("kx", [P, NB, SMALL])
        kn = dsa("kn", [P, NB, 2 * DH])
        kn_t = dsa("kn_t", [P, S])
        mean = dsa("mean", [P, NB])
        score = dsa("score", [P, S])
        best = dsa("best", [P, 8])
        nmax = dsa("nmax", [P, 8])
        psum_p = dsa("psum_p", [P, 8])
        rsum = dsa("rsum", [P, 8])
        o_tok = fixed("o_tok", [P, NB, 1024], at=o_tok_at)
        latent = fixed("latent", [P, 2, LC, S], at=q_at)
        sq_lat = fixed("sq_lat", [P, 2, LC, S], at=k_at)
        att = Region(o_tok_at + 16384)
        q_st = att("q_st", [P, S])
        k_st = att("k_st", [P, S])
        s_m = att("s_m", [P, 2, S])
        p_s = att("p_s", [P, 2, S])
        p_t = att("p_t", [P, 2, S])
        y_dsa = fixed("y_dsa", [P, DC, S], at=q_at)
        sq_dsa = fixed("sq_dsa", [P, DC, S], at=k_at)
        in_h = Region(h_base + 16384)
        qi_t = fixed("qi_t", [P, 4, S], at=h_base)
        mask = fixed("mask", [P, NB, S], at=h_base + 8192)
        v_tok = fixed("v_tok", [P, NB, 1024], at=h_base + 16384)
        relu = fixed("relu", [P, IH, S], at=ada_base)
        o_out = fixed("o_out", [P, NB, D], at=phase + 49152)

        ps = ctx.enter_context(nc.psum_tensor("ps", [P, 8, S], F32))

        sems = {}

        def sem(name):
            if name not in sems:
                sems[name] = ctx.enter_context(nc.semaphore(name))
            return sems[name]

        raw_in = [sem(f"raw_in{i}") for i in range(2)]
        vec_in, x_in = sem("vec_in"), sem("x_in")
        hi_done, lo_done, tile_done = sem("hi_done"), sem("lo_done"), sem("tile_done")
        ada_here = [sem(f"ada_here{i}") for i in range(2)]
        ada_late = [sem(f"ada_late{i}") for i in range(2)]
        ada_used, ada_mm = sem("ada_used"), sem("ada_mm")

        def raw_tile(s, kc=8):
            return raw[s // 2][:, 0:kc, (s % 2) * P:(s % 2 + 1) * P]

        def split_tile(w, s, kc=8):
            return w[:, s, 0:kc * P].rearrange("p (k n) -> p k n", n=P)

        def f32(t):
            return t.bitcast(F32)

        def flat(t):
            return t.rearrange("p a b -> p (a b)")

        def gain(layer, k, d):
            return vec_t[:, DC + (layer * 4 + k) * DC + d:DC + (layer * 4 + k) * DC + d + 1]

        def shift(layer, k, d):
            at = layer * 48 + k * DC + d
            return mod[:, at:at + 1]

        H_SCALED = {0: 0, 2: 1, 3: 2, 5: 3}
        SQ_BASE = [0, 8, 16, 24, 32, 40, 42, 44, 52, 60]

        def load_quad(sp, q, src_a, src_b, kc=8):
            for side, src in enumerate((src_a, src_b)):
                if not (isinstance(q, int) and q == 0):
                    sp.wait_ge(lo_done, q * 4 - 2 + 2 * side)
                if isinstance(src, list):
                    for dst, part, signal in src:
                        sp.dma_start(dst, part).then_inc(signal, 16)
                else:
                    sp.dma_start(raw[side][:, 0:kc, :], src).then_inc(raw_in[side], 16)

        def first_slab(j):
            return isinstance(j, int) and j < 4

        def load_ada(sp, layer, jj):
            j = jj + 12 * layer
            src = ada_w[layer].rearrange("(b k p) n -> b p k n", b=2, p=P)
            for b in range(2):
                if not (isinstance(j, int) and j == 0):
                    sp.wait_ge(ada_used, j * 2 - 1 + b)
                sp.dma_start(ada_in[b][:, :, :], src[b][:, :, bass.ds(jj * 512, 512)])\
                    .then_inc(ada_here[b] if first_slab(j) else ada_late[b], 16)

        def rows(w):
            return w.rearrange("(k p) n -> p k n", p=P)

        def act_split(act, q, s, kc=8, src=None, dst=None):
            act.wait_ge(raw_in[s // 2], q * 16 + 16)
            if not (isinstance(q, int) and q == 0):
                act.wait_ge(tile_done, q * 4 + s - 3)
            nc.scalar.activation(split_tile(w_hi, s, kc) if dst is None else dst(w_hi),
                                 raw_tile(s, kc) if src is None else src, ACT.Copy).then_inc(hi_done, 1)

        def dve_split(dve, q, s, kc=8, src=None, dst=None):
            dve.wait_ge(hi_done, q * 4 + s + 1)
            lo, hi = (split_tile(w, s, kc) if dst is None else dst(w) for w in (w_lo, w_hi))
            nc.vector.tensor_tensor(lo, raw_tile(s, kc) if src is None else src, f32(hi),
                                    ALU.subtract).then_inc(lo_done, 1)

        def pe_tile(pe, q, s, r_hi, r_lo, kc=8, before=None, ready=None):
            pe.wait_ge(lo_done, q * 4 + s + 1)
            if before:
                before()
            hi, lo = split_tile(w_hi, s, kc), split_tile(w_lo, s, kc)
            for k in range(kc):
                if ready:
                    ready(k)
                nc.tensor.matmul(ps[:, s, :], hi[:, k, :], r_hi[:, k, :], start=k == 0, stop=False)
                nc.tensor.matmul(ps[:, s, :], hi[:, k, :], r_lo[:, k, :], start=False, stop=False)
                last = nc.tensor.matmul(ps[:, s, :], lo[:, k, :], r_hi[:, k, :], start=False, stop=k == kc - 1)
            last.then_inc(tile_done, 1)

        def dve_ada(dve, ch, j, quarter):
            b = quarter // 2
            if quarter % 2 == 0:
                if first_slab(j):
                    dve.wait_ge(ada_here[b], j * 16 + 16)
                else:
                    dve.wait_ge(ada_late[b], j * 16 - 48)
            for k in (quarter % 2 * 2, quarter % 2 * 2 + 1):
                cc = c_act[:, 4 * b + k:4 * b + k + 1]
                if b == 0 and k == 0:
                    ins = nc.vector.tensor_scalar(ada_acc[:, :], ada_in[b][:, k, :], cc, None, ALU.mult)
                else:
                    ins = nc.vector.scalar_tensor_tensor(ada_acc[:, :], ada_in[b][:, k, :], cc,
                                                         ada_acc[:, :], ALU.mult, ALU.add)
                if k == 3:
                    ins.then_inc(ada_used, 1)
                    dve.wait_ge(ada_used, j * 2 + b + 1)
                else:
                    ch(ins)

        def dve_ada_beside(dve, ch, j, s):
            if s == 1:
                dve_ada_out(dve, ch, j - 1)
            for quarter in ((), (0,), (1,), (2, 3))[s]:
                dve_ada(dve, ch, j, quarter)

        def pe_ada(pe, j):
            pe.wait_ge(ada_used, j * 2 + 2)
            for n in range(4):
                last = nc.tensor.matmul(ps[:, 7, n:n + 1], ada_acc[:, n * P:(n + 1) * P], ones[:, 0:1],
                                        start=True, stop=True)
            last.then_inc(ada_mm, 1)

        def dve_ada_out(dve, ch, j):
            dve.wait_ge(ada_mm, j + 1)
            ch(nc.vector.tensor_tensor(mod[:, bass.ds(j * 4, 4)], ps[:, 7, 0:4],
                                       bias_t[:, bass.ds(j * 4, 4)], ALU.add))

        def dve_coef(dve, ch, layer, ks):
            for k in ks:
                m = layer * 48 + (1, 2, 4, 5)[k] * DC
                g0 = DC + (layer * 4 + k) * DC
                ch(nc.vector.scalar_tensor_tensor(coef[:, layer, k, :], mod[:, m:m + DC], 1.0,
                                                  vec_t[:, g0:g0 + DC], ALU.add, ALU.mult))

        def act_squares(act, n, src, sq, chunks=DC, wait=None):
            for d in range(chunks):
                if wait:
                    wait(d)
                nc.scalar.activation(sq[:, d, :], src[:, d, :], ACT.Square).then_inc(sem("sq_made"), 1)

        def pe_stats(pe, n, sq, chunks=DC):
            for d in range(chunks):
                pe.wait_ge(sem("sq_made"), SQ_BASE[n] + d + 1)
                for b in range(NB):
                    last = nc.tensor.matmul(ps[:, 4, b:b + 1], sq[:, d, b * P:(b + 1) * P], ones[:, 0:1],
                                            start=d == 0 and b == 0, stop=d == chunks - 1,
                                            skip_group_check=True)
            last.then_inc(sem("stat_made"), 1)

        def dve_var(dve, n, width=D):
            dve.wait_ge(sem("stat_made"), n + 1)
            nc.vector.tensor_scalar(var[:, 0:NB], ps[:, 4, 0:NB], 1.0 / width, EPS,
                                    ALU.mult, ALU.add).then_inc(sem("var_made"), 1)
            dve.wait_ge(sem("rinv_made"), n + 1)
            nc.vector.tensor_tensor(diag[:, :, :], over_heads(ident[:, :]), along(rinv[:, 0:NB]),
                                    ALU.mult).then_inc(sem("diag_made"), 1)

        def pool_root(pool, n):
            pool.wait_ge(sem("var_made"), n + 1)
            nc.gpsimd.tensor_tensor(rinv[:, 0:NB], var[:, 0:NB], half[:, 0:NB], ALU.pow)\
                .then_inc(sem("rinv_made"), 1)

        def pe_bcast(pe, n):
            pe.wait_ge(sem("diag_made"), n + 1)
            nc.tensor.matmul(ps[:, 5, :], ones[:, :], flat(diag[:, :, :]), start=True, stop=True)\
                .then_inc(sem("root_out"), 1)

        def dve_residual(dve, ch, n, layer, k, y, m):
            dve.wait_ge(sem("root_out"), n + 1)
            for d in range(DC):
                ch(nc.vector.scalar_tensor_tensor(tmp[:, d % 2, :], ps[:, 5, :], coef[:, layer, k, d:d + 1],
                                                  y[:, d, :], ALU.mult, ALU.mult))
                nc.vector.tensor_tensor(x_t[:, d, :], x_t[:, d, :], tmp[:, d % 2, :], ALU.add)\
                    .then_inc(sem("x_made"), 1)
                dve.wait_ge(sem("x_made"), 8 * m + d + 1)

        def dve_h(dve, ch, n, layer, k, m):
            dve.wait_ge(sem("root_out"), n + 1)

            for d in range(DC):
                nc.vector.scalar_tensor_tensor(tmp[:, d % 3, :], ps[:, 5, :], coef[:, layer, k, d:d + 1],
                                               x_t[:, d, :], ALU.mult, ALU.mult).then_inc(sem("h_scaled"), 1)
                if d:
                    low_of(d - 1, dve, layer, k, m)
            low_of(DC - 1, dve, layer, k, m)

        def low_of(d, dve, layer, k, m):
            dve.wait_ge(sem("h_rounded"), 8 * m + d + 1)
            nc.vector.scalar_tensor_tensor(h_lo[:, d, :], tmp[:, d % 3, :], shift(layer, 3 * (k // 2), d),
                                           f32(h_hi[:, d, :]), ALU.add, ALU.subtract)\
                .then_inc(sem("h_made"), 1)
            dve.wait_ge(sem("h_made"), 8 * m + d + 1)

        def act_h(act, layer, k, m):
            for d in range(DC):
                act.wait_ge(sem("h_scaled"), 8 * H_SCALED[m] + d + 1)
                nc.scalar.activation(h_hi[:, d, :], tmp[:, d % 3, :], ACT.Identity,
                                     bias=shift(layer, 3 * (k // 2), d)).then_inc(sem("h_rounded"), 1)


        def gdn_in_act(act, i, s, conv):
            act.wait_ge(tile_done, i * 4 + s + 1)
            if conv:
                nc.scalar.activation(conv_u[s % 2][:, 3:3 + S], ps[:, s, :], ACT.Copy)
                nc.scalar.activation(conv_a[s % 2], ps[:, s, :], ACT.Identity,
                                     scale=conv_t[:, CONV - 1, bass.ds(i * 4 + s, 1)]).then_inc(sem("gdn_out_of_ps"), 1)
            else:
                nc.scalar.activation(z_t[:, i * 4 + s - QKV, :], ps[:, s, :], ACT.Silu)\
                    .then_inc(sem("gdn_out_of_ps"), 1)

        def gdn_conv_act(act, i, s):
            act.wait_ge(sem("conv_made"), i * 4 + s + 1)
            nc.scalar.activation(qkv[:, i * 4 + s, :] if isinstance(i, int) else
                                 qkv[:, bass.ds(i * 4 + s, 1), :].rearrange("p a b -> p (a b)"),
                                 conv_a[s % 2], ACT.Silu).then_inc(sem("qkv_made"), 1)

        def gdn_conv_dve(dve, ch, i, s):
            dve.wait_ge(sem("gdn_out_of_ps"), i * 4 + s + 1)
            for j in range(CONV - 1):
                ins = nc.vector.scalar_tensor_tensor(conv_a[s % 2], conv_u[s % 2][:, j:j + S],
                                                     conv_t[:, j, bass.ds(i * 4 + s, 1)],
                                                     conv_a[s % 2], ALU.mult, ALU.add)
                if j < CONV - 2:
                    ch(ins)
                else:
                    ins.then_inc(sem("conv_made"), 1)

        N_CONV = QKV // 4
        sq_ring = [tmp[:, 0, :], tmp[:, 1, :], conv_u[0][:, 0:S], conv_u[1][:, 0:S]]

        def act_qk_squares(act, t):
            act.wait_ge(sem("qkv_made"), QKV)
            for j in range(4 * t, 4 * t + 4):
                if j >= 4:
                    act.wait_ge(sem("qk_sum"), j - 3)
                nc.scalar.activation(sq_ring[j % 4], qkv[:, j, :], ACT.Square).then_inc(sem("qk_sq"), 1)

        def pe_qk_sums(pe, t):
            for j in range(4 * t, 4 * t + 4):
                pe.wait_ge(sem("qk_sq"), j + 1)
                for b in range(NB):
                    at = b * 2 * H + j
                    last = nc.tensor.matmul(ps[:, 4, at:at + 1], sq_ring[j % 4][:, b * P:(b + 1) * P],
                                            ones[:, 0:1], start=True, stop=True)
                last.then_inc(sem("qk_sum"), 1)

        def pe_gates(pe):
            pe.wait_ge(sem("ba_split"), 1)
            for k in range(DC):
                nc.tensor.matmul(ps[0:2 * H, 6, :], ba_hi[:, k, :], h_hi[:, k, :], start=k == 0, stop=False)
                nc.tensor.matmul(ps[0:2 * H, 6, :], ba_hi[:, k, :], h_lo[:, k, :], start=False, stop=False)
                last = nc.tensor.matmul(ps[0:2 * H, 6, :], ba_lo[:, k, :], h_hi[:, k, :],
                                        start=False, stop=k == DC - 1)
            last.then_inc(sem("gates_mm"), 1)

        def act_gates_out(act):
            act.wait_ge(sem("gates_mm"), 1)
            nc.scalar.activation(tmp[0:2 * H, 2, :], ps[0:2 * H, 6, :], ACT.Copy).then_inc(sem("gates_out"), 1)

        def pe_gates_turn(pe):
            pe.wait_ge(sem("gates_out"), 1)
            for b in range(NB):
                last = nc.tensor.transpose(ps[:, 5, b * 2 * H:(b + 1) * 2 * H], tmp[0:2 * H, 2, b * P:(b + 1) * P],
                                           ident[0:2 * H, 0:2 * H])
            last.then_inc(sem("gates_turned"), 1)

        def dve_gates(dve, ch):
            dve.wait_ge(sem("gates_turned"), 1)
            ch(nc.vector.tensor_copy(ba[:, :, :], ps[:, 5, 0:NB * 2 * H].rearrange("p (a b) -> p a b", a=NB)))
            a_in, g0, g1 = ba[:, :, H:2 * H], gtmp[:, 0, :, :], gtmp[:, 1, :, :]
            ch(nc.vector.tensor_tensor(a_in, a_in, dt_b[:, 0, :].unsqueeze(1).to_broadcast([P, NB, H]), ALU.add))
            ch(nc.vector.tensor_scalar(g0, a_in, -1.0, None, ALU.mult))
            nc.vector.tensor_tensor(g0, g0, a_in, ALU.min).then_inc(sem("gate_abs"), 1)
            dve.wait_ge(sem("gate_exp"), 3)
            ch(nc.vector.tensor_scalar(beta[:, :, :], beta[:, :, :], 1.0, None, ALU.add))
            ch(nc.vector.reciprocal(beta[:, :, :], beta[:, :, :]))
            ch(nc.vector.tensor_scalar(g1, g1, 1.0, None, ALU.add))
            nc.vector.tensor_scalar(a_in, a_in, 0.0, None, ALU.max).then_inc(sem("gate_abs"), 1)
            dve.wait_ge(sem("gate_abs"), 2)
            dve.wait_ge(sem("gate_exp"), 4)
            ch(nc.vector.tensor_tensor(g0, g1, a_in, ALU.add))
            nc.vector.scalar_tensor_tensor(gate[:, :, :], g0, -1.0,
                                           dt_b[:, 1, :].unsqueeze(1).to_broadcast([P, NB, H]),
                                           ALU.mult, ALU.mult).then_inc(sem("gate_made"), 1)
            dve.wait_ge(sem("gate_made"), 1)

        def pe_g_sums(pe):
            pe.wait_ge(sem("gate_made"), 1)
            g_all = gate[:, :, :].rearrange("p a b -> p (a b)")
            nc.tensor.matmul(ps[:, 6, 0:NB * H], upto[:, :], g_all, start=True, stop=True)
            nc.tensor.matmul(ps[:, 6, NB * H:2 * NB * H], ones[:, :], g_all, start=True, stop=True)\
                .then_inc(sem("g_sums_mm"), 1)

        def pool_qk_root(pool):
            pool.wait_ge(sem("l2_made"), 1)
            nc.gpsimd.tensor_tensor(l2r[:, :, :], l2[:, :, :], half[:, 0:NB * 2 * H].rearrange("p (a b) -> p a b", a=NB), ALU.pow).then_inc(sem("l2_root"), 1)

        def act_g_exp(act):
            act.wait_ge(sem("g_sums_made"), 1)
            nc.scalar.activation(gexp[:, :, :, :], gsum[:, :, :, :], ACT.Exp).then_inc(sem("g_exp_made"), 1)

        def dve_factors(dve, ch):
            dve.wait_ge(sem("qk_sum"), 2 * H)
            nc.vector.tensor_scalar(l2[:, :, :], ps[:, 4, 0:NB * 2 * H].rearrange("p (a b) -> p a b", a=NB),
                                    EPS, None, ALU.add).then_inc(sem("l2_made"), 1)
            dve.wait_ge(sem("g_sums_mm"), 1)
            ch(nc.vector.tensor_copy(gsum[:, 0:2, :, :], ps[:, 6, 0:2 * NB * H].rearrange("p (t a b) -> p t a b", t=2, a=NB)))
            nc.vector.tensor_tensor(gsum[:, 2, :, :], gsum[:, 1, :, :], gsum[:, 0, :, :], ALU.subtract)\
                .then_inc(sem("g_sums_made"), 1)
            dve.wait_ge(sem("l2_root"), 1)
            ch(nc.vector.tensor_scalar(q_f[:, :, :], l2r[:, :, 0:H], float(P) ** -0.5, None, ALU.mult))
            dve.wait_ge(sem("g_exp_made"), 1)
            ch.inc(nc.vector.tensor_tensor(qg_f[:, :, :], q_f[:, :, :], gexp[:, 0, :, :], ALU.mult))
            ch.inc(nc.vector.tensor_tensor(kl_f[:, :, :], l2r[:, :, H:2 * H], gexp[:, 2, :, :], ALU.mult))
            ch(nc.vector.tensor_tensor(kb_f[:, :, :], beta[:, :, :], gexp[:, 0, :, :], ALU.mult))
            ch(nc.vector.tensor_tensor(kb_f[:, :, :], kb_f[:, :, :], l2r[:, :, H:2 * H], ALU.mult))

        def act_gates(act):
            act.wait_ge(sem("gate_abs"), 1)
            nc.scalar.activation(beta[:, :, :], ba[:, :, 0:H], ACT.Exp, scale=-1.0).then_inc(sem("gate_exp"), 1)
            nc.scalar.activation(gtmp[:, 1, :, :], gtmp[:, 0, :, :], ACT.Exp).then_inc(sem("gate_exp"), 1)
            nc.scalar.activation(dt_b[:, 1, :], dt_b[:, 1, :], ACT.Exp).then_inc(sem("gate_exp"), 1)
            act.wait_ge(sem("gate_abs"), 2)
            nc.scalar.activation(gtmp[:, 1, :, :], gtmp[:, 1, :, :], ACT.Ln).then_inc(sem("gate_exp"), 1)

        def bank(g, n):
            return ps[:, 4 * g + n, :].rearrange("p (h n) -> p h n", h=HG)

        def first(c):
            return isinstance(c, int) and c == 0

        def heads(t, g, c):
            return t[:, c, g * HG:(g + 1) * HG] if isinstance(c, int) else \
                t[:, bass.ds(c, 1), g * HG:(g + 1) * HG].rearrange("p a b -> p (a b)")

        def tt(out, a, b, op):
            return nc.vector.tensor_tensor(out, a, b, op)

        def free_for_core(eng):
            eng.wait_ge(tile_done, 4 * N_GDN_IN)
            eng.wait_ge(ada_used, 24)

        def pool_stage(pool, g, c):
            if not first(c):
                pool.wait_ge(sem(f"w_mm{g}"), c)
            nc.gpsimd.tensor_tensor(slots[g]["J"][:, :, :], over_heads(upto[:, :]), along(heads(gate, g, c)),
                                    ALU.mult).then_inc(sem(f"g_row{g}"), 1)
            if not first(c):
                pool.wait_ge(sem(f"vnew_mm{g}"), c)
            f = 2 * H + g * HG
            nc.gpsimd.tensor_tensor(slots[g]["C"][:, :, :], qkv[:, f:f + HG, bass.ds(c * P, P)],
                                    over_heads(ones[:, :]), ALU.mult).then_inc(sem(f"v_staged{g}"), 1)

        def pool_beta(pool, g, c):
            pool.wait_ge(sem(f"decay{g}"), c * 2 + 1)
            nc.gpsimd.tensor_tensor(slots[g]["K"][:, :, :], slots[g]["K"][:, :, :], along(heads(beta, g, c)),
                                    ALU.mult).then_inc(sem(f"decay_beta{g}"), 1)

        def pool_level(pool, g, c, lv):
            if lv == 1:
                pool.wait_ge(sem(f"lt_out{g}"), c + 1)
            if lv >= 3:
                pool.wait_ge(sem(f"y_mm{g}"), c * (LEVELS - 1) + lv - 2)
            nc.gpsimd.tensor_tensor(slots[g]["JO"[lv % 2]][:, :, :], slots[g]["N"][:, :, :],
                                    over_heads(level_t[:, lv, :]), ALU.mult)\
                .then_inc(sem(f"level{g}"), 1)

        def core_pool(pool, g, c, ce, cs):
            o = 1 - g
            for lv in range(1, LEVELS):
                pool_level(pool, g, c, lv)
                if lv == 2 and cs is not None:
                    pool_stage(pool, o, cs)
                if lv == 5 and cs is not None:
                    pool_beta(pool, o, cs)

        def core_start_pool(pool, g, c):
            pool_stage(pool, g, c)
            pool_beta(pool, g, c)

        def pe_tokens(pe, g, c):
            m = slots[g]
            pe.wait_ge(sem(f"staged{g}"), c * 2 + 2)
            pe.wait_ge(sem(f"v_staged{g}"), c + 1)
            if not first(c):
                pe.wait_ge(sem(f"o_out{g}"), c)
                pe.wait_ge(sem(f"state_made{g}"), c * HG)
            for n, slot in enumerate("ABC"):
                for h in range(HG):
                    last = nc.tensor.transpose(bank(g, n)[:, h, :], m[slot][:, h, :], ident[:, :])
                last.then_inc(sem(f"qkv_tok{g}"), 1)

        def pe_sum_rows(pe, g, c):
            pe.wait_ge(sem(f"g_row{g}"), c + 1)
            nc.tensor.matmul(ps[:, 4 * g + 3, :], ones[:, :], flat(slots[g]["J"][:, :, :]),
                             start=True, stop=True).then_inc(sem(f"grow_mm{g}"), 1)

        def pe_features(pe, g, c):
            for n, slot in enumerate("ADB"):
                pe.wait_ge(sem(f"tok_made{g}"), c * 3 + n + 1)
                for h in range(HG):
                    last = nc.tensor.transpose(bank(g, n)[:, h, :], slots[g][slot][:, h, :], ident[:, :])
                last.then_inc(sem(f"feat_mm{g}"), 1)

        def pe_kk(pe, g, c):
            m = slots[g]
            pe.wait_ge(sem(f"feat_out{g}"), c * 3 + 3)
            for n, (left, right) in enumerate((("I", "I"), ("I", "G"))):
                for h in range(HG):
                    last = nc.tensor.matmul(bank(g, n)[:, h, :], m[left][:, h, :], m[right][:, h, :],
                                            start=True, stop=True)
                last.then_inc(sem(f"kk_mm{g}"), 1)

        def pe_turn_l(pe, g, c):
            pe.wait_ge(sem(f"l_made{g}"), c + 1)
            for h in range(HG):
                last = nc.tensor.transpose(bank(g, 2)[:, h, :], slots[g]["K"][:, h, :], ident[:, :])
            last.then_inc(sem(f"lt_mm{g}"), 1)

        def pe_level_y(pe, g, c, lv):
            m = slots[g]
            pe.wait_ge(sem(f"level{g}"), c * (LEVELS - 1) + lv)
            pe.wait_ge(sem(f"x_made{g}"), c * (LEVELS - 1) + lv)
            for h in range(HG):
                last = nc.tensor.matmul(bank(g, 3)[:, h, :], m["JO"[lv % 2]][:, h, :], m["A"][:, h, :],
                                        start=True, stop=True)
            last.then_inc(sem(f"y_mm{g}"), 1)

        def pe_level_x(pe, g, c, lv):
            m = slots[g]
            pe.wait_ge(sem(f"y_out{g}"), c * (LEVELS - 1) + lv)
            pe.wait_ge(sem(f"inv_made{g}"), c * LEVELS + lv)
            n, left, right = (0, "B", "D") if lv < LEVELS - 1 else (1, "D", "B")
            for h in range(HG):
                last = nc.tensor.matmul(bank(g, n)[:, h, :], m[left][:, h, :], m[right][:, h, :],
                                        start=True, stop=True)
            last.then_inc(sem(f"x_mm{g}"), 1)

        def pe_level_turn(pe, g, c, lv):
            pe.wait_ge(sem(f"x_made{g}"), c * (LEVELS - 1) + lv + 1)
            if lv == 1:
                pe.wait_ge(sem(f"attn_made{g}"), c + 1)
            for h in range(HG):
                last = nc.tensor.transpose(bank(g, 1)[:, h, :], slots[g]["A"][:, h, :], ident[:, :])
            last.then_inc(sem(f"xt_mm{g}"), 1)

        def pe_w(pe, g, c):
            m = slots[g]
            pe.wait_ge(sem(f"inv_made{g}"), c * LEVELS + LEVELS)
            for h in range(HG):
                last = nc.tensor.matmul(bank(g, 2)[:, h, :], m["E"][:, h, :], m["B"][:, h, :],
                                        start=True, stop=True)
            last.then_inc(sem(f"w_mm{g}"), 1)

        def pe_values(pe, g, c):
            m = slots[g]
            pe.wait_ge(sem(f"w_out{g}"), c + 1)
            for h in range(HG):
                nc.tensor.matmul(bank(g, 3)[:, h, :], m["B"][:, h, :], m["C"][:, h, :],
                                 start=True, stop=False)
                last = nc.tensor.matmul(bank(g, 3)[:, h, :], m["G"][:, h, :], state[:, g * HG + h, :],
                                        start=False, stop=True)
            last.then_inc(sem(f"vnew_mm{g}"), 1)

        def pe_out(pe, g, c):
            m = slots[g]
            pe.wait_ge(sem(f"vnew_out{g}"), c + 1)
            for h in range(HG):
                nc.tensor.matmul(bank(g, 0)[:, h, :], state[:, g * HG + h, :], m["H"][:, h, :],
                                 start=True, stop=False)
                last = nc.tensor.matmul(bank(g, 0)[:, h, :], m["I"][:, h, :], m["M"][:, h, :],
                                        start=False, stop=True)
            last.then_inc(sem(f"o_mm{g}"), 1)
            for h in range(HG):
                last = nc.tensor.matmul(bank(g, 1)[:, h, :], m["F"][:, h, :], m["I"][:, h, :],
                                        start=True, stop=True)
            last.then_inc(sem(f"kv_mm{g}"), 1)

        def core_pe(pe, g, c, ce, cs):
            o = 1 - g
            for lv in range(1, LEVELS):
                pe_level_y(pe, g, c, lv)
                if lv == 1 and ce is not None:
                    pe_w(pe, o, ce)
                if lv == 2 and ce is not None:
                    pe_out(pe, o, ce)
                if cs is not None and lv == 3:
                    pe_sum_rows(pe, o, cs)
                if cs is not None and lv == 5:
                    pe_kk(pe, o, cs)
                if cs is not None and lv == 6:
                    pe_turn_l(pe, o, cs)
                pe_level_x(pe, g, c, lv)
                if lv == 1 and ce is not None:
                    pe_values(pe, o, ce)
                if cs is not None and lv == 4:
                    pe_features(pe, o, cs)
                if lv < LEVELS - 1:
                    pe_level_turn(pe, g, c, lv)
                if cs is not None and lv == 2:
                    pe_tokens(pe, o, cs)

        def core_start_pe(pe, g, c):
            pe_tokens(pe, g, c)
            pe_sum_rows(pe, g, c)
            pe_features(pe, g, c)
            pe_kk(pe, g, c)
            pe_turn_l(pe, g, c)

        def core_end_pe(pe, g, c):
            pe_w(pe, g, c)
            pe_values(pe, g, c)
            pe_out(pe, g, c)

        def out_of(g, n, slot, signal, scale=1.0):
            nc.scalar.activation(slots[g][slot][:, :, :], bank(g, n), ACT.Copy, scale=scale)\
                .then_inc(sem(f"{signal}{g}"), 1)

        def act_stage(act, g, c):
            for n, (slot, used) in enumerate((("A", "w_mm"), ("B", "vnew_mm"))):
                if not first(c):
                    act.wait_ge(sem(f"{used}{g}"), c)
                f = n * H + g * HG
                nc.scalar.activation(slots[g][slot][:, :, :], qkv[:, f:f + HG, bass.ds(c * P, P)], ACT.Copy)\
                    .then_inc(sem(f"staged{g}"), 1)

        def act_decay(act, g, c):
            for slot, k, scale in (("K", 1, -1.0), ("M", 2, 1.0)):
                act.wait_ge(sem(f"decay_arg{g}"), c * 2 + k)
                nc.scalar.activation(slots[g][slot][:, :, :], slots[g][slot][:, :, :], ACT.Exp, scale=scale)\
                    .then_inc(sem(f"decay{g}"), 1)

        def act_features(act, g, c):
            for n, slot in enumerate("GHI"):
                act.wait_ge(sem(f"feat_mm{g}"), c * 3 + n + 1)
                out_of(g, n, slot, "feat_out")

        def act_turn_l(act, g, c):
            act.wait_ge(sem(f"lt_mm{g}"), c + 1)
            out_of(g, 2, "N", "lt_out")

        def act_level(act, g, c, lv):
            act.wait_ge(sem(f"y_mm{g}"), c * (LEVELS - 1) + lv)
            out_of(g, 3, "D", "y_out")

        def act_level_turn(act, g, c, lv):
            act.wait_ge(sem(f"xt_mm{g}"), c * (LEVELS - 2) + lv)
            out_of(g, 1, "B", "inv_made")

        def act_w(act, g, c):
            act.wait_ge(sem(f"w_mm{g}"), c + 1)
            out_of(g, 2, "G", "w_out", -1.0)

        def act_values(act, g, c):
            act.wait_ge(sem(f"vnew_mm{g}"), c + 1)
            out_of(g, 3, "I", "vnew_out")

        def act_out(act, g, c):
            act.wait_ge(sem(f"o_mm{g}"), c + 1)
            nc.scalar.activation(qkv[:, g * HG:(g + 1) * HG, bass.ds(c * P, P)], bank(g, 0), ACT.Copy)\
                .then_inc(sem(f"o_out{g}"), 1)

        def core_act(act, g, c, ce, cs):
            o = 1 - g
            for lv in range(1, LEVELS):
                act_level(act, g, c, lv)
                if lv == 1 and ce is not None:
                    act_w(act, o, ce)
                if lv == 2 and ce is not None:
                    act_out(act, o, ce)
                if cs is not None and lv == 5:
                    act_decay(act, o, cs)
                if lv == 1 and ce is not None:
                    act_values(act, o, ce)
                if cs is not None and lv == 4:
                    act_features(act, o, cs)
                if lv < LEVELS - 1:
                    act_level_turn(act, g, c, lv)
                if lv == 1 and cs is not None:
                    act_stage(act, o, cs)
            if cs is not None:
                act_turn_l(act, o, cs)

        def core_start_act(act, g, c):
            act_stage(act, g, c)
            act_decay(act, g, c)
            act_features(act, g, c)
            act_turn_l(act, g, c)

        def core_end_act(act, g, c):
            act_w(act, g, c)
            act_values(act, g, c)
            act_out(act, g, c)

        def dve_decay(dve, ch, g, c):
            m = slots[g]
            dve.wait_ge(sem(f"grow_mm{g}"), c + 1)
            ch(tt(m["J"][:, :, :], bank(g, 3), along(heads(gsum[:, 0, :, :], g, c)), ALU.subtract))
            tt(m["K"][:, :, :], m["J"][:, :, :], over_heads(mask_l[:, :]), ALU.add).then_inc(sem(f"decay_arg{g}"), 1)
            tt(m["M"][:, :, :], m["J"][:, :, :], over_heads(mask_t[:, :]), ALU.subtract)\
                .then_inc(sem(f"decay_arg{g}"), 1)

        def dve_tokens(dve, ch, g, c):
            dve_q_k(dve, ch, g, c)
            dve_k_v(dve, ch, g, c)

        def dve_q_k(dve, ch, g, c):
            m = slots[g]
            dve.wait_ge(sem(f"qkv_tok{g}"), c * 3 + 3)
            ch.inc(tt(m["A"][:, :, :], bank(g, 0), along(heads(q_f, g, c)), ALU.mult))
            tt(m["D"][:, :, :], bank(g, 0), along(heads(qg_f, g, c)), ALU.mult)\
                .then_inc(sem(f"tok_made{g}"), 1)
            ch.inc(tt(m["B"][:, :, :], bank(g, 1), along(heads(l2r[:, :, H:2 * H], g, c)), ALU.mult))

        def dve_k_v(dve, ch, g, c):
            m = slots[g]
            ch.inc(tt(m["E"][:, :, :], bank(g, 1), along(heads(kb_f, g, c)), ALU.mult))
            tt(m["F"][:, :, :], bank(g, 1), along(heads(kl_f, g, c)), ALU.mult)\
                .then_inc(sem(f"tok_made{g}"), 1)
            tt(m["C"][:, :, :], bank(g, 2), along(heads(beta, g, c)), ALU.mult)\
                .then_inc(sem(f"tok_made{g}"), 1)

        def dve_l(dve, ch, g, c):
            m = slots[g]
            dve.wait_ge(sem(f"decay_beta{g}"), c + 1)
            dve.wait_ge(sem(f"kk_mm{g}"), c * 2 + 1)
            tt(m["K"][:, :, :], bank(g, 0), m["K"][:, :, :], ALU.mult).then_inc(sem(f"l_made{g}"), 1)
            dve.wait_ge(sem(f"decay{g}"), c * 2 + 2)
            dve.wait_ge(sem(f"kk_mm{g}"), c * 2 + 2)
            tt(m["M"][:, :, :], bank(g, 1), m["M"][:, :, :], ALU.mult).then_inc(sem(f"attn_made{g}"), 1)

        def dve_first(dve, ch, g, c):
            m = slots[g]
            dve.wait_ge(sem(f"feat_mm{g}"), c * 3 + 3)
            dve.wait_ge(sem(f"l_made{g}"), c + 1)
            ch(tt(m["A"][:, :, :], m["K"][:, :, :], over_heads(first_l[:, :]), ALU.mult))
            tt(m["A"][:, :, :], m["A"][:, :, :], over_heads(ident[:, :]), ALU.add).then_inc(sem(f"x_made{g}"), 1)

        def dve_first_turned(dve, ch, g, c):
            m = slots[g]
            dve.wait_ge(sem(f"lt_out{g}"), c + 1)
            ch(tt(m["B"][:, :, :], m["N"][:, :, :], over_heads(first_t[:, :]), ALU.mult))
            tt(m["B"][:, :, :], m["B"][:, :, :], over_heads(ident[:, :]), ALU.add).then_inc(sem(f"inv_made{g}"), 1)

        def dve_level(dve, g, c, lv):
            m = slots[g]
            dve.wait_ge(sem(f"x_mm{g}"), c * (LEVELS - 1) + lv)
            if lv < LEVELS - 1:
                dve.wait_ge(sem(f"x_made{g}"), c * (LEVELS - 1) + lv)
                tt(m["A"][:, :, :], m["A"][:, :, :], bank(g, 0), ALU.subtract).then_inc(sem(f"x_made{g}"), 1)
            else:
                tt(m["B"][:, :, :], m["B"][:, :, :], bank(g, 1), ALU.subtract).then_inc(sem(f"inv_made{g}"), 1)

        def dve_state(dve, g, c):
            dve.wait_ge(sem(f"kv_mm{g}"), c + 1)
            for h in range(HG):
                at = g * HG + h
                last_g = gexp[:, 1, c, at:at + 1] if isinstance(c, int) else \
                    gexp[:, 1, bass.ds(c, 1), at:at + 1].rearrange("p a b -> p (a b)")
                nc.vector.scalar_tensor_tensor(state[:, at, :], state[:, at, :], last_g, bank(g, 1)[:, h, :],
                                               ALU.mult, ALU.add).then_inc(sem(f"state_made{g}"), 1)

        def core_dve(dve, ch, g, c, ce, cs):
            o = 1 - g
            for lv in range(1, LEVELS):
                dve_level(dve, g, c, lv)
                if lv == 2 and ce is not None:
                    dve_state(dve, o, ce)
                if cs is not None and lv == 2:
                    dve_q_k(dve, ch, o, cs)
                if cs is not None and lv == 3:
                    dve_k_v(dve, ch, o, cs)
                    dve_decay(dve, ch, o, cs)
                if cs is not None and lv == 5:
                    dve_l(dve, ch, o, cs)
                    dve_first(dve, ch, o, cs)
            if cs is not None:
                dve_first_turned(dve, ch, o, cs)

        def core_start_dve(dve, ch, g, c):
            dve_tokens(dve, ch, g, c)
            dve_decay(dve, ch, g, c)
            dve_l(dve, ch, g, c)
            dve_first(dve, ch, g, c)
            dve_first_turned(dve, ch, g, c)

        def core_loop(turn, start, end, eng, chain=None):
            n = chain.n if chain else 0
            start(0, 0)
            per = 2 * (chain.n - n) if chain else 0
            turn(0, 0, None, 0)
            n = chain.n if chain else 0
            with eng.Fori(1, NB) as c:
                if chain:
                    chain.turns = c * per - per
                turn(1, c - 1, c - 1, c)
                turn(0, c, c - 1, c)
            if chain:
                assert chain.n == n + per, (chain.n, n, per)
                chain.turns, chain.n = None, n + (NB - 1) * per
            turn(1, NB - 1, NB - 1, None)
            if end:
                end(1, NB - 1)

        def gdn_norm_pe(pe):
            pe.wait_ge(sem("o_sq"), H)
            for h in range(H):
                for b in range(NB):
                    last = nc.tensor.matmul(ps[:, 4, h * NB + b:h * NB + b + 1], sq_gdn[:, h, b * P:(b + 1) * P],
                                            ones[:, 0:1], start=True, stop=True)
            last.then_inc(sem("o_stat"), 1)
            for h in range(H):
                pe.wait_ge(sem("o_diag"), h + 1)
                if h >= 2:
                    pe.wait_ge(sem("o_scaled"), h - 1)
                nc.tensor.matmul(ps[:, 5 + h % 2, :], ones[:, :],
                                 flat(diag[:, :, :]) if h % 2 == 0 else tmp[:, 2, :],
                                 start=True, stop=True).then_inc(sem("o_root"), 1)

        def gdn_norm_act(act):
            for g in range(NG):
                act.wait_ge(sem(f"o_out{g}"), NB)
            for h in range(H):
                nc.scalar.activation(sq_gdn[:, h, :], qkv[:, h, :], ACT.Square).then_inc(sem("o_sq"), 1)
            for h in range(H):
                act.wait_ge(sem("o_gated"), h + 1)
                nc.scalar.activation(h_hi[:, h, :], tmp[:, h % 2, :], ACT.Copy).then_inc(sem("h_rounded"), 1)

        def gdn_norm_dve(dve, ch):
            dve.wait_ge(sem("o_stat"), 1)
            nc.vector.tensor_scalar(var[:, :], ps[:, 4, 0:H * NB], 1.0 / P, EPS, ALU.mult, ALU.add)\
                .then_inc(sem("o_var"), 1)
            dve.wait_ge(sem("o_rinv"), 1)

            def make_diag(h):
                if h >= 2:
                    dve.wait_ge(sem("o_root"), h - 1)
                dst = diag[:, :, :] if h % 2 == 0 else tmp[:, 2, :].rearrange("p (a b) -> p a b", a=NB)
                nc.vector.tensor_tensor(dst, over_heads(ident[:, :]), along(rinv[:, h * NB:(h + 1) * NB]),
                                        ALU.mult).then_inc(sem("o_diag"), 1)

            def low(h):
                dve.wait_ge(sem("h_rounded"), 8 + h + 1)
                nc.vector.tensor_tensor(h_lo[:, h, :], tmp[:, h % 2, :], f32(h_hi[:, h, :]), ALU.subtract)\
                    .then_inc(sem("h_made"), 1)
                dve.wait_ge(sem("h_made"), 8 + h + 1)

            make_diag(0)
            for h in range(H):
                if h + 1 < H:
                    make_diag(h + 1)
                dve.wait_ge(sem("o_root"), h + 1)
                nc.vector.scalar_tensor_tensor(tmp[:, h % 2, :], ps[:, 5 + h % 2, :], gnorm,
                                               qkv[:, h, :], ALU.mult, ALU.mult).then_inc(sem("o_scaled"), 1)
                dve.wait_ge(sem("o_scaled"), h + 1)
                nc.vector.tensor_tensor(tmp[:, h % 2, :], tmp[:, h % 2, :], z_t[:, h, :], ALU.mult)\
                    .then_inc(sem("o_gated"), 1)
                if h:
                    low(h - 1)
            low(H - 1)

        y_out = sem("y_out")

        def dve_y(dve, q, s, y, d, yt, add):
            dve.wait_ge(tile_done, q * 4 + s + 1)
            if add:
                dve.wait_ge(y_out, yt)
                nc.vector.tensor_tensor(y[:, d, :], y[:, d, :], ps[:, s, :], ALU.add).then_inc(y_out, 1)
            else:
                nc.vector.tensor_copy(y[:, d, :], ps[:, s, :]).then_inc(y_out, 1)

        def plain_out(eng, kind, q0, y, y0, nxt, ch=None):
            for j in range(2):
                for s in range(4):
                    if kind == "dve":
                        dve_y(eng, q0 + j, s, y, 4 * j + s, y0 + 4 * j + s, False)
                        if j == 0:
                            dve_split(eng, q0 + 1, s)
                    elif j == 0:
                        act_split(eng, q0 + 1, s)
                    if j == 1 and nxt:
                        nxt(s)

        F0 = [sum(PARTS[:p]) for p in range(3)]
        Y_FFN = [8, 40]

        def part_quads(layer, p):
            q = Q_FFN[layer] + F0[p] // 2 + 2 * p
            return q, PARTS[p] // 2, layer * (FC // 2) + F0[p] // 2

        def ffn_sp(sp, layer):
            w_in, w_out = rows(ffn_w_in[layer]), ffn_w_out[layer]
            for p in range(3):
                q, n, _ = part_quads(layer, p)

                def body(i):
                    at = i * 256 + F0[p] * P
                    load_quad(sp, i + q, w_in[:, :, bass.ds(at, 256)], w_in[:, :, bass.ds(at + FC * P, 256)])

                repeat(sp, n, body)
                kc = PARTS[p]
                part = rows(w_out[F0[p] * P:(F0[p] + kc) * P, :])
                for j in range(2):
                    load_quad(sp, q + n + j, part[:, :, j * 512:j * 512 + 256],
                              part[:, :, j * 512 + 256:j * 512 + 512], kc)

        def ffn_act(act, layer, nxt):
            for p in range(3):
                q, n, c0 = part_quads(layer, p)
                kc = PARTS[p]

                def epilogue(i, s):
                    act.wait_ge(tile_done, i * 4 + 4 * q + s + 1)
                    ci = i + c0
                    if s < 2:
                        if not (isinstance(ci, int) and ci == 0):
                            act.wait_ge(sem("ffn_mul"), ci * 2 + s - 1)
                        nc.scalar.activation(silu_g[:, s, :], ps[:, s, :], ACT.Silu).then_inc(sem("ffn_silu"), 1)
                    else:
                        act.wait_ge(sem("ffn_mul"), ci * 2 + s - 1)
                        out = g_hi[:, i * 2 + s - 2, :] if isinstance(i, int) else \
                            flat(g_hi[:, bass.ds(i * 2 + s - 2, 1), :])
                        nc.scalar.activation(out, gated[:, s - 2, :], ACT.Copy).then_inc(sem("ffn_hi"), 1)

                def body(i):
                    for s in range(4):
                        epilogue(i, s)
                        act_split(act, i + q + 1, s)

                repeat(act, n - 1, body)
                for s in range(4):
                    epilogue(n - 1, s)
                    act_split(act, q + n, s, kc)
                for s in range(4):
                    act_split(act, q + n + 1, s, kc)
                for s in range(4):
                    if p < 2:
                        act_split(act, q + n + 2, s)
                    elif nxt:
                        nxt(s)

        def ffn_dve(dve, ch, layer, nxt):
            for p in range(3):
                q, n, c0 = part_quads(layer, p)
                kc = PARTS[p]

                def epilogue(i, s, split):
                    ci = i + c0
                    if s < 2:
                        split(s)
                        return
                    dve.wait_ge(tile_done, i * 4 + 4 * q + s + 1)
                    dve.wait_ge(sem("ffn_silu"), ci * 2 + s - 1)
                    nc.vector.tensor_tensor(gated[:, s - 2, :], silu_g[:, s - 2, :], ps[:, s, :], ALU.mult)\
                        .then_inc(sem("ffn_mul"), 1)
                    split(s)
                    dve.wait_ge(sem("ffn_hi"), ci * 2 + s - 1)
                    one = bass.ds(i * 2 + s - 2, 1)
                    nc.vector.tensor_tensor(flat(g_lo[:, one, :]), gated[:, s - 2, :], f32(flat(g_hi[:, one, :])),
                                            ALU.subtract).then_inc(sem("ffn_lo"), 1)

                def ada(i, s):
                    if layer == 0:
                        dve_ada_beside(dve, ch, i + 12 + F0[p] // 2, s)

                def body(i):
                    for s in range(4):
                        ada(i, s)
                        epilogue(i, s, lambda s: dve_split(dve, i + q + 1, s))

                repeat(dve, n - 1, body, ch)
                for s in range(4):
                    ada(n - 1, s)
                    epilogue(n - 1, s, lambda s: dve_split(dve, q + n, s, kc))
                y0 = Y_FFN[layer] + 8 * p
                for j in range(2):
                    for s in range(4):
                        dve_y(dve, q + n + j, s, y_ffn, 4 * j + s, y0 + 4 * j + s, p > 0)
                        if j == 0:
                            dve_split(dve, q + n + 1, s, kc)
                        elif p < 2:
                            dve_split(dve, q + n + 2, s)
                        elif nxt:
                            nxt(s)
                    if layer == 0 and p == 2 and j == 0:
                        dve_ada_out(dve, ch, 22)
                        for part in range(4):
                            dve_ada(dve, ch, 23, part)
            if layer == 0:
                dve_ada_out(dve, ch, 23)

        def ffn_pe(pe, layer, m):
            for p in range(3):
                q, n, c0 = part_quads(layer, p)
                y0 = Y_FFN[layer] + 8 * p

                def body(i):
                    for s in range(4):
                        def free():
                            if isinstance(i, int) and i == 0:
                                pe.wait_ge(y_out, y0 - 4 + s + 1)
                            else:
                                pe.wait_ge(sem("ffn_silu" if s < 2 else "ffn_mul"), (i + c0) * 2 - 1 + s % 2)

                        def ready(k):
                            if isinstance(i, int) and i == 0 and p == 0 and s == 0:
                                pe.wait_ge(sem("h_made"), 8 * m + k + 1)

                        pe_tile(pe, i + q, s, h_hi, h_lo, before=free, ready=ready)
                        if layer == 0 and s == 0 and not (isinstance(i, int) and i + F0[p] == 0):
                            pe_ada(pe, i + 11 + F0[p] // 2)

                repeat(pe, n, body)
                last_ci = c0 + n - 1
                for j in range(2):
                    for s in range(4):
                        def free():
                            if j == 0:
                                pe.wait_ge(sem("ffn_silu" if s < 2 else "ffn_mul"), 2 * last_ci + s % 2 + 1)
                            else:
                                pe.wait_ge(y_out, y0 + s + 1)

                        def ready(k):
                            if j == 0 and s == 0:
                                pe.wait_ge(sem("ffn_lo"), 2 * c0 + k + 1)

                        pe_tile(pe, q + n + j, s, g_hi, g_lo, PARTS[p], before=free, ready=ready)
                    if layer == 0 and p == 2:
                        pe_ada(pe, 22 + j)

        def raw_half(s):
            return flat(raw[s // 2][:, :, :])[:, (s % 2) * 1024:(s % 2 + 1) * 1024]

        def dsa_views(quad, s):
            if quad == 1 and s == 0:
                n = DC * SMALL
                return raw_half(0)[:, 0:n], lambda w: w[:, 0, 0:n]
            return raw_half(s), lambda w: w[:, s, :]

        def dsa_sp(sp):
            w_in = rows(dsa_w_in[0])
            load_quad(sp, Q_DSA, w_in[:, :, 0:LAT], w_in[:, :, LAT:2 * LAT])
            small = raw_half(0)[:, 0:DC * SMALL].rearrange("p (k n) -> p k n", k=DC)
            qi = raw_half(1).rearrange("p (k n) -> p k n", k=LC)
            uq = flat(raw[1][:, :, :]).rearrange("p (k n) -> p k n", k=LC)
            load_quad(sp, Q_DSA + 1,
                      [(small, w_in[:, :, 2 * LAT:], raw_in[0]), (qi, rows(dsa_w_qidx[0]), sem("qi_in"))],
                      [(uq, rows(dsa_w_uq[0]), raw_in[1])])
            uk = flat(raw[0][:, :, :]).rearrange("p (h n) -> p h n", n=LAT)
            uv = flat(raw[1][:, :, :]).rearrange("p (k h v) -> p k h v", k=LC, v=DH)
            uv_src = dsa_w_uv[0].rearrange("h (k p) v -> p k h v", p=P)
            load_quad(sp, Q_DSA + 2, [(uk, dsa_w_uk[0].rearrange("(g a) d n -> (a d) g n", a=2), raw_in[0])],
                      [(uv[:, 0, :, :], uv_src[:, 0, :, :], raw_in[1]),
                       (uv[:, 1, :, :], uv_src[:, 1, :, :], sem("uv_in"))])
            w_out = rows(dsa_w_out[0])
            for j in range(2):
                load_quad(sp, Q_DSA_OUT + j, w_out[:, :, j * 512:j * 512 + 256],
                          w_out[:, :, j * 512 + 256:j * 512 + 512])

        def dsa_split_act(act, quad, s):
            src, dst = dsa_views(quad, s)
            if (quad, s) == (1, 1):
                act.wait_ge(sem("qi_in"), 16)
            if (quad, s) == (2, 3):
                act.wait_ge(sem("uv_in"), 16)
            act_split(act, Q_DSA + quad, s, src=src, dst=dst)

        def dsa_split_dve(dve, quad, s):
            src, dst = dsa_views(quad, s)
            dve_split(dve, Q_DSA + quad, s, src=src, dst=dst)

        def mm3(out, l_hi, l_lo, r_hi, r_lo, first, last):
            nc.tensor.matmul(out, l_hi, r_hi, start=first, stop=False)
            nc.tensor.matmul(out, l_hi, r_lo, start=False, stop=False)
            return nc.tensor.matmul(out, l_lo, r_hi, start=False, stop=last)

        AT_QI, AT_Q, AT_UK, AT_K, AT_V = 0, 4, 12, 20, 28
        LAST = {3: 4 * Q_DSA + 6, 11: 4 * Q_DSA + 8, 18: 4 * Q_DSA + 9, 19: 4 * Q_DSA + 10, 35: 4 * Q_DSA + 12}

        def proj_ready(act, t):
            if t in LAST:
                act.wait_ge(tile_done, LAST[t])
            else:
                act.wait_ge(sem("proj_mm"), t + 1 - sum(x < t for x in LAST))

        def dsa_in_pe(pe, m):
            for s in range(4):
                pe_tile(pe, Q_DSA, s, h_hi, h_lo, before=lambda: pe.wait_ge(y_out, Y_FFN[0] + 20 + s + 1),
                        ready=(lambda k: pe.wait_ge(sem("h_made"), 8 * m + k + 1)) if s == 0 else None)
            pe.wait_ge(lo_done, 4 * Q_DSA + 5)
            w = [t[:, 0, 0:DC * SMALL].rearrange("p (k n) -> p k n", n=SMALL) for t in (w_hi, w_lo)]
            for b in range(NB):
                blk = slice(b * P, (b + 1) * P)
                for k in range(DC):
                    last = mm3(ps[:, 6, b * SMALL:(b + 1) * SMALL], h_hi[:, k, blk], h_lo[:, k, blk],
                               w[0][:, k, :], w[1][:, k, :], k == 0, k == DC - 1)
            last.then_inc(tile_done, 1)
            for n in (5, 6):
                if n == 6:
                    pe.wait_ge(sem("lat_made"), LC)
                pe_stats(pe, n, sq_lat[:, n - 5, :, :], LC)
                pe_bcast(pe, n)
            pe.wait_ge(sem("kn_made"), 1)
            for b in range(NB):
                last = nc.tensor.transpose(ps[:, 7, b * P:(b + 1) * P], kn[:, b, :], ident[:, :])
            last.then_inc(sem("knt_mm"), 1)
            pe.wait_ge(sem("lat_made"), LC)
            pe.wait_ge(lo_done, 4 * Q_DSA + 6)
            wq = [t[:, 1, :].rearrange("p (k n) -> p k n", k=LC) for t in (w_hi, w_lo)]
            for j in range(4):
                pe.wait_ge(sem("sq_made"), SQ_BASE[5] + j + 1)
                for k in range(LC):
                    last = mm3(ps[:, j, :], wq[0][:, k, j * P:(j + 1) * P], wq[1][:, k, j * P:(j + 1) * P],
                               cq_hi[:, k, :], cq_lo[:, k, :], k == 0, k == LC - 1)
                last.then_inc(tile_done if j == 3 else sem("proj_mm"), 1)

        def indexer_pe(pe, b):
            n = (b + 1) * P
            if b == 1:
                pe.wait_ge(sem("lat_made"), 2 * LC)
                pe.wait_ge(sem("knt_out"), 1)
                pe.wait_ge(sem("proj_out"), AT_QI + 4)
            for j in range(IH):
                t = (b - 1) * IH + j
                if t >= 4:
                    pe.wait_ge(sem("relu_made"), t - 3)
                lanes = slice(64 * (j % 2), 64 * (j % 2) + 64)
                nc.tensor.matmul(ps[:, 4 + t % 4, 0:n], qi_t[lanes, j // 2, b * P:(b + 1) * P],
                                 kn_t[lanes, 0:n], start=True, stop=True).then_inc(sem("logit_mm"), 1)

        def dsa_q_pe(pe):
            for j in range(8):
                if j < 4:
                    pe.wait_ge(sem("proj_out"), AT_QI + j + 1)
                if j >= 4:
                    pe.wait_ge(sem("proj_out"), AT_Q + j - 3)
                if j == 0:
                    pe.wait_ge(lo_done, 4 * Q_DSA + 8)
                cols = slice(j * P, (j + 1) * P)
                for k in range(LC):
                    last = mm3(ps[:, j % 4, :], w_hi[:, 2 + k, cols], w_lo[:, 2 + k, cols],
                               cq_hi[:, k, :], cq_lo[:, k, :], k == 0, k == LC - 1)
                    if j == 7:
                        last.then_inc(tile_done, 1)
                if j < 7:
                    last.then_inc(sem("proj_mm"), 1)

        def dsa_k_pe(pe):
            pe.wait_ge(lo_done, 4 * Q_DSA + 10)
            t = 0
            for w in (w_hi, w_lo):
                for k in range(LC):
                    for s in (0, 1):
                        if t < 4:
                            pe.wait_ge(sem("proj_out"), AT_Q + t + 5)
                        else:
                            pe.wait_ge(sem("proj_out"), AT_UK + t - 3)
                        for r in range(4):
                            last = nc.tensor.transpose(ps[:, t % 4, r * P:(r + 1) * P],
                                                       f32(w[:, s, r * LAT + k * P:r * LAT + (k + 1) * P]),
                                                       ident[:, :])
                        last.then_inc(sem("proj_mm") if t < 6 else tile_done, 1)
                        t += 1
            for j in range(8):
                pe.wait_ge(sem("proj_out"), AT_UK + 8)
                if j >= 4:
                    pe.wait_ge(sem("proj_out"), AT_K + j - 3)
                for k in range(LC):
                    cols = slice(j * P, (j + 1) * P)
                    last = mm3(ps[:, j % 4, :], uk_hi[:, k, cols], uk_lo[:, k, cols],
                               ckv_hi[:, k, :], ckv_lo[:, k, :], k == 0, k == LC - 1)
                last.then_inc(sem("proj_mm"), 1)

        def dsa_v_pe(pe):
            for j in range(8):
                b, cols = j // 2, slice(j % 2 * 512, j % 2 * 512 + 512)
                blk = slice(b * P, (b + 1) * P)
                if j < 4:
                    pe.wait_ge(sem("proj_out"), AT_K + j + 5)
                else:
                    pe.wait_ge(sem("proj_out"), AT_V + j - 3)
                if j == 0:
                    pe.wait_ge(lo_done, 4 * Q_DSA + 12)
                for k in range(LC):
                    last = mm3(ps[:, j % 4, :], ckv_hi[:, k, blk], ckv_lo[:, k, blk],
                               w_hi[:, 2 + k, cols], w_lo[:, 2 + k, cols], k == 0, k == LC - 1)
                    if j == 7:
                        last.then_inc(tile_done, 1)
                if j < 7:
                    last.then_inc(sem("proj_mm"), 1)

        def dsa_in_act(act):
            for s in range(4):
                act.wait_ge(tile_done, 4 * Q_DSA + s + 1)
                nc.scalar.activation(latent[:, s // 2, s % 2, :], ps[:, s, :], ACT.Copy).then_inc(sem("lat_here"), 1)
                nc.scalar.activation(sq_lat[:, s // 2, s % 2, :], ps[:, s, :], ACT.Square).then_inc(sem("sq_made"), 1)
                dsa_split_act(act, 1, s)
            for half_ in range(2):
                for k in range(LC):
                    act.wait_ge(sem("lat_scaled"), half_ * LC + k + 1)
                    dst = (cq_hi, ckv_hi)[half_]
                    nc.scalar.activation(dst[:, k, :], tmp[:, k, :], ACT.Copy).then_inc(sem("lat_hi"), 1)
            act.wait_ge(sem("knt_mm"), 1)
            nc.scalar.activation(kn_t[:, :], ps[:, 7, :], ACT.Copy).then_inc(sem("knt_out"), 1)
            for j in range(4):
                proj_ready(act, AT_QI + j)
                nc.scalar.activation(qi_t[:, j, :], ps[:, j, :], ACT.Copy).then_inc(sem("proj_out"), 1)

        def relu_act(act, b):
            n = (b + 1) * P
            if b > 1:
                act.wait_ge(sem("relu_used"), (b - 1) * IH)
            for j in range(IH):
                t = (b - 1) * IH + j
                act.wait_ge(sem("logit_mm"), t + 1)
                nc.scalar.activation(relu[:, j, 0:n], ps[:, 4 + t % 4, 0:n], ACT.Relu).then_inc(sem("relu_made"), 1)

        def dsa_qkv_act(act, nxt):
            relu_act(act, 1)
            for j in range(8):
                proj_ready(act, AT_Q + j)
                nc.scalar.activation(q_t[:, j, :], ps[:, j % 4, :], ACT.Copy, scale=DH ** -0.5)\
                    .then_inc(sem("proj_out"), 1)
            for s in range(4):
                dsa_split_act(act, 2, s)
            relu_act(act, 2)
            for t in range(8):
                proj_ready(act, AT_UK + t)
                dst = (uk_hi, uk_lo)[t // 4]
                nc.scalar.activation(dst[:, t // 2 % 2, (t % 2) * 512:(t % 2) * 512 + 512], ps[:, t % 4, :],
                                     ACT.Copy).then_inc(sem("proj_out"), 1)
            for j in range(8):
                proj_ready(act, AT_K + j)
                nc.scalar.activation(k_t[:, j, :], ps[:, j % 4, :], ACT.Copy).then_inc(sem("proj_out"), 1)
            relu_act(act, 3)
            for j in range(8):
                proj_ready(act, AT_V + j)
                nc.scalar.activation(v_tok[:, j // 2, j % 2 * 512:j % 2 * 512 + 512], ps[:, j % 4, :],
                                     ACT.Copy).then_inc(sem("proj_out"), 1)
            for s in range(4):
                nxt(s)

        def dsa_in_dve(dve, ch):
            for s in range(4):
                dsa_split_dve(dve, 1, s)
            dve.wait_ge(tile_done, 4 * Q_DSA + 5)
            ch(nc.vector.tensor_copy(kx[:, :, :], ps[:, 6, 0:NB * SMALL].rearrange("p (b n) -> p b n", b=NB)))
            k_x, w_x, k_1 = kx[:, :, 0:DH], kx[:, :, DH:SMALL], kn[:, :, 0:DH]
            ch(nc.vector.tensor_reduce(mean[:, :], k_x, AX_X, ALU.add))
            ch(nc.vector.tensor_scalar(mean[:, :], mean[:, :], 1.0 / DH, None, ALU.mult))
            ch(nc.vector.tensor_tensor(k_x, k_x, along(mean[:, :], DH), ALU.subtract))
            ch(nc.vector.tensor_tensor(k_1, k_x, k_x, ALU.mult))
            ch(nc.vector.tensor_reduce(mean[:, :], k_1, AX_X, ALU.add))
            nc.vector.tensor_scalar(mean[:, :], mean[:, :], 1.0 / DH, EPS, ALU.mult, ALU.add)\
                .then_inc(sem("ln_var"), 1)
            ch(nc.vector.tensor_scalar(w_x, w_x, IH ** -0.5 * DH ** -0.5, None, ALU.mult))
            dve.wait_ge(sem("ln_root"), 1)
            ch(nc.vector.tensor_tensor(k_x, k_x, along(mean[:, :], DH), ALU.mult))
            ch(nc.vector.tensor_tensor(k_x, k_x, ln_gb[:, 0, :].unsqueeze(1).to_broadcast([P, NB, DH]), ALU.mult))
            for a in range(2):
                ch(nc.vector.tensor_tensor(kn[:, :, a * DH:(a + 1) * DH], k_x,
                                           ln_gb[:, 1, :].unsqueeze(1).to_broadcast([P, NB, DH]), ALU.add))
            nc.vector.tensor_copy(mask[:, 0, 0:P], causal[:, :]).then_inc(sem("kn_made"), 1)
            for half_ in range(2):
                dve_var(dve, 5 + half_, LAT)
                dve.wait_ge(sem("root_out"), 6 + half_)
                dve.wait_ge(sem("lat_here"), 2 + 2 * half_)
                for k in range(LC):
                    nc.vector.scalar_tensor_tensor(tmp[:, k, :], ps[:, 5, :], qn_g[:, half_, k:k + 1],
                                                   latent[:, half_, k, :], ALU.mult, ALU.mult)\
                        .then_inc(sem("lat_scaled"), 1)
                for k in range(LC):
                    dve.wait_ge(sem("lat_hi"), half_ * LC + k + 1)
                    hi, lo = ((cq_hi, cq_lo), (ckv_hi, ckv_lo))[half_]
                    nc.vector.tensor_tensor(lo[:, k, :], tmp[:, k, :], f32(hi[:, k, :]), ALU.subtract)\
                        .then_inc(sem("lat_made"), 1)
                dve.wait_ge(sem("lat_made"), half_ * LC + LC)

        def indexer_dve(dve, ch, b):
            n = (b + 1) * P
            for j in range(IH):
                t = (b - 1) * IH + j
                dve.wait_ge(sem("relu_made"), t + 1)
                w = kx[:, b, DH + j:DH + j + 1]
                if j == 0:
                    ins = nc.vector.tensor_scalar(score[:, 0:n], relu[:, j, 0:n], w, None, ALU.mult)
                else:
                    ins = nc.vector.scalar_tensor_tensor(score[:, 0:n], relu[:, j, 0:n], w, score[:, 0:n],
                                                         ALU.mult, ALU.add)
                ins.then_inc(sem("relu_used"), 1)
                dve.wait_ge(sem("relu_used"), t + 1)
            ch(nc.vector.tensor_tensor(score[:, b * P:n], score[:, b * P:n], causal[:, :], ALU.add))
            for _ in range(TOPK // 8):
                ch(nc.vector.max(best[:, :], score[:, 0:n]))
                ch(nc.vector.match_replace(score[:, 0:n], best[:, :], score[:, 0:n], TAKEN))
            ch(nc.vector.tensor_scalar(mask[:, b, 0:n], score[:, 0:n], 2.0 / 3.0 * TAKEN, -BIG, ALU.is_gt, ALU.mult))

        UNITS = [(a, b) for a in range(2) for b in range(NB)]

        def att_pe(pe, i):
            def scores(u):
                a, b = UNITS[u]
                lanes, n = slice(64 * a, 64 * a + 64), (b + 1) * P
                if u == 0:
                    pe.wait_ge(sem("qk_staged"), i * 2 + 2)
                if not (isinstance(i, int) and i == 0 and u < 4):
                    pe.wait_ge(sem("s_out"), i * 8 + u - 3)
                nc.tensor.matmul(s_bank(u)[:, 0:n],
                                 q_st[lanes, b * P:(b + 1) * P], k_st[lanes, 0:n],
                                 start=True, stop=True).then_inc(sem("s_mm"), 1)

            def turn(u):
                a, b = UNITS[u]
                pe.wait_ge(sem("p_made"), i * 8 + u + 1)
                if not (isinstance(i, int) and i == 0 and u < 2):
                    pe.wait_ge(sem("pt_out"), i * 8 + u - 1)
                for k in range(b + 1):
                    last = nc.tensor.transpose(ps[:, 4 + u % 2, k * P:(k + 1) * P], p_s[:, u % 2, k * P:(k + 1) * P],
                                               ident[:, :])
                last.then_inc(sem("pt_mm"), 1)

            def values(u):
                a, b = UNITS[u]
                pe.wait_ge(sem("pt_out"), i * 8 + u + 1)
                if not (isinstance(i, int) and i == 0 and u < 2):
                    pe.wait_ge(sem("o_ready"), i * 8 + u - 1)
                for k in range(b + 1):
                    v = v_tok[:, k, bass.ds(i * 128 + a * 64, 64)]
                    last = nc.tensor.matmul(ps[:, 6 + u % 2, 0:DH], p_t[:, u % 2, k * P:(k + 1) * P], v,
                                            start=k == 0, stop=k == b)
                last.then_inc(sem("o_mm"), 1)

            for t in range(len(UNITS) + 3):
                if t < 8:
                    scores(t)
                if 0 <= t - 2 < 8:
                    turn(t - 2)
                if 0 <= t - 3 < 8:
                    values(t - 3)

        def s_bank(u):
            return ps[:, u % 4, :]

        def att_pool(pool, i):
            if isinstance(i, int) and i == 0:
                pool.wait_ge(sem("proj_out"), AT_V + 8)
            else:
                pool.wait_ge(sem("s_mm"), i * 8)
            for dst, src in ((q_st, q_t), (k_st, k_t)):
                part = flat(src[:, bass.ds(i, 1), :]).rearrange("p (b n) -> p b n", n=P)
                nc.gpsimd.tensor_tensor(dst[:, :].rearrange("p (b n) -> p b n", n=P), part,
                                        over_heads(ones[:, :]), ALU.mult)\
                    .then_inc(sem("qk_staged"), 1)

        def att_act(act, i):
            for t in range(len(UNITS) + 1):
                if t < 8:
                    a, b = UNITS[t]
                    n = (b + 1) * P
                    act.wait_ge(sem("nmax_made"), i * 8 + t + 1)
                    if not (isinstance(i, int) and i == 0 and t < 2):
                        act.wait_ge(sem("pt_mm"), i * 8 + t - 1)
                    nc.scalar.activation(p_s[:, t % 2, 0:n], s_m[:, t % 2, 0:n], ACT.Exp, bias=nmax[:, t:t + 1],
                                         accum_out=psum_p[:, t:t + 1]).then_inc(sem("p_made"), 1)
                u = t - 1
                if u >= 0:
                    n = (UNITS[u][1] + 1) * P
                    act.wait_ge(sem("pt_mm"), i * 8 + u + 1)
                    if not (isinstance(i, int) and i == 0 and u < 2):
                        act.wait_ge(sem("o_mm"), i * 8 + u - 1)
                    nc.scalar.activation(p_t[:, u % 2, 0:n], ps[:, 4 + u % 2, 0:n], ACT.Copy)\
                        .then_inc(sem("pt_out"), 1)

        def att_dve(dve, ch, i):
            for t in range(len(UNITS) + 3):
                if t < 8:
                    a, b = UNITS[t]
                    n = (b + 1) * P
                    dve.wait_ge(sem("s_mm"), i * 8 + t + 1)
                    if not (isinstance(i, int) and i == 0 and t < 2):
                        dve.wait_ge(sem("p_made"), i * 8 + t - 1)
                    nc.vector.tensor_tensor(s_m[:, t % 2, 0:n], s_bank(t)[:, 0:n], mask[:, b, 0:n], ALU.add)\
                        .then_inc(sem("s_out"), 1)
                    dve.wait_ge(sem("s_out"), i * 8 + t + 1)
                    nc.vector.tensor_reduce(nmax[:, t:t + 1], s_m[:, t % 2, 0:n], AX_X, ALU.max, negate=True)\
                        .then_inc(sem("nmax_made"), 1)
                u = t - 3
                if u >= 0:
                    a, b = UNITS[u]
                    dve.wait_ge(sem("p_made"), i * 8 + u + 1)
                    ch(nc.vector.reciprocal(rsum[:, u:u + 1], psum_p[:, u:u + 1]))
                    dve.wait_ge(sem("o_mm"), i * 8 + u + 1)
                    nc.vector.tensor_scalar(o_tok[:, b, bass.ds(i * 128 + a * 64, 64)], ps[:, 6 + u % 2, 0:DH],
                                            rsum[:, u:u + 1], None, ALU.mult).then_inc(sem("o_ready"), 1)

        def o_turn_pe(pe, m):
            pe.wait_ge(sem("o_ready"), 64)
            for d in range(8):
                if d >= 4:
                    pe.wait_ge(sem("h_made"), 8 * m + d - 3)
                for b in range(NB):
                    last = nc.tensor.transpose(ps[:, d % 4, b * P:(b + 1) * P], o_tok[:, b, d * P:(d + 1) * P],
                                               ident[:, :])
                last.then_inc(sem("att_turned"), 1)

        def o_turn_act(act):
            for d in range(8):
                act.wait_ge(sem("att_turned"), d + 1)
                nc.scalar.activation(h_hi[:, d, :], ps[:, d % 4, :], ACT.Copy).then_inc(sem("h_rounded"), 1)

        def o_turn_dve(dve, m):
            for d in range(8):
                dve.wait_ge(sem("h_rounded"), 8 * m + d + 1)
                nc.vector.tensor_tensor(h_lo[:, d, :], ps[:, d % 4, :], f32(h_hi[:, d, :]), ALU.subtract)\
                    .then_inc(sem("h_made"), 1)
            dve.wait_ge(sem("h_made"), 8 * m + 8)

        block = ctx.enter_context(nc.Block())
        N_MISC = 5

        @block.sync
        def _(sp):
            sp.dma_start(row_vec[0:DC, :], c.rearrange("a (k p) -> (a k) p", p=P)).then_inc(vec_in, 16)
            sp.dma_start(row_vec[DC:9 * DC, :], norm_g.rearrange("a b (k p) -> (a b k) p", p=P)).then_inc(vec_in, 16)
            sp.dma_start(row_bias[:, :], ada_b.rearrange("a (k p) -> (a k) p", p=P)).then_inc(vec_in, 16)
            sp.dma_start(row_conv[:, :], gdn_conv_w[0].rearrange("j (k p) -> (j k) p", p=P)).then_inc(vec_in, 16)
            sp.dma_start(row_vec[9 * DC:9 * DC + 1, :], gdn_norm_g).then_inc(vec_in, 16)
            sp.dma_start(row_vec[9 * DC + 1:9 * DC + 1 + LC, :], dsa_q_norm_g[0].rearrange("(k p) -> k p", p=P))\
                .then_inc(vec_in, 16)
            sp.dma_start(row_vec[9 * DC + 1 + LC:VEC, :], dsa_kv_norm_g[0].rearrange("(k p) -> k p", p=P))\
                .then_inc(vec_in, 16)
            load_ada(sp, 0, 0)
            sp.dma_start(x_tok[:, :, :], x[0].rearrange("(b p) d -> p b d", p=P)).then_inc(x_in, 16)
            for jj in range(1, 3):
                load_ada(sp, 0, jj)
            w_in = rows(gdn_w_in[0])

            def gdn_quad(i):
                at = i * 512
                load_quad(sp, i, w_in[:, :, bass.ds(at, 256)], w_in[:, :, bass.ds(at + 256, 256)])

            gdn_quad(0)
            load_ada(sp, 0, 3)
            misc = [(ba_raw[:, :, :], w_in[:, :, (QKV + H) * P:]),
                    (dt_b[:, 0, :], gdn_dt_bias[0].partition_broadcast(P)),
                    (dt_b[:, 1, :], gdn_a_log[0].partition_broadcast(P)),
                    (ln_gb[:, 0, :], dsa_kidx_ln_g[0].partition_broadcast(P)),
                    (ln_gb[:, 1, :], dsa_kidx_ln_b[0].partition_broadcast(P))]
            assert len(misc) == N_MISC
            for dst, src in misc:
                sp.dma_start(dst, src).then_inc(sem("misc_in"), 16)

            def gdn_turn(i):
                gdn_quad(i)

            repeat(sp, N_GDN_IN, gdn_turn, first=1)
            w_out = rows(gdn_w_out[0])
            for j in range(2):
                load_quad(sp, Q_GDN_OUT + j, w_out[:, :, j * 512:j * 512 + 256],
                          w_out[:, :, j * 512 + 256:j * 512 + 512])
            ffn_sp(sp, 0)
            if stop > 1:
                dsa_sp(sp)
                ffn_sp(sp, 1)
            for b in range(NB):
                sp.wait_ge(sem("x_out"), 2 * b + 2)
                sp.dma_start(out[0, b * P:(b + 1) * P, :], o_out[:, b, :]).then_inc(sem("stored"), 16)
            sp.wait_ge(sem("stored"), 16 * NB)

        @block.gpsimd
        def _(pool):
            ch = Chain(pool, sem("pool_chain"))

            def fill(t, value, *cuts):
                ch(nc.gpsimd.memset(t, value))
                for compare, other, base, pattern, channel in cuts:
                    ch(nc.gpsimd.affine_select(out=t, in_=t, compare_op=compare, fill=other, base=base,
                                               pattern=pattern, channel_multiplier=channel))

            fill(ident[:, :], 0.0, (ALU.not_equal, 1.0, 0, [[-1, P]], 1))
            ch(nc.gpsimd.memset(ones[:, :], 1.0))
            nc.gpsimd.memset(half[:, :], -0.5).then_inc(sem("consts"), 1)
            for u in conv_u:
                ch(nc.gpsimd.memset(u[:, 0:3], 0.0))
            fill(upto[:, :], 1.0, (ALU.is_ge, 0.0, 0, [[1, P]], -1))
            fill(mask_l[:, :], 0.0, (ALU.is_gt, BIG, 0, [[-1, P]], 1))
            fill(mask_t[:, :], 0.0, (ALU.is_ge, BIG, 0, [[1, P]], -1))
            fill(causal[:, :], 0.0, (ALU.is_ge, -BIG, 0, [[-1, P]], 1))
            fill(first_l[:, :], -1.0, (ALU.is_equal, 0.0, -1, [[-2, P // 2], [0, 2]], 1),
                 (ALU.is_ge, 0.0, 0, [[0, P // 2], [-1, 2]], 0))
            for lv in range(LEVELS):
                n = 1 << lv
                pairs = P // (2 * n)
                cuts = [(ALU.is_ge, 0.0, 0, [[-2 * n, pairs], [0, 2], [0, n]], 1),
                        (ALU.is_ge, 0.0, n - 1, [[2 * n, pairs], [0, 2], [0, n]], -1),
                        (ALU.is_gt, 0.0, 0, [[0, pairs], [1, 2], [0, n]], 0)]
                fill(first_t[:, :] if lv == 0 else level_t[:, lv, :], -1.0 if lv == 0 else 1.0, *cuts)
            nc.gpsimd.memset(state[:, :, :], 0.0).then_inc(sem("consts"), 1)
            pool_root(pool, 0)
            repeat(pool, 12, lambda j: load_ada(pool, 0, j), first=4)
            pool.wait_ge(sem("qkv_made"), QKV)
            pool_qk_root(pool)
            pool.wait_ge(sem("gate_made"), 1)
            free_for_core(pool)
            core_loop(lambda *a: core_pool(pool, *a), lambda *a: core_start_pool(pool, *a), None, pool)
            pool.wait_ge(sem("o_var"), 1)
            nc.gpsimd.tensor_tensor(rinv[:, :], var[:, :], half[:, 0:32], ALU.pow).then_inc(sem("o_rinv"), 1)
            for n in (1, 2):
                pool_root(pool, n)
            repeat(pool, 12, lambda j: load_ada(pool, 1, j))
            for n in range(3, 5 if stop > 1 else 4):
                pool_root(pool, n)
            if stop > 1:
                pool.wait_ge(sem("ln_var"), 1)
                nc.gpsimd.tensor_tensor(mean[:, :], mean[:, :], half[:, 0:NB], ALU.pow).then_inc(sem("ln_root"), 1)
                for n in (5, 6):
                    pool_root(pool, n)
                repeat(pool, AH // 2, lambda i: att_pool(pool, i))
                for n in (7, 8, 9):
                    pool_root(pool, n)

        @block.scalar
        def _(act):
            act.wait_ge(sem("vec_out"), 1)
            nc.scalar.activation(c_act[:, :], vec_t[:, 0:DC], ACT.Silu).then_inc(sem("c_made"), 1)
            for d in range(DC):
                act.wait_ge(sem("x_turned"), d + 1)
                nc.scalar.activation(x_t[:, d, :], ps[:, d % 4, :], ACT.Copy).then_inc(sem("x_here"), 1)
            act_squares(act, 0, x_t, sq_gdn, wait=lambda d: act.wait_ge(sem("x_here"), d + 1))
            for s in range(4):
                act_split(act, 0, s)
            act.wait_ge(sem("misc_in"), 16 * N_MISC)
            nc.scalar.activation(ba_hi[:, :, :], ba_raw[:, :, :], ACT.Copy).then_inc(sem("ba_rounded"), 1)
            act_h(act, 0, 0, 0)

            def gdn_turn(i):
                for s in range(4):
                    gdn_in_act(act, i, s, True)
                    act_split(act, i + 1, s)
                    gdn_conv_act(act, i, s)

            repeat(act, N_CONV, gdn_turn)
            for i in range(N_CONV, N_GDN_IN):
                for s in range(4):
                    gdn_in_act(act, i, s, False)
                    act_split(act, i + 1, s)
                    if i == N_CONV:
                        if s == 1:
                            act_gates_out(act)
                        act_qk_squares(act, s)
                if i == N_CONV:
                    act_gates(act)
                    act_g_exp(act)
            free_for_core(act)
            core_loop(lambda *a: core_act(act, *a), lambda *a: core_start_act(act, *a),
                      lambda *a: core_end_act(act, *a), act)
            gdn_norm_act(act)
            plain_out(act, "act", Q_GDN_OUT, None, None, lambda s: act_split(act, Q_FFN[0], s))
            act_squares(act, 1, y_gdn, sq_gdn, wait=lambda d: act.wait_ge(y_out, d + 1))
            act_squares(act, 2, x_t, sq_gdn, wait=lambda d: act.wait_ge(sem("x_made"), d + 1))
            act_h(act, 0, 2, 2)
            ffn_act(act, 0, (lambda s: act_split(act, Q_DSA, s)) if stop > 1 else None)
            act_squares(act, 3, y_ffn, sq_ffn, wait=lambda d: act.wait_ge(y_out, Y_FFN[0] + 16 + d + 1))
            if stop > 1:
                act_squares(act, 4, x_t, sq_ffn, wait=lambda d: act.wait_ge(sem("x_made"), 8 + d + 1))
                act_h(act, 1, 0, 3)
                dsa_in_act(act)
                dsa_qkv_act(act, lambda s: act_split(act, Q_DSA_OUT, s))
                repeat(act, AH // 2, lambda i: att_act(act, i))
                o_turn_act(act)
                plain_out(act, "act", Q_DSA_OUT, None, None, lambda s: act_split(act, Q_FFN[1], s))
                act_squares(act, 7, y_dsa, sq_dsa, wait=lambda d: act.wait_ge(y_out, 32 + d + 1))
                act_squares(act, 8, x_t, sq_dsa, wait=lambda d: act.wait_ge(sem("x_made"), 16 + d + 1))
                act_h(act, 1, 2, 5)
                ffn_act(act, 1, None)
                act_squares(act, 9, y_ffn, sq_ffn, wait=lambda d: act.wait_ge(y_out, Y_FFN[1] + 16 + d + 1))

        @block.vector
        def _(dve):
            ch = Chain(dve, sem("dve_chain"))
            dve.wait_ge(sem("vec_turned"), 1)
            nc.vector.tensor_copy(vec_t[:, :], ps[:, 6, 0:VEC]).then_inc(sem("vec_out"), 1)
            dve.wait_ge(sem("vec_out"), 1)
            ch.inc(nc.vector.tensor_copy(bias_t[:, :], ps[:, 6, 128:224]))
            ch(nc.vector.tensor_copy(conv_t[:, :, :], ps[:, 6, 256:352].rearrange("p (j k) -> p j k", j=CONV)))
            dve.wait_ge(sem("c_made"), 1)
            for j in range(4):
                for part in range(4):
                    dve_ada(dve, ch, j, part)
                dve_ada_out(dve, ch, j)
            dve_coef(dve, ch, 0, [0])
            for s in range(4):
                dve_split(dve, 0, s)
            dve.wait_ge(sem("ba_rounded"), 1)
            nc.vector.tensor_tensor(ba_lo[:, :, :], ba_raw[:, :, :], f32(ba_hi[:, :, :]), ALU.subtract)\
                .then_inc(sem("ba_split"), 1)
            dve_var(dve, 0)
            dve_h(dve, ch, 0, 0, 0, 0)

            def gdn_turn(i):
                for s in range(4):
                    dve_ada_beside(dve, ch, i + 4, s)
                    gdn_conv_dve(dve, ch, i, s)
                    dve_split(dve, i + 1, s)

            repeat(dve, N_CONV, gdn_turn, ch)
            for i in range(N_CONV, N_GDN_IN):
                for s in range(4):
                    dve_ada_beside(dve, ch, i + 4, s)
                    dve_split(dve, i + 1, s)
                if i == N_CONV:
                    dve_gates(dve, ch)
                    dve_factors(dve, ch)
            dve_ada_out(dve, ch, 11)
            dve_coef(dve, ch, 0, [1, 2, 3])
            dve.wait_ge(sem("consts"), 2)
            free_for_core(dve)
            core_loop(lambda *a: core_dve(dve, ch, *a), lambda *a: core_start_dve(dve, ch, *a), None, dve, ch)
            gdn_norm_dve(dve, ch)
            plain_out(dve, "dve", Q_GDN_OUT, y_gdn, 0, lambda s: dve_split(dve, Q_FFN[0], s))
            dve.wait_ge(y_out, 8)
            dve_var(dve, 1)
            dve_residual(dve, ch, 1, 0, 1, y_gdn, 0)
            dve_var(dve, 2)
            dve_h(dve, ch, 2, 0, 2, 2)
            ffn_dve(dve, ch, 0, (lambda s: dve_split(dve, Q_DSA, s)) if stop > 1 else None)
            dve_coef(dve, ch, 1, [0, 1, 2, 3])
            dve.wait_ge(y_out, Y_FFN[0] + 24)
            dve_var(dve, 3)
            dve_residual(dve, ch, 3, 0, 3, y_ffn, 1)
            if stop > 1:
                dve_var(dve, 4)
                dve_h(dve, ch, 4, 1, 0, 3)
                dsa_in_dve(dve, ch)
                indexer_dve(dve, ch, 1)
                for s in range(4):
                    dsa_split_dve(dve, 2, s)
                for b in range(2, NB):
                    indexer_dve(dve, ch, b)
                for s in range(4):
                    dve_split(dve, Q_DSA_OUT, s)
                repeat(dve, AH // 2, lambda i: att_dve(dve, ch, i), ch)
                o_turn_dve(dve, 4)
                plain_out(dve, "dve", Q_DSA_OUT, y_dsa, 32, lambda s: dve_split(dve, Q_FFN[1], s))
                dve.wait_ge(y_out, 40)
                dve_var(dve, 7)
                dve_residual(dve, ch, 7, 1, 1, y_dsa, 2)
                dve_var(dve, 8)
                dve_h(dve, ch, 8, 1, 2, 5)
                ffn_dve(dve, ch, 1, None)
                dve.wait_ge(y_out, Y_FFN[1] + 24)
                dve_var(dve, 9)
                dve_residual(dve, ch, 9, 1, 3, y_ffn, 3)
            for t in range(2 * NB):
                dve.wait_ge(sem("x_back"), t + 1)
                nc.vector.tensor_copy(o_out[:, t // 2, t % 2 * 512:t % 2 * 512 + 512], ps[:, t % 4, :])\
                    .then_inc(sem("x_out"), 1)

        @block.tensor
        def _(pe):
            pe.wait_ge(sem("consts"), 1)
            pe.wait_ge(vec_in, 16 * 7)
            for at, t, n in ((0, row_vec, VEC), (128, row_bias, 96), (256, row_conv, 96)):
                last = nc.tensor.transpose(ps[:, 6, at:at + n], t[:, :], ident[0:n, 0:n])
            last.then_inc(sem("vec_turned"), 1)
            pe.wait_ge(x_in, 16)
            for d in range(DC):
                if d >= 4:
                    pe.wait_ge(sem("x_here"), d - 3)
                for b in range(NB):
                    last = nc.tensor.transpose(ps[:, d % 4, b * P:(b + 1) * P], x_tok[:, b, d * P:(d + 1) * P],
                                               ident[:, :])
                last.then_inc(sem("x_turned"), 1)
            for j in range(4):
                pe_ada(pe, j)
            pe_stats(pe, 0, sq_gdn)
            pe_bcast(pe, 0)

            def gdn_turn(i, sums=False):
                for s in range(4):
                    def free():
                        if not (isinstance(i, int) and i == 0):
                            pe.wait_ge(sem("gdn_out_of_ps"), i * 4 - 3 + s)

                    def ready(k):
                        if isinstance(i, int) and i == 0 and s == 0:
                            pe.wait_ge(sem("h_made"), k + 1)

                    pe_tile(pe, i, s, h_hi, h_lo, before=free, ready=ready)
                    if s == 0 and not (isinstance(i, int) and i == 0):
                        pe_ada(pe, i + 3)
                    if sums and QKV < i * 4 + s <= QKV + 4:
                        pe_qk_sums(pe, i * 4 + s - QKV - 1)
                    if sums and i * 4 + s == QKV + 4:
                        pe_g_sums(pe)
                    if sums and i * 4 + s == QKV:
                        pe_gates(pe)
                    if sums and i * 4 + s == QKV + 1:
                        pe_gates_turn(pe)

            repeat(pe, N_CONV, gdn_turn)
            for i in range(N_CONV, N_GDN_IN):
                gdn_turn(i, sums=True)
            pe_ada(pe, 11)
            pe.wait_ge(sem("consts"), 2)
            pe.wait_ge(sem("gdn_out_of_ps"), 4 * N_GDN_IN)
            core_loop(lambda *a: core_pe(pe, *a), lambda *a: core_start_pe(pe, *a),
                      lambda *a: core_end_pe(pe, *a), pe)
            gdn_norm_pe(pe)
            for j in range(2):
                for s in range(4):
                    pe_tile(pe, Q_GDN_OUT + j, s, h_hi, h_lo,
                            before=(lambda: pe.wait_ge(y_out, s + 1)) if j else None,
                            ready=(lambda k: pe.wait_ge(sem("h_made"), 8 + k + 1)) if j == s == 0 else None)
            pe_stats(pe, 1, sq_gdn)
            pe_bcast(pe, 1)
            pe_stats(pe, 2, sq_gdn)
            pe_bcast(pe, 2)
            ffn_pe(pe, 0, 2)
            pe_stats(pe, 3, sq_ffn)
            pe_bcast(pe, 3)
            if stop > 1:
                pe_stats(pe, 4, sq_ffn)
                pe_bcast(pe, 4)
                dsa_in_pe(pe, 3)
                indexer_pe(pe, 1)
                dsa_q_pe(pe)
                indexer_pe(pe, 2)
                dsa_k_pe(pe)
                indexer_pe(pe, 3)
                dsa_v_pe(pe)
                repeat(pe, AH // 2, lambda i: att_pe(pe, i))
                o_turn_pe(pe, 4)
                for j in range(2):
                    for s in range(4):
                        pe_tile(pe, Q_DSA_OUT + j, s, h_hi, h_lo,
                                before=(lambda: pe.wait_ge(y_out, 32 + s + 1)) if j else None,
                                ready=(lambda k: pe.wait_ge(sem("h_made"), 40)) if j == s == 0 else None)
                pe_stats(pe, 7, sq_dsa)
                pe_bcast(pe, 7)
                pe_stats(pe, 8, sq_dsa)
                pe_bcast(pe, 8)
                ffn_pe(pe, 1, 5)
                pe_stats(pe, 9, sq_ffn)
                pe_bcast(pe, 9)
            pe.wait_ge(sem("x_made"), 32 if stop > 1 else 16)
            for t in range(2 * NB):
                if t >= 4:
                    pe.wait_ge(sem("x_out"), t - 3)
                b = t // 2
                for r in range(4):
                    last = nc.tensor.transpose(ps[:, t % 4, r * P:(r + 1) * P],
                                               x_t[:, t % 2 * 4 + r, b * P:(b + 1) * P], ident[:, :])
                last.then_inc(sem("x_back"), 1)


_INS = ["x", "c", "ada_w", "ada_b", "norm_g", "ffn_w_in", "ffn_w_out", "gdn_w_in", "gdn_conv_w", "gdn_a_log",
        "gdn_dt_bias", "gdn_norm_g", "gdn_w_out", "dsa_w_in", "dsa_q_norm_g", "dsa_kv_norm_g", "dsa_w_uq",
        "dsa_w_uk", "dsa_w_uv", "dsa_w_qidx", "dsa_kidx_ln_g", "dsa_kidx_ln_b", "dsa_w_out"]
_OUTS = [((1, 512, 1024), "float32")]


def kernel(**inputs):
    import numpy as _np
    import concourse.bacc as _bacc
    from concourse import mybir as _mybir
    from concourse.bass_utils import run_bass_kernel_spmd as _run

    nc = _bacc.Bacc("TRN2", target_bir_lowering=False, num_devices=1)
    arrays, args = {}, []
    for name in _INS:
        a = _np.ascontiguousarray(inputs[name])
        arrays[f"in_{name}_dram"] = a
        args.append(nc.dram_tensor(f"in_{name}_dram", a.shape, _mybir.dt.from_np(a.dtype), kind="ExternalInput").ap())
    for i, (shape, dtype) in enumerate(_OUTS):
        dt = _mybir.dt.from_np(_np.dtype(dtype))
        args.append(nc.dram_tensor(f"out_{i}_dram", shape, dt, kind="ExternalOutput").ap())
    build_trunk(nc, *args)
    r = _run(nc, [arrays], core_ids=[0])
    return r.results[0]["out_0_dram"]
```

```python
from contextlib import ExitStack

import concourse.bass as bass
from concourse import mybir

F32 = mybir.dt.float32
F32R = mybir.dt.float32r
ALU = mybir.AluOpType
ACT = mybir.ActivationFunctionType
AX_X = mybir.AxisListType.X

P = 128
BIG = 1.0e30
TAKEN = -3.0e38
EPS = 1e-6


class Chain:

    def __init__(self, eng, sem):
        self.eng, self.sem, self.n, self.turns = eng, sem, 0, None

    def inc(self, ins):
        ins.then_inc(self.sem, 1)
        self.n += 1

    def wait(self):
        self.eng.wait_ge(self.sem, self.n if self.turns is None else self.turns + self.n)

    def __call__(self, ins):
        self.inc(ins)
        self.wait()

    def behind(self, ins):
        self.inc(ins)
        self.eng.wait_ge(self.sem, self.n - 1)


def repeat(eng, n, body, chain=None, first=0):
    start = chain.n if chain else 0
    body(first)
    per = chain.n - start if chain else 0
    rest = n - first - 1
    if rest < 3:
        for i in range(first + 1, n):
            body(i)
        return
    with eng.Fori(first + 1, n) as i:
        if chain:
            chain.turns = i * per - (first + 1) * per
        body(i)
    if chain:
        assert chain.n == start + 2 * per, (chain.n, start, per)
        chain.turns = None
        chain.n = start + per * (rest + 1)


def over_heads(square, n=4):
    return square.unsqueeze(1).to_broadcast([P, n, square.shape[-1]])


def along(cols, m=P):
    return cols.unsqueeze(2).to_broadcast([P, cols.shape[-1], m])


def build_trunk(nc, x, c, ada_w, ada_b, norm_g, ffn_w_in, ffn_w_out,
                gdn_w_in, gdn_conv_w, gdn_a_log, gdn_dt_bias, gdn_norm_g, gdn_w_out,
                dsa_w_in, dsa_q_norm_g, dsa_kv_norm_g, dsa_w_uq, dsa_w_uk, dsa_w_uv,
                dsa_w_qidx, dsa_kidx_ln_g, dsa_kidx_ln_b, dsa_w_out, out):
    _, S, D = x.shape
    DC = D // P
    NB = S // P
    FC = ffn_w_out.shape[1] // P
    H = gdn_a_log.shape[1]
    CONV = gdn_conv_w.shape[1]
    QKV = gdn_conv_w.shape[2] // P
    HG = 4
    NG = H // HG
    LEVELS = 7
    AH, DH, LAT = dsa_w_uk.shape[1:]
    LC = LAT // P
    IH = dsa_w_qidx.shape[2] // DH
    SMALL = DH + IH
    TOPK = min(256, S // 4)
    PARTS = [8, 8, 6]
    assert S == 512 and D == 1024 and H == 8 and QKV == 24 and sum(PARTS) == FC
    assert LAT == 256 and DH == 64 and AH == 16 and IH == 8 and TOPK == P

    Q_GDN_IN = 0
    N_GDN_IN = (QKV + H) // 4
    Q_GDN_OUT = Q_GDN_IN + N_GDN_IN
    Q_FFN = [Q_GDN_OUT + 2, 0]
    N_FFN = sum(p // 2 + 2 for p in PARTS)
    Q_DSA = Q_FFN[0] + N_FFN
    Q_DSA_OUT = Q_DSA + 3
    Q_FFN[1] = Q_DSA_OUT + 2

    with ExitStack() as ctx:
        place = [(nc.sbuf_base + 31) // 32 * 32]

        def fixed(name, shape, dt=F32, at=None):
            size = 4
            for n in shape[1:]:
                size *= n
            size = (size + 31) // 32 * 32
            if at is None:
                at = place[0]
                place[0] += size
                assert place[0] <= nc.sbuf_usable_end, name
            t = nc.alloc_sbuf_tensor_at(name, shape, dt, offset=at)
            return t

        class Region:
            def __init__(self, at):
                self.at = at

            def __call__(self, name, shape, dt=F32):
                size = 4
                for n in shape[1:]:
                    size *= n
                t = fixed(name, shape, dt, at=self.at)
                self.at += (size + 31) // 32 * 32
                assert self.at <= nc.sbuf_usable_end, name
                return t

        ident = fixed("ident", [P, P])
        ones = fixed("ones", [P, P])
        upto = fixed("upto", [P, P])
        mask_l = fixed("mask_l", [P, P])
        mask_t = fixed("mask_t", [P, P])
        first_l = fixed("first_l", [P, P])
        first_t = fixed("first_t", [P, P])
        level_t = fixed("level_t", [P, LEVELS, P])
        causal = fixed("causal", [P, P])
        ln_gb = fixed("ln_gb", [P, 2, DH])
        half = fixed("half", [P, 64])
        VEC = DC + 8 * DC + 1 + 2 * LC
        vec_t = fixed("vec_t", [P, VEC])
        gnorm = vec_t[:, 9 * DC:9 * DC + 1]
        qn_g = vec_t[:, 9 * DC + 1:VEC].rearrange("p (a k) -> p a k", a=2)
        bias_t = fixed("bias_t", [P, 96])
        conv_t = fixed("conv_t", [P, CONV, QKV])
        mod = fixed("mod", [P, 96])
        c_act = fixed("c_act", [P, DC])
        coef = fixed("coef", [P, 2, 4, DC])
        raw = [fixed(f"raw{i}", [P, 8, 256]) for i in range(2)]
        w_hi = fixed("w_hi", [P, 4, 1024], F32R)
        w_lo = fixed("w_lo", [P, 4, 1024], F32R)
        x_t = fixed("x_t", [P, DC, S])
        small_at = place[0]
        diag = fixed("diag", [P, NB, P])
        tmp = fixed("tmp", [P, 3, S])
        var = fixed("var", [P, 32])
        rinv = fixed("rinv", [P, 32])
        ada_acc = fixed("ada_acc", [P, 512])
        h_base = place[0]
        h_hi = fixed("h_hi", [P, DC, S], F32R)
        h_lo = fixed("h_lo", [P, DC, S], F32R)
        ada_base = place[0]
        ada_in = [fixed(f"ada_in{i}", [P, 4, 512]) for i in range(2)]
        phase = place[0]

        pre = Region(phase)
        x_tok = pre("x_tok", [P, NB, D])
        row_vec = pre("row_vec", [VEC, P])
        row_bias = pre("row_bias", [96, P])
        row_conv = pre("row_conv", [96, P])

        early_slab = {j: [pre(f"early_slab{j}{i}", [P, 4, 512]) for i in range(2)] for j in (2, 3)}
        assert pre.at <= phase + 65536
        sq_first = fixed("sq_first", [P, DC, S], at=h_base)

        gdn = Region(phase)
        qkv_at = gdn.at
        qkv = gdn("qkv", [P, QKV, S])
        z_t = gdn("z_t", [P, H, S])
        state = gdn("state", [P, H, P])
        ba_at = gdn.at
        ba_raw = gdn("ba_raw", [P, DC, 2 * H])
        ba_hi = gdn("ba_hi", [P, DC, 2 * H], F32R)
        ba_lo = gdn("ba_lo", [P, DC, 2 * H], F32R)
        ba = gdn("ba", [P, NB, 2 * H])
        beta = gdn("beta", [P, NB, H])
        gate = gdn("gate", [P, NB, H])
        gtmp = gdn("gtmp", [P, 2, NB, H])
        dt_b = gdn("dt_b", [P, 2, H])
        gsum = gdn("gsum", [P, 3, NB, H])
        gexp = fixed("gexp", [P, 3, NB, H], at=ba_at)
        l2 = gtmp[:, :, :, :].rearrange("p a b c -> p (a b c)").rearrange("p (a b) -> p a b", a=NB)
        l2r = gdn("l2r", [P, NB, 2 * H])
        q_f = gdn("q_f", [P, NB, H])
        qg_f = gdn("qg_f", [P, NB, H])
        kb_f = gdn("kb_f", [P, NB, H])
        kl_f = gdn("kl_f", [P, NB, H])
        conv_u = [gdn(f"conv_u{i}", [P, S + 8]) for i in range(2)]
        conv_a = [tmp[:, i, :] for i in range(2)]
        y_gdn = fixed("y_gdn", [P, DC, S], at=qkv_at + 16384)
        sq_gdn = fixed("sq_gdn", [P, DC, S], at=qkv_at + 32768)
        def at_h(i):
            return h_base + 2048 * i

        room = ([small_at + 2048 * i for i in range(4)] + [at_h(i) for i in (0, 1, 2, 3, 8, 9, 10, 11)]
                + [ada_base + 2048 * i for i in range(8)] + [at_h(i) for i in (4, 5, 6, 7, 12, 13, 14, 15)])
        slot_names = "A B C D E F G H I J K M N O".split()
        slots = [{n: fixed(f"m{g}{n}", [P, HG, P], at=room.pop(0)) for n in slot_names}
                 for g in range(NG)]

        ffn = Region(phase)
        g_hi = ffn("g_hi", [P, 8, S], F32R)
        g_lo = ffn("g_lo", [P, 8, S], F32R)
        y_ffn = ffn("y_ffn", [P, DC, S])
        silu_g = ffn("silu_g", [P, 2, S])
        gated = ffn("gated", [P, 2, S])
        sq_ffn = ffn("sq_ffn", [P, DC, S])

        dsa = Region(phase)
        o_tok_at = dsa.at
        uk_hi = dsa("uk_hi", [P, LC, 1024], F32R)
        uk_lo = dsa("uk_lo", [P, LC, 1024], F32R)
        cq_hi = dsa("cq_hi", [P, LC, S], F32R)
        cq_lo = dsa("cq_lo", [P, LC, S], F32R)
        ckv_hi = dsa("ckv_hi", [P, LC, S], F32R)
        ckv_lo = dsa("ckv_lo", [P, LC, S], F32R)
        q_at = dsa.at
        q_t = dsa("q_t", [P, 8, S])
        k_at = dsa.at
        k_t = dsa("k_t", [P, 8, S])
        kx = dsa("kx", [P, NB, SMALL])
        kn = dsa("kn", [P, NB, 2 * DH])
        kn_t = dsa("kn_t", [P, S])
        kx_t = kn_t
        mean = dsa("mean", [P, NB])
        score = [dsa("score", [P, S]), tmp[:, 2, :]]
        best = dsa("best", [P, 2, 8])
        nmax = dsa("nmax", [P, 8])
        psum_p = dsa("psum_p", [P, 8])
        rsum = dsa("rsum", [P, 8])
        o_tok = fixed("o_tok", [P, NB, 1024], at=o_tok_at)
        latent = fixed("latent", [P, 2, LC, S], at=q_at)
        sq_lat = fixed("sq_lat", [P, 2, LC, S], at=k_at)
        att = Region(o_tok_at + 16384)
        q_st = att("q_st", [P, S])
        k_st = att("k_st", [P, S])
        s_m = att("s_m", [P, 2, S])
        p_s = att("p_s", [P, 2, S])
        p_t = att("p_t", [P, 2, S])
        y_dsa = fixed("y_dsa", [P, DC, S], at=q_at)
        sq_dsa = fixed("sq_dsa", [P, DC, S], at=k_at)
        qi_t = fixed("qi_t", [P, 4, S], at=h_base)
        mask = fixed("mask", [P, NB, S], at=h_base + 8192)
        v_tok = fixed("v_tok", [P, NB, 1024], at=h_base + 16384)
        relu = fixed("relu", [P, IH, S], at=ada_base)
        o_out = fixed("o_out", [P, NB, D], at=phase + 49152)

        ps = ctx.enter_context(nc.psum_tensor("ps", [P, 8, S], F32))

        sems = {}

        def sem(name):
            if name not in sems:
                sems[name] = ctx.enter_context(nc.semaphore(name))
            return sems[name]

        raw_in = [sem(f"raw_in{i}") for i in range(2)]
        vec_in, x_in = sem("vec_in"), sem("x_in")
        hi_done, lo_done, tile_done = sem("hi_done"), sem("lo_done"), sem("tile_done")
        ada_here = [sem(f"ada_here{i}") for i in range(2)]
        ada_late = [sem(f"ada_late{i}") for i in range(2)]
        ada_used, ada_mm = sem("ada_used"), sem("ada_mm")

        def raw_tile(s, kc=8):
            return raw[s // 2][:, 0:kc, (s % 2) * P:(s % 2 + 1) * P]

        def split_tile(w, s, kc=8):
            return w[:, s, 0:kc * P].rearrange("p (k n) -> p k n", n=P)

        def f32(t):
            return t.bitcast(F32)

        def flat(t):
            return t.rearrange("p a b -> p (a b)")

        def gain(layer, k, d):
            return vec_t[:, DC + (layer * 4 + k) * DC + d:DC + (layer * 4 + k) * DC + d + 1]

        def shift(layer, k, d):
            at = layer * 48 + k * DC + d
            return mod[:, at:at + 1]

        H_SCALED = {0: 0, 2: 1, 3: 2, 5: 3}
        SQ_BASE = [0, 8, 16, 24, 32, 40, 42, 44, 52, 60]

        def load_quad(sp, q, src_a, src_b, kc=8):
            for side, src in enumerate((src_a, src_b)):
                if not (isinstance(q, int) and q == 0):
                    sp.wait_ge(lo_done, q * 4 - 2 + 2 * side)
                if isinstance(src, list):
                    for dst, part, signal in src:
                        sp.dma_start(dst, part).then_inc(signal, 16)
                else:
                    sp.dma_start(raw[side][:, 0:kc, :], src).then_inc(raw_in[side], 16)

        def slab_here(j):
            if not isinstance(j, int) or j > 3:
                return ada_late
            return ada_here if j < 2 else [sem(f"slab_here{j}")] * 2

        def slab_place(j):
            return early_slab[j] if isinstance(j, int) and j in (2, 3) else ada_in

        def load_ada(sp, layer, jj):
            j = jj + 12 * layer
            src = ada_w[layer].rearrange("(b k p) n -> b p k n", b=2, p=P)
            for b in range(2):
                if not (isinstance(j, int) and j in (0, 2, 3)):
                    sp.wait_ge(ada_used, j * 2 - 1 + b)
                sp.dma_start(slab_place(j)[b][:, :, :], src[b][:, :, bass.ds(jj * 512, 512)])\
                    .then_inc(slab_here(j)[b], 16)

        def rows(w):
            return w.rearrange("(k p) n -> p k n", p=P)

        def act_split(act, q, s, kc=8, src=None, dst=None):
            act.wait_ge(raw_in[s // 2], q * 16 + 16)
            if not (isinstance(q, int) and q == 0):
                act.wait_ge(tile_done, q * 4 + s - 3)
            nc.scalar.activation(split_tile(w_hi, s, kc) if dst is None else dst(w_hi),
                                 raw_tile(s, kc) if src is None else src, ACT.Copy).then_inc(hi_done, 1)

        def split(eng, ops, q, s, kc=8, src=None, dst=None):
            eng.wait_ge(hi_done, q * 4 + s + 1)
            lo, hi = (split_tile(w, s, kc) if dst is None else dst(w) for w in (w_lo, w_hi))
            ops.tensor_tensor(lo, raw_tile(s, kc) if src is None else src, f32(hi),
                              ALU.subtract).then_inc(lo_done, 1)

        def dve_split(dve, q, s, kc=8, src=None, dst=None):
            split(dve, nc.vector, q, s, kc, src, dst)

        def pe_tile(pe, q, s, r_hi, r_lo, kc=8, before=None, ready=None):
            pe.wait_ge(lo_done, q * 4 + s + 1)
            if before:
                before()
            hi, lo = split_tile(w_hi, s, kc), split_tile(w_lo, s, kc)
            for k in range(kc):
                if ready:
                    ready(k)
                nc.tensor.matmul(ps[:, s, :], hi[:, k, :], r_hi[:, k, :], start=k == 0, stop=False)
                nc.tensor.matmul(ps[:, s, :], hi[:, k, :], r_lo[:, k, :], start=False, stop=False)
                last = nc.tensor.matmul(ps[:, s, :], lo[:, k, :], r_hi[:, k, :], start=False, stop=k == kc - 1)
            last.then_inc(tile_done, 1)

        def pe_first_quad(pe, q, r_hi, r_lo, ready, before=None, after=None, between=None):
            side = 2
            pe.wait_ge(lo_done, q * 4 + 4)
            for s in range(4):
                if before:
                    before(s)

            def product(s, k):
                hi, lo = split_tile(w_hi, s)[:, k, :], split_tile(w_lo, s)[:, k, :]
                nc.tensor.matmul(ps[:, s, :], hi, r_hi[:, k, :], start=k == 0, stop=False)
                nc.tensor.matmul(ps[:, s, :], hi, r_lo[:, k, :], start=False, stop=False)
                return nc.tensor.matmul(ps[:, s, :], lo, r_hi[:, k, :], start=False, stop=k == DC - 1)

            for k in range(side):
                ready(k)
                for s in range(4):
                    product(s, k)
                if between:
                    between(k)
            for s in range(4):
                for k in range(side, DC):
                    if s == 0:
                        ready(k)
                    last = product(s, k)
                    if between and s == 0 and k < DC // 2:
                        between(k)
                last.then_inc(tile_done, 1)
                if after:
                    after(s)

        def dve_ada(dve, ch, j, quarter):
            b = quarter // 2
            if quarter % 2 == 0:
                if isinstance(j, int) and j < 4:
                    dve.wait_ge(slab_here(j)[b], (16, 32, 32, 32)[j])
                else:
                    dve.wait_ge(ada_late[b], j * 16 - 48)
            for k in (quarter % 2 * 2, quarter % 2 * 2 + 1):
                cc = c_act[:, 4 * b + k:4 * b + k + 1]
                if b == 0 and k == 0:
                    ins = nc.vector.tensor_scalar(ada_acc[:, :], slab_place(j)[b][:, k, :], cc, None, ALU.mult)
                else:
                    ins = nc.vector.scalar_tensor_tensor(ada_acc[:, :], slab_place(j)[b][:, k, :], cc,
                                                         ada_acc[:, :], ALU.mult, ALU.add)
                if k == 3:
                    ins.then_inc(ada_used, 1)
                    dve.wait_ge(ada_used, j * 2 + b + 1)
                else:
                    ch(ins)

        def dve_ada_beside(dve, ch, j, s):
            if s == 1:
                dve_ada_out(dve, ch, j - 1)
            for quarter in ((), (0,), (1,), (2, 3))[s]:
                dve_ada(dve, ch, j, quarter)

        def pe_ada(pe, j):
            pe.wait_ge(ada_used, j * 2 + 2)
            for n in range(4):
                last = nc.tensor.matmul(ps[:, 7, n:n + 1], ada_acc[:, n * P:(n + 1) * P], ones[:, 0:1],
                                        start=True, stop=True)
            last.then_inc(ada_mm, 1)

        def dve_ada_out(dve, ch, j):
            dve.wait_ge(ada_mm, j + 1)
            ch(nc.vector.tensor_tensor(mod[:, bass.ds(j * 4, 4)], ps[:, 7, 0:4],
                                       bias_t[:, bass.ds(j * 4, 4)], ALU.add))

        def dve_coef(dve, ch, layer, ks):
            for k in ks:
                m = layer * 48 + (1, 2, 4, 5)[k] * DC
                g0 = DC + (layer * 4 + k) * DC
                ch(nc.vector.scalar_tensor_tensor(coef[:, layer, k, :], mod[:, m:m + DC], 1.0,
                                                  vec_t[:, g0:g0 + DC], ALU.add, ALU.mult))

        def act_square(act, src, sq, d):
            nc.scalar.activation(sq[:, d, :], src[:, d, :], ACT.Square).then_inc(sem("sq_made"), 1)

        def act_squares(act, n, src, sq, chunks=DC, wait=None):
            for d in range(chunks):
                if wait:
                    wait(d)
                act_square(act, src, sq, d)

        def pe_stat(pe, n, sq, d, chunks=DC):
            pe.wait_ge(sem("sq_made"), SQ_BASE[n] + d + 1)
            for b in range(NB):
                last = nc.tensor.matmul(ps[:, 4, b * P:(b + 1) * P], sq[:, d, b * P:(b + 1) * P], ones[:, :],
                                        start=d == 0 and b == 0, stop=d == chunks - 1,
                                        skip_group_check=True)
            if d == chunks - 1:
                last.then_inc(sem("stat_made"), 1)

        def pe_stats(pe, n, sq, chunks=DC):
            for d in range(chunks):
                pe_stat(pe, n, sq, d, chunks)

        def pe_stat_behind(pe, n, sq, t):
            if t:
                pe_stat(pe, n, sq, t - 1)
            if t == DC - 1:
                pe_stat(pe, n, sq, t)

        def dve_var(dve, n, width=D):
            dve.wait_ge(sem("stat_made"), n + 1)
            nc.vector.tensor_scalar(var[:, 0:NB], ps[:, 4, 0:NB * P:P], 1.0 / width, EPS,
                                    ALU.mult, ALU.add).then_inc(sem("var_made"), 1)
            dve.wait_ge(sem("rinv_made"), n + 1)
            nc.vector.tensor_tensor(diag[:, :, :], over_heads(ident[:, :]), along(rinv[:, 0:NB]),
                                    ALU.mult).then_inc(sem("diag_made"), 1)

        def pool_root(pool, n):
            pool.wait_ge(sem("var_made"), n + 1)
            nc.gpsimd.tensor_tensor(rinv[:, 0:NB], var[:, 0:NB], half[:, 0:NB], ALU.pow)\
                .then_inc(sem("rinv_made"), 1)

        def pe_bcast(pe, n):
            pe.wait_ge(sem("diag_made"), n + 1)
            nc.tensor.matmul(ps[:, 5, :], ones[:, :], flat(diag[:, :, :]), start=True, stop=True)\
                .then_inc(sem("root_out"), 1)

        def dve_residual(dve, n, layer, k, y, m):
            dve.wait_ge(sem("root_out"), n + 1)
            for d in range(DC):
                if d >= 3 and (d - 3) % 2:
                    dve.wait_ge(sem("x_pool"), 4 * m + (d - 3) // 2 + 1)
                nc.vector.scalar_tensor_tensor(tmp[:, d % 3, :], ps[:, 5, :], coef[:, layer, k, d:d + 1],
                                               y[:, d, :], ALU.mult, ALU.mult).then_inc(sem("y_scaled"), 1)
                if d % 2 == 0:
                    dve.wait_ge(sem("y_scaled"), 8 * m + d + 1)
                    nc.vector.tensor_tensor(x_t[:, d, :], x_t[:, d, :], tmp[:, d % 3, :], ALU.add)\
                        .then_inc(sem("x_made"), 1)
                    dve.wait_ge(sem("x_made"), 4 * m + d // 2 + 1)
            dve.wait_ge(sem("x_pool"), 4 * m + 4)

        def pool_residual(pool, m):
            for d in range(1, DC, 2):
                pool.wait_ge(sem("y_scaled"), 8 * m + d + 1)
                nc.gpsimd.tensor_tensor(x_t[:, d, :], x_t[:, d, :], tmp[:, d % 3, :], ALU.add)\
                    .then_inc(sem("x_pool"), 1)

        def x_ready(eng, m, d):
            eng.wait_ge(sem("x_pool" if d % 2 else "x_made"), 4 * m + d // 2 + 1)

        def dve_h(dve, n, layer, k, m):
            dve.wait_ge(sem("root_out"), n + 1)

            def low(d):
                dve.wait_ge(sem("h_rounded"), 8 * m + d + 1)
                nc.vector.scalar_tensor_tensor(h_lo[:, d, :], tmp[:, d % 3, :], shift(layer, 3 * (k // 2), d),
                                               f32(h_hi[:, d, :]), ALU.add, ALU.subtract)\
                    .then_inc(sem("h_made"), 1)
                dve.wait_ge(sem("h_made"), 8 * m + d + 1)

            for d in range(DC):
                nc.vector.scalar_tensor_tensor(tmp[:, d % 3, :], ps[:, 5, :], coef[:, layer, k, d:d + 1],
                                               x_t[:, d, :], ALU.mult, ALU.mult).then_inc(sem("h_scaled"), 1)
                if d:
                    low(d - 1)
            low(DC - 1)

        def h_here(eng, m, d):
            eng.wait_ge(sem("h_made"), 8 * m + d + 1)

        def act_h(act, layer, k, m):
            for d in range(DC):
                act.wait_ge(sem("h_scaled"), 8 * H_SCALED[m] + d + 1)
                nc.scalar.activation(h_hi[:, d, :], tmp[:, d % 3, :], ACT.Identity,
                                     bias=shift(layer, 3 * (k // 2), d)).then_inc(sem("h_rounded"), 1)

        def gdn_in_act(act, i, s, conv):
            act.wait_ge(tile_done, i * 4 + s + 1)
            if conv:
                nc.scalar.activation(conv_u[s % 2][:, 3:3 + S], ps[:, s, :], ACT.Copy)
                nc.scalar.activation(conv_a[s % 2], ps[:, s, :], ACT.Identity,
                                     scale=conv_t[:, CONV - 1, bass.ds(i * 4 + s, 1)]).then_inc(sem("gdn_out_of_ps"), 1)
            else:
                nc.scalar.activation(z_t[:, i * 4 + s - QKV, :], ps[:, s, :], ACT.Silu)\
                    .then_inc(sem("gdn_out_of_ps"), 1)

        def gdn_conv_act(act, i, s):
            act.wait_ge(sem("conv_made"), i * 4 + s + 1)
            nc.scalar.activation(qkv[:, i * 4 + s, :] if isinstance(i, int) else
                                 qkv[:, bass.ds(i * 4 + s, 1), :].rearrange("p a b -> p (a b)"),
                                 conv_a[s % 2], ACT.Silu).then_inc(sem("qkv_made"), 1)

        def gdn_conv_dve(dve, ch, i, s):
            dve.wait_ge(sem("gdn_out_of_ps"), i * 4 + s + 1)
            for j in range(CONV - 1):
                ins = nc.vector.scalar_tensor_tensor(conv_a[s % 2], conv_u[s % 2][:, j:j + S],
                                                     conv_t[:, j, bass.ds(i * 4 + s, 1)],
                                                     conv_a[s % 2], ALU.mult, ALU.add)
                if j < CONV - 2:
                    ch(ins)
                else:
                    ins.then_inc(sem("conv_made"), 1)

        N_CONV = QKV // 4
        sq_ring = [tmp[:, 0, :], tmp[:, 1, :], conv_u[0][:, 0:S], conv_u[1][:, 0:S]]

        def act_qk_squares(act, t):
            act.wait_ge(sem("qkv_made"), QKV)
            for j in range(4 * t, 4 * t + 4):
                if j >= 4:
                    act.wait_ge(sem("qk_sum"), j - 3)
                nc.scalar.activation(sq_ring[j % 4], qkv[:, j, :], ACT.Square).then_inc(sem("qk_sq"), 1)

        def pe_qk_sums(pe, t):
            for j in range(4 * t, 4 * t + 4):
                pe.wait_ge(sem("qk_sq"), j + 1)
                for b in range(NB):
                    at = j * NB + b
                    last = nc.tensor.matmul(ps[:, 4, at:at + P], sq_ring[j % 4][:, b * P:(b + 1) * P],
                                            ones[:, :], start=True, stop=True)
                last.then_inc(sem("qk_sum"), 1)

        def pe_gates(pe):
            pe.wait_ge(sem("ba_split"), 1)
            for k in range(DC):
                nc.tensor.matmul(ps[0:2 * H, 6, :], ba_hi[:, k, :], h_hi[:, k, :], start=k == 0, stop=False)
                nc.tensor.matmul(ps[0:2 * H, 6, :], ba_hi[:, k, :], h_lo[:, k, :], start=False, stop=False)
                last = nc.tensor.matmul(ps[0:2 * H, 6, :], ba_lo[:, k, :], h_hi[:, k, :],
                                        start=False, stop=k == DC - 1)
            last.then_inc(sem("gates_mm"), 1)

        def act_gates_out(act):
            act.wait_ge(sem("gates_mm"), 1)
            nc.scalar.activation(tmp[0:2 * H, 2, :], ps[0:2 * H, 6, :], ACT.Copy).then_inc(sem("small_out"), 1)

        def pe_gates_turn(pe):
            pe.wait_ge(sem("small_out"), 1)
            for b in range(NB):
                last = nc.tensor.transpose(ps[:, 5, b * 2 * H:(b + 1) * 2 * H], tmp[0:2 * H, 2, b * P:(b + 1) * P],
                                           ident[0:2 * H, 0:2 * H])
            last.then_inc(sem("small_turned"), 1)

        def dve_gates(dve, ch):
            dve.wait_ge(sem("small_turned"), 1)
            ch(nc.vector.tensor_copy(ba[:, :, :], ps[:, 5, 0:NB * 2 * H].rearrange("p (a b) -> p a b", a=NB)))
            a_in, g0, g1 = ba[:, :, H:2 * H], gtmp[:, 0, :, :], gtmp[:, 1, :, :]
            ch(nc.vector.tensor_tensor(a_in, a_in, dt_b[:, 0, :].unsqueeze(1).to_broadcast([P, NB, H]), ALU.add))
            ch(nc.vector.tensor_scalar(g0, a_in, -1.0, None, ALU.mult))
            nc.vector.tensor_tensor(g0, g0, a_in, ALU.min).then_inc(sem("gate_abs"), 1)
            dve.wait_ge(sem("gate_exp"), 3)
            ch(nc.vector.tensor_scalar(beta[:, :, :], beta[:, :, :], 1.0, None, ALU.add))
            ch(nc.vector.reciprocal(beta[:, :, :], beta[:, :, :]))
            ch(nc.vector.tensor_scalar(g1, g1, 1.0, None, ALU.add))
            nc.vector.tensor_scalar(a_in, a_in, 0.0, None, ALU.max).then_inc(sem("gate_abs"), 1)
            dve.wait_ge(sem("gate_abs"), 2)
            dve.wait_ge(sem("gate_exp"), 4)
            ch(nc.vector.tensor_tensor(g0, g1, a_in, ALU.add))
            nc.vector.scalar_tensor_tensor(gate[:, :, :], g0, -1.0,
                                           dt_b[:, 1, :].unsqueeze(1).to_broadcast([P, NB, H]),
                                           ALU.mult, ALU.mult).then_inc(sem("gate_made"), 1)
            dve.wait_ge(sem("gate_made"), 1)

        def pe_g_sums(pe):
            pe.wait_ge(sem("gate_made"), 1)
            g_all = gate[:, :, :].rearrange("p a b -> p (a b)")
            nc.tensor.matmul(ps[:, 6, 0:NB * H], upto[:, :], g_all, start=True, stop=True)
            nc.tensor.matmul(ps[:, 6, NB * H:2 * NB * H], ones[:, :], g_all, start=True, stop=True)\
                .then_inc(sem("g_sums_mm"), 1)

        def pool_qk_root(pool):
            pool.wait_ge(sem("small_sum"), 1)
            nc.gpsimd.tensor_tensor(l2r[:, :, :], l2[:, :, :],
                                    half[:, 0:NB * 2 * H].rearrange("p (a b) -> p a b", a=NB), ALU.pow)\
                .then_inc(sem("small_root"), 1)

        def act_g_exp(act):
            act.wait_ge(sem("g_sums_made"), 1)
            nc.scalar.activation(gexp[:, :, :, :], gsum[:, :, :, :], ACT.Exp).then_inc(sem("g_exp_made"), 1)

        def dve_sums(dve, ch):
            dve.wait_ge(sem("qk_sum"), 2 * H)
            nc.vector.tensor_scalar(l2[:, :, :], ps[:, 4, 0:NB * 2 * H].rearrange("p (j b) -> p b j", b=NB),
                                    EPS, None, ALU.add).then_inc(sem("small_sum"), 1)
            dve.wait_ge(sem("g_sums_mm"), 1)
            ch(nc.vector.tensor_copy(gsum[:, 0:2, :, :],
                                     ps[:, 6, 0:2 * NB * H].rearrange("p (t a b) -> p t a b", t=2, a=NB)))
            nc.vector.tensor_tensor(gsum[:, 2, :, :], gsum[:, 1, :, :], gsum[:, 0, :, :], ALU.subtract)\
                .then_inc(sem("g_sums_made"), 1)

        def dve_factors(dve, ch):
            dve.wait_ge(sem("small_root"), 1)
            ch(nc.vector.tensor_scalar(q_f[:, :, :], l2r[:, :, 0:H], float(P) ** -0.5, None, ALU.mult))
            dve.wait_ge(sem("g_exp_made"), 1)
            ch.inc(nc.vector.tensor_tensor(qg_f[:, :, :], q_f[:, :, :], gexp[:, 0, :, :], ALU.mult))
            ch.inc(nc.vector.tensor_tensor(kl_f[:, :, :], l2r[:, :, H:2 * H], gexp[:, 2, :, :], ALU.mult))
            ch(nc.vector.tensor_tensor(kb_f[:, :, :], beta[:, :, :], gexp[:, 0, :, :], ALU.mult))
            ch(nc.vector.tensor_tensor(kb_f[:, :, :], kb_f[:, :, :], l2r[:, :, H:2 * H], ALU.mult))

        def act_gates(act):
            act.wait_ge(sem("gate_abs"), 1)
            nc.scalar.activation(beta[:, :, :], ba[:, :, 0:H], ACT.Exp, scale=-1.0).then_inc(sem("gate_exp"), 1)
            nc.scalar.activation(gtmp[:, 1, :, :], gtmp[:, 0, :, :], ACT.Exp).then_inc(sem("gate_exp"), 1)
            nc.scalar.activation(dt_b[:, 1, :], dt_b[:, 1, :], ACT.Exp).then_inc(sem("gate_exp"), 1)
            act.wait_ge(sem("gate_abs"), 2)
            nc.scalar.activation(gtmp[:, 1, :, :], gtmp[:, 1, :, :], ACT.Ln).then_inc(sem("gate_exp"), 1)

        def bank(g, n):
            return ps[:, 4 * g + n, :].rearrange("p (h n) -> p h n", h=HG)

        def first(c):
            return isinstance(c, int) and c == 0

        def heads(t, g, c):
            return t[:, c, g * HG:(g + 1) * HG] if isinstance(c, int) else \
                t[:, bass.ds(c, 1), g * HG:(g + 1) * HG].rearrange("p a b -> p (a b)")

        def tt(out, a, b, op):
            return nc.vector.tensor_tensor(out, a, b, op)

        def free_for_core(eng):
            eng.wait_ge(tile_done, 4 * N_GDN_IN)
            eng.wait_ge(ada_used, 24)

        def pool_stage(pool, g, c):
            if not first(c):
                pool.wait_ge(sem(f"w_mm{g}"), c)
            nc.gpsimd.tensor_tensor(slots[g]["J"][:, :, :], over_heads(upto[:, :]), along(heads(gate, g, c)),
                                    ALU.mult).then_inc(sem(f"g_row{g}"), 1)
            if not first(c):
                pool.wait_ge(sem(f"vnew_mm{g}"), c)
            f = 2 * H + g * HG
            nc.gpsimd.tensor_tensor(slots[g]["C"][:, :, :], qkv[:, f:f + HG, bass.ds(c * P, P)],
                                    over_heads(ones[:, :]), ALU.mult).then_inc(sem(f"v_staged{g}"), 1)

        def pool_beta(pool, g, c):
            pool.wait_ge(sem(f"decay{g}"), c * 2 + 1)
            nc.gpsimd.tensor_tensor(slots[g]["K"][:, :, :], slots[g]["K"][:, :, :], along(heads(beta, g, c)),
                                    ALU.mult).then_inc(sem(f"decay_beta{g}"), 1)

        def pool_level(pool, g, c, lv):
            if lv == 1:
                pool.wait_ge(sem(f"lt_out{g}"), c + 1)
            if lv >= 3:
                pool.wait_ge(sem(f"y_mm{g}"), c * (LEVELS - 1) + lv - 2)
            nc.gpsimd.tensor_tensor(slots[g]["JO"[lv % 2]][:, :, :], slots[g]["N"][:, :, :],
                                    over_heads(level_t[:, lv, :]), ALU.mult)\
                .then_inc(sem(f"level{g}"), 1)

        def core_pool(pool, g, c, ce, cs):
            o = 1 - g
            for lv in range(1, LEVELS):
                pool_level(pool, g, c, lv)
                if lv == 2 and cs is not None:
                    pool_stage(pool, o, cs)
                if lv == 5 and cs is not None:
                    pool_beta(pool, o, cs)

        def core_start_pool(pool, g, c):
            pool_stage(pool, g, c)
            pool_beta(pool, g, c)

        def pe_tokens(pe, g, c):
            m = slots[g]
            pe.wait_ge(sem(f"staged{g}"), c * 2 + 2)
            pe.wait_ge(sem(f"v_staged{g}"), c + 1)
            if not first(c):
                pe.wait_ge(sem(f"o_out{g}"), c)
                pe.wait_ge(sem(f"state_made{g}"), c * HG)
            for n, slot in enumerate("ABC"):
                for h in range(HG):
                    last = nc.tensor.transpose(bank(g, n)[:, h, :], m[slot][:, h, :], ident[:, :])
                last.then_inc(sem(f"qkv_tok{g}"), 1)

        def pe_sum_rows(pe, g, c):
            pe.wait_ge(sem(f"g_row{g}"), c + 1)
            nc.tensor.matmul(ps[:, 4 * g + 3, :], ones[:, :], flat(slots[g]["J"][:, :, :]),
                             start=True, stop=True).then_inc(sem(f"grow_mm{g}"), 1)

        def pe_features(pe, g, c):
            for n, slot in enumerate("ADB"):
                pe.wait_ge(sem(f"tok_made{g}"), c * 3 + n + 1)
                for h in range(HG):
                    last = nc.tensor.transpose(bank(g, n)[:, h, :], slots[g][slot][:, h, :], ident[:, :])
                last.then_inc(sem(f"feat_mm{g}"), 1)

        def pe_kk(pe, g, c):
            m = slots[g]
            pe.wait_ge(sem(f"feat_out{g}"), c * 3 + 3)
            for n, (left, right) in enumerate((("I", "I"), ("I", "G"))):
                for h in range(HG):
                    last = nc.tensor.matmul(bank(g, n)[:, h, :], m[left][:, h, :], m[right][:, h, :],
                                            start=True, stop=True)
                last.then_inc(sem(f"kk_mm{g}"), 1)

        def pe_turn_l(pe, g, c):
            pe.wait_ge(sem(f"l_made{g}"), c + 1)
            for h in range(HG):
                last = nc.tensor.transpose(bank(g, 2)[:, h, :], slots[g]["K"][:, h, :], ident[:, :])
            last.then_inc(sem(f"lt_mm{g}"), 1)

        def pe_level_y(pe, g, c, lv):
            m = slots[g]
            pe.wait_ge(sem(f"level{g}"), c * (LEVELS - 1) + lv)
            pe.wait_ge(sem(f"x_made{g}"), c * (LEVELS - 1) + lv)
            for h in range(HG):
                last = nc.tensor.matmul(bank(g, 3)[:, h, :], m["JO"[lv % 2]][:, h, :], m["A"][:, h, :],
                                        start=True, stop=True)
            last.then_inc(sem(f"y_mm{g}"), 1)

        def pe_level_x(pe, g, c, lv):
            m = slots[g]
            pe.wait_ge(sem(f"y_out{g}"), c * (LEVELS - 1) + lv)
            pe.wait_ge(sem(f"inv_made{g}"), c * LEVELS + lv)
            n, left, right = (0, "B", "D") if lv < LEVELS - 1 else (1, "D", "B")
            for h in range(HG):
                last = nc.tensor.matmul(bank(g, n)[:, h, :], m[left][:, h, :], m[right][:, h, :],
                                        start=True, stop=True)
            last.then_inc(sem(f"x_mm{g}"), 1)

        def pe_level_turn(pe, g, c, lv):
            pe.wait_ge(sem(f"x_made{g}"), c * (LEVELS - 1) + lv + 1)
            if lv == 1:
                pe.wait_ge(sem(f"attn_made{g}"), c + 1)
            for h in range(HG):
                last = nc.tensor.transpose(bank(g, 1)[:, h, :], slots[g]["A"][:, h, :], ident[:, :])
            last.then_inc(sem(f"xt_mm{g}"), 1)

        def pe_w(pe, g, c):
            m = slots[g]
            pe.wait_ge(sem(f"inv_made{g}"), c * LEVELS + LEVELS)
            for h in range(HG):
                last = nc.tensor.matmul(bank(g, 2)[:, h, :], m["E"][:, h, :], m["B"][:, h, :],
                                        start=True, stop=True)
            last.then_inc(sem(f"w_mm{g}"), 1)

        def pe_values(pe, g, c):
            m = slots[g]
            pe.wait_ge(sem(f"w_out{g}"), c + 1)
            for h in range(HG):
                nc.tensor.matmul(bank(g, 3)[:, h, :], m["B"][:, h, :], m["C"][:, h, :],
                                 start=True, stop=False)
                last = nc.tensor.matmul(bank(g, 3)[:, h, :], m["G"][:, h, :], state[:, g * HG + h, :],
                                        start=False, stop=True)
            last.then_inc(sem(f"vnew_mm{g}"), 1)

        def pe_out(pe, g, c):
            m = slots[g]
            pe.wait_ge(sem(f"vnew_out{g}"), c + 1)
            for h in range(HG):
                nc.tensor.matmul(bank(g, 0)[:, h, :], state[:, g * HG + h, :], m["H"][:, h, :],
                                 start=True, stop=False)
                last = nc.tensor.matmul(bank(g, 0)[:, h, :], m["I"][:, h, :], m["M"][:, h, :],
                                        start=False, stop=True)
            last.then_inc(sem(f"o_mm{g}"), 1)
            if isinstance(c, int) and c == NB - 1:
                return
            for h in range(HG):
                last = nc.tensor.matmul(bank(g, 1)[:, h, :], m["F"][:, h, :], m["I"][:, h, :],
                                        start=True, stop=True)
            last.then_inc(sem(f"kv_mm{g}"), 1)

        def core_pe(pe, g, c, ce, cs):
            o = 1 - g
            for lv in range(1, LEVELS):
                pe_level_y(pe, g, c, lv)
                if lv == 1 and ce is not None:
                    pe_w(pe, o, ce)
                if lv == 2 and ce is not None:
                    pe_out(pe, o, ce)
                if cs is not None and lv == 3:
                    pe_sum_rows(pe, o, cs)
                if cs is not None and lv == 5:
                    pe_kk(pe, o, cs)
                if cs is not None and lv == 6:
                    pe_turn_l(pe, o, cs)
                pe_level_x(pe, g, c, lv)
                if lv == 1 and ce is not None:
                    pe_values(pe, o, ce)
                if cs is not None and lv == 4:
                    pe_features(pe, o, cs)
                if lv < LEVELS - 1:
                    pe_level_turn(pe, g, c, lv)
                if cs is not None and lv == 2:
                    pe_tokens(pe, o, cs)
                if cs is None and lv == 4:
                    norm_sums_pe(pe, o)

        def core_start_pe(pe, g, c):
            pe_sum_rows(pe, g, c)
            pe_tokens(pe, g, c)
            pe_features(pe, g, c)
            pe_kk(pe, g, c)
            pe_turn_l(pe, g, c)

        def core_end_pe(pe, g, c):
            pe_w(pe, g, c)
            norm_root_pe(pe, 0)
            pe_values(pe, g, c)
            norm_root_pe(pe, 1)
            pe_out(pe, g, c)

        def out_of(g, n, slot, signal, scale=1.0):
            nc.scalar.activation(slots[g][slot][:, :, :], bank(g, n), ACT.Copy, scale=scale)\
                .then_inc(sem(f"{signal}{g}"), 1)

        def act_stage(act, g, c):
            for n, (slot, used) in enumerate((("A", "w_mm"), ("B", "vnew_mm"))):
                if not first(c):
                    act.wait_ge(sem(f"{used}{g}"), c)
                f = n * H + g * HG
                nc.scalar.activation(slots[g][slot][:, :, :], qkv[:, f:f + HG, bass.ds(c * P, P)], ACT.Copy)\
                    .then_inc(sem(f"staged{g}"), 1)

        def act_decay(act, g, c):
            for slot, k, scale in (("K", 1, -1.0), ("M", 2, 1.0)):
                act.wait_ge(sem(f"decay_arg{g}"), c * 2 + k)
                nc.scalar.activation(slots[g][slot][:, :, :], slots[g][slot][:, :, :], ACT.Exp, scale=scale)\
                    .then_inc(sem(f"decay{g}"), 1)

        def act_features(act, g, c):
            for n, slot in enumerate("GHI"):
                act.wait_ge(sem(f"feat_mm{g}"), c * 3 + n + 1)
                out_of(g, n, slot, "feat_out")

        def act_turn_l(act, g, c):
            act.wait_ge(sem(f"lt_mm{g}"), c + 1)
            out_of(g, 2, "N", "lt_out")

        def act_level(act, g, c, lv):
            act.wait_ge(sem(f"y_mm{g}"), c * (LEVELS - 1) + lv)
            out_of(g, 3, "D", "y_out")

        def act_level_turn(act, g, c, lv):
            act.wait_ge(sem(f"xt_mm{g}"), c * (LEVELS - 2) + lv)
            out_of(g, 1, "B", "inv_made")

        def act_w(act, g, c):
            act.wait_ge(sem(f"w_mm{g}"), c + 1)
            out_of(g, 2, "G", "w_out", -1.0)

        def act_values(act, g, c):
            act.wait_ge(sem(f"vnew_mm{g}"), c + 1)
            out_of(g, 3, "I", "vnew_out")

        def act_out(act, g, c):
            act.wait_ge(sem(f"o_mm{g}"), c + 1)
            nc.scalar.activation(qkv[:, g * HG:(g + 1) * HG, bass.ds(c * P, P)], bank(g, 0), ACT.Copy)\
                .then_inc(sem(f"o_out{g}"), 1)

        def core_act(act, g, c, ce, cs):
            o = 1 - g
            for lv in range(1, LEVELS):
                act_level(act, g, c, lv)
                if lv == 1 and ce is not None:
                    act_w(act, o, ce)
                if lv == 2 and ce is not None:
                    act_out(act, o, ce)
                if cs is not None and lv == 5:
                    act_decay(act, o, cs)
                if lv == 1 and ce is not None:
                    act_values(act, o, ce)
                if cs is not None and lv == 4:
                    act_features(act, o, cs)
                if lv < LEVELS - 1:
                    act_level_turn(act, g, c, lv)
                if lv == 1 and cs is not None:
                    act_stage(act, o, cs)
                if lv == 3 and cs is None:
                    norm_squares_act(act, o)
            if cs is not None:
                act_turn_l(act, o, cs)

        def core_start_act(act, g, c):
            act_stage(act, g, c)
            act_decay(act, g, c)
            act_features(act, g, c)
            act_turn_l(act, g, c)

        def core_end_act(act, g, c):
            act_w(act, g, c)
            act_values(act, g, c)
            norm_hi_act(act, 0)
            act_out(act, g, c)
            norm_hi_act(act, 1)

        def dve_decay(dve, ch, g, c):
            m = slots[g]
            dve.wait_ge(sem(f"grow_mm{g}"), c + 1)
            ch(tt(m["J"][:, :, :], bank(g, 3), along(heads(gsum[:, 0, :, :], g, c)), ALU.subtract))
            tt(m["K"][:, :, :], m["J"][:, :, :], over_heads(mask_l[:, :]), ALU.add).then_inc(sem(f"decay_arg{g}"), 1)
            tt(m["M"][:, :, :], m["J"][:, :, :], over_heads(mask_t[:, :]), ALU.subtract)\
                .then_inc(sem(f"decay_arg{g}"), 1)

        def dve_tokens(dve, ch, g, c):
            dve_q_k(dve, ch, g, c)
            dve_k_v(dve, ch, g, c)

        def dve_q_k(dve, ch, g, c):
            m = slots[g]
            dve.wait_ge(sem(f"qkv_tok{g}"), c * 3 + 3)
            ch.inc(tt(m["A"][:, :, :], bank(g, 0), along(heads(q_f, g, c)), ALU.mult))
            tt(m["D"][:, :, :], bank(g, 0), along(heads(qg_f, g, c)), ALU.mult)\
                .then_inc(sem(f"tok_made{g}"), 1)
            ch.inc(tt(m["B"][:, :, :], bank(g, 1), along(heads(l2r[:, :, H:2 * H], g, c)), ALU.mult))

        def dve_k_v(dve, ch, g, c):
            m = slots[g]
            ch.inc(tt(m["E"][:, :, :], bank(g, 1), along(heads(kb_f, g, c)), ALU.mult))
            tt(m["F"][:, :, :], bank(g, 1), along(heads(kl_f, g, c)), ALU.mult)\
                .then_inc(sem(f"tok_made{g}"), 1)
            tt(m["C"][:, :, :], bank(g, 2), along(heads(beta, g, c)), ALU.mult)\
                .then_inc(sem(f"tok_made{g}"), 1)

        def dve_l(dve, ch, g, c):
            m = slots[g]
            dve.wait_ge(sem(f"decay_beta{g}"), c + 1)
            dve.wait_ge(sem(f"kk_mm{g}"), c * 2 + 1)
            tt(m["K"][:, :, :], bank(g, 0), m["K"][:, :, :], ALU.mult).then_inc(sem(f"l_made{g}"), 1)
            dve.wait_ge(sem(f"decay{g}"), c * 2 + 2)
            dve.wait_ge(sem(f"kk_mm{g}"), c * 2 + 2)
            tt(m["M"][:, :, :], bank(g, 1), m["M"][:, :, :], ALU.mult).then_inc(sem(f"attn_made{g}"), 1)

        def dve_first(dve, ch, g, c):
            m = slots[g]
            dve.wait_ge(sem(f"feat_mm{g}"), c * 3 + 3)
            dve.wait_ge(sem(f"l_made{g}"), c + 1)
            ch(tt(m["A"][:, :, :], m["K"][:, :, :], over_heads(first_l[:, :]), ALU.mult))
            tt(m["A"][:, :, :], m["A"][:, :, :], over_heads(ident[:, :]), ALU.add).then_inc(sem(f"x_made{g}"), 1)

        def dve_first_turned(dve, ch, g, c):
            m = slots[g]
            dve.wait_ge(sem(f"lt_out{g}"), c + 1)
            ch(tt(m["B"][:, :, :], m["N"][:, :, :], over_heads(first_t[:, :]), ALU.mult))
            tt(m["B"][:, :, :], m["B"][:, :, :], over_heads(ident[:, :]), ALU.add).then_inc(sem(f"inv_made{g}"), 1)

        def dve_level(dve, g, c, lv):
            m = slots[g]
            dve.wait_ge(sem(f"x_mm{g}"), c * (LEVELS - 1) + lv)
            if lv < LEVELS - 1:
                dve.wait_ge(sem(f"x_made{g}"), c * (LEVELS - 1) + lv)
                tt(m["A"][:, :, :], m["A"][:, :, :], bank(g, 0), ALU.subtract).then_inc(sem(f"x_made{g}"), 1)
            else:
                tt(m["B"][:, :, :], m["B"][:, :, :], bank(g, 1), ALU.subtract).then_inc(sem(f"inv_made{g}"), 1)

        def dve_state(dve, g, c):
            dve.wait_ge(sem(f"kv_mm{g}"), c + 1)
            for h in range(HG):
                at = g * HG + h
                last_g = gexp[:, 1, c, at:at + 1] if isinstance(c, int) else \
                    gexp[:, 1, bass.ds(c, 1), at:at + 1].rearrange("p a b -> p (a b)")
                nc.vector.scalar_tensor_tensor(state[:, at, :], state[:, at, :], last_g, bank(g, 1)[:, h, :],
                                               ALU.mult, ALU.add).then_inc(sem(f"state_made{g}"), 1)

        def core_dve(dve, ch, g, c, ce, cs):
            o = 1 - g
            for lv in range(1, LEVELS):
                dve_level(dve, g, c, lv)
                if lv == 2 and ce is not None and cs is not None:
                    dve_state(dve, o, ce)
                if lv == 5 and cs is None:
                    norm_var_dve(dve, o)
                if cs is not None and lv == 2:
                    dve_q_k(dve, ch, o, cs)
                if cs is not None and lv == 3:
                    dve_k_v(dve, ch, o, cs)
                    dve_decay(dve, ch, o, cs)
                if cs is not None and lv == 5:
                    dve_l(dve, ch, o, cs)
                    dve_first(dve, ch, o, cs)
            if cs is not None:
                dve_first_turned(dve, ch, o, cs)

        def core_start_dve(dve, ch, g, c):
            dve_decay(dve, ch, g, c)
            dve_tokens(dve, ch, g, c)
            dve_l(dve, ch, g, c)
            dve_first(dve, ch, g, c)
            dve_first_turned(dve, ch, g, c)

        def core_loop(turn, start, end, eng, chain=None):
            n = chain.n if chain else 0
            start(0, 0)
            per = 2 * (chain.n - n) if chain else 0
            turn(0, 0, None, 0)
            n = chain.n if chain else 0
            with eng.Fori(1, NB) as c:
                if chain:
                    chain.turns = c * per - per
                turn(1, c - 1, c - 1, c)
                turn(0, c, c - 1, c)
            if chain:
                assert chain.n == n + per, (chain.n, n, per)
                chain.turns, chain.n = None, n + (NB - 1) * per
            turn(1, NB - 1, NB - 1, None)
            if end:
                end(1, NB - 1)

        def norm_squares_act(act, g):
            act.wait_ge(sem(f"o_out{g}"), NB)
            for h in range(g * HG, (g + 1) * HG):
                nc.scalar.activation(sq_gdn[:, h, :], qkv[:, h, :], ACT.Square).then_inc(sem("o_sq"), 1)

        def norm_sums_pe(pe, g):
            if g:
                pe.wait_ge(sem("o_var"), g)
            for h in range(g * HG, (g + 1) * HG):
                pe.wait_ge(sem("o_sq"), h + 1)
                for b in range(NB):
                    last = nc.tensor.matmul(ps[:, 3, h * NB + b:h * NB + b + P], sq_gdn[:, h, b * P:(b + 1) * P],
                                            ones[:, :], start=True, stop=True)
            last.then_inc(sem("o_stat"), 1)

        def norm_var_dve(dve, g):
            dve.wait_ge(sem("o_stat"), g + 1)
            at = slice(g * HG * NB, (g + 1) * HG * NB)
            nc.vector.tensor_scalar(var[:, at], ps[:, 3, at], 1.0 / P, EPS, ALU.mult, ALU.add)\
                .then_inc(sem("o_var"), 1)

        def norm_root_pool(pool, g):
            pool.wait_ge(sem("o_var"), g + 1)
            at = slice(g * HG * NB, (g + 1) * HG * NB)
            nc.gpsimd.tensor_tensor(rinv[:, at], var[:, at], half[:, at], ALU.pow).then_inc(sem("o_rinv"), 1)

        def root_bank(h):
            return ps[:, (1 if h < 2 else 5) + h % 2, :]

        def norm_root_pe(pe, h):
            pe.wait_ge(sem("o_diag"), h + 1)
            if h >= 2:
                pe.wait_ge(sem("o_scaled"), h - 1)
            nc.tensor.matmul(root_bank(h), ones[:, :],
                             flat(diag[:, :, :]) if h % 2 == 0 else tmp[:, 2, :],
                             start=True, stop=True).then_inc(sem("o_root"), 1)

        def norm_hi_act(act, h):
            act.wait_ge(sem("o_gated"), h + 1)
            nc.scalar.activation(h_hi[:, h, :], tmp[:, h % 2, :], ACT.Copy).then_inc(sem("h_rounded"), 1)

        def gdn_norm_pe(pe):
            norm_root_pe(pe, 2)
            norm_sums_pe(pe, 1)
            for h in range(3, H):
                norm_root_pe(pe, h)

        def gdn_norm_act(act):
            norm_squares_act(act, 1)
            for h in range(2, H):
                norm_hi_act(act, h)

        def gdn_norm_dve(dve):
            def make_diag(h):
                dve.wait_ge(sem("o_rinv"), h // HG + 1)
                if h >= 2:
                    dve.wait_ge(sem("o_root"), h - 1)
                dst = diag[:, :, :] if h % 2 == 0 else tmp[:, 2, :].rearrange("p (a b) -> p a b", a=NB)
                nc.vector.tensor_tensor(dst, over_heads(ident[:, :]), along(rinv[:, h * NB:(h + 1) * NB]),
                                        ALU.mult).then_inc(sem("o_diag"), 1)

            def low(h):
                dve.wait_ge(sem("h_rounded"), 8 + h + 1)
                nc.vector.tensor_tensor(h_lo[:, h, :], tmp[:, h % 2, :], f32(h_hi[:, h, :]), ALU.subtract)\
                    .then_inc(sem("h_made"), 1)
                h_here(dve, 1, h)

            make_diag(0)
            for h in range(H):
                if h == HG - 1:
                    norm_var_dve(dve, 1)
                if h + 1 < H:
                    make_diag(h + 1)
                dve.wait_ge(sem("o_root"), h + 1)
                nc.vector.scalar_tensor_tensor(tmp[:, h % 2, :], root_bank(h), gnorm,
                                               qkv[:, h, :], ALU.mult, ALU.mult).then_inc(sem("o_scaled"), 1)
                dve.wait_ge(sem("o_scaled"), h + 1)
                nc.vector.tensor_tensor(tmp[:, h % 2, :], tmp[:, h % 2, :], z_t[:, h, :], ALU.mult)\
                    .then_inc(sem("o_gated"), 1)
                if h:
                    low(h - 1)
            low(H - 1)

        y_out = sem("y_out")

        def dve_y(dve, q, s, y, d, yt, add):
            dve.wait_ge(tile_done, q * 4 + s + 1)
            if add:
                dve.wait_ge(y_out, yt)
                nc.vector.tensor_tensor(y[:, d, :], y[:, d, :], ps[:, s, :], ALU.add).then_inc(y_out, 1)
            else:
                nc.vector.tensor_copy(y[:, d, :], ps[:, s, :]).then_inc(y_out, 1)

        def plain_out(eng, kind, q0, y, y0, nxt, sq=None):
            for j in range(2):
                for s in range(4):
                    if kind == "dve":
                        dve_y(eng, q0 + j, s, y, 4 * j + s, y0 + 4 * j + s, False)
                        if j == 0:
                            dve_split(eng, q0 + 1, s)
                    elif j == 0:
                        act_split(eng, q0 + 1, s)
                    if j == 1 and nxt:
                        nxt(s)
                    if kind == "act":
                        eng.wait_ge(y_out, y0 + 4 * j + s + 1)
                        act_square(eng, y, sq, 4 * j + s)

        F0 = [sum(PARTS[:p]) for p in range(3)]
        Y_FFN = [8, 40]

        def part_quads(layer, p):
            q = Q_FFN[layer] + F0[p] // 2 + 2 * p
            return q, PARTS[p] // 2, layer * (FC // 2) + F0[p] // 2

        def ffn_sp(sp, layer):
            w_in, w_out = rows(ffn_w_in[layer]), ffn_w_out[layer]
            for p in range(3):
                q, n, _ = part_quads(layer, p)

                def body(i):
                    at = i * 256 + F0[p] * P
                    load_quad(sp, i + q, w_in[:, :, bass.ds(at, 256)], w_in[:, :, bass.ds(at + FC * P, 256)])

                repeat(sp, n, body)
                kc = PARTS[p]
                part = rows(w_out[F0[p] * P:(F0[p] + kc) * P, :])
                for j in range(2):
                    load_quad(sp, q + n + j, part[:, :, j * 512:j * 512 + 256],
                              part[:, :, j * 512 + 256:j * 512 + 512], kc)

        def ffn_act(act, layer, nxt):
            for p in range(3):
                q, n, c0 = part_quads(layer, p)
                kc = PARTS[p]

                def epilogue(i, s):
                    act.wait_ge(tile_done, i * 4 + 4 * q + s + 1)
                    ci = i + c0
                    if s < 2:
                        if not (isinstance(ci, int) and ci == 0):
                            act.wait_ge(sem("ffn_mul"), ci * 2 + s - 1)
                        nc.scalar.activation(silu_g[:, s, :], ps[:, s, :], ACT.Silu).then_inc(sem("ffn_silu"), 1)
                    else:
                        act.wait_ge(sem("ffn_mul"), ci * 2 + s - 1)
                        out = g_hi[:, i * 2 + s - 2, :] if isinstance(i, int) else \
                            flat(g_hi[:, bass.ds(i * 2 + s - 2, 1), :])
                        nc.scalar.activation(out, gated[:, s - 2, :], ACT.Copy).then_inc(sem("ffn_hi"), 1)

                def body(i):
                    for s in range(4):
                        epilogue(i, s)
                        act_split(act, i + q + 1, s)

                repeat(act, n - 1, body)
                for s in range(4):
                    epilogue(n - 1, s)
                    act_split(act, q + n, s, kc)
                for t in range(DC):
                    s = t % 4
                    if t < 4:
                        act_split(act, q + n + 1, s, kc)
                    elif p < 2:
                        act_split(act, q + n + 2, s)
                    elif nxt:
                        nxt(s)
                    if p == 2:
                        act.wait_ge(y_out, Y_FFN[layer] + 16 + t + 1)
                        act_square(act, y_ffn, sq_ffn, t)

        def ffn_dve(dve, ch, layer, nxt):
            for p in range(3):
                q, n, c0 = part_quads(layer, p)
                kc = PARTS[p]

                def epilogue(i, s, split):
                    ci = i + c0
                    if s < 2:
                        split(s)
                        return
                    dve.wait_ge(tile_done, i * 4 + 4 * q + s + 1)
                    dve.wait_ge(sem("ffn_silu"), ci * 2 + s - 1)
                    nc.vector.tensor_tensor(gated[:, s - 2, :], silu_g[:, s - 2, :], ps[:, s, :], ALU.mult)\
                        .then_inc(sem("ffn_mul"), 1)
                    split(s)
                    dve.wait_ge(sem("ffn_hi"), ci * 2 + s - 1)
                    one = bass.ds(i * 2 + s - 2, 1)
                    nc.vector.tensor_tensor(flat(g_lo[:, one, :]), gated[:, s - 2, :], f32(flat(g_hi[:, one, :])),
                                            ALU.subtract).then_inc(sem("ffn_lo"), 1)

                def ada(i, s):
                    if layer == 0:
                        dve_ada_beside(dve, ch, i + 12 + F0[p] // 2, s)

                def body(i):
                    for s in range(4):
                        ada(i, s)
                        epilogue(i, s, lambda s: dve_split(dve, i + q + 1, s))

                repeat(dve, n - 1, body, ch)
                for s in range(4):
                    ada(n - 1, s)
                    epilogue(n - 1, s, lambda s: dve_split(dve, q + n, s, kc))
                y0 = Y_FFN[layer] + 8 * p
                for j in range(2):
                    for s in range(4):
                        dve_y(dve, q + n + j, s, y_ffn, 4 * j + s, y0 + 4 * j + s, p > 0)
                        if j == 0:
                            dve_split(dve, q + n + 1, s, kc)
                        elif p < 2:
                            dve_split(dve, q + n + 2, s)
                        elif nxt:
                            nxt(s)
                    if layer == 0 and p == 2 and j == 0:
                        dve_ada_out(dve, ch, 22)
                        for part in range(4):
                            dve_ada(dve, ch, 23, part)
            if layer == 0:
                dve_ada_out(dve, ch, 23)

        def ffn_pe(pe, layer, m):
            for p in range(3):
                q, n, c0 = part_quads(layer, p)
                y0 = Y_FFN[layer] + 8 * p

                def body(i):
                    if p == 0 and isinstance(i, int) and i == 0:
                        pe_first_quad(pe, q, h_hi, h_lo, lambda k: h_here(pe, m, k),
                                      lambda s: pe.wait_ge(y_out, y0 - 4 + s + 1))
                        return
                    for s in range(4):
                        def free():
                            if isinstance(i, int) and i == 0:
                                pe.wait_ge(y_out, y0 - 4 + s + 1)
                            else:
                                pe.wait_ge(sem("ffn_silu" if s < 2 else "ffn_mul"), (i + c0) * 2 - 1 + s % 2)

                        pe_tile(pe, i + q, s, h_hi, h_lo, before=free)
                        if layer == 0 and s == 0 and not (isinstance(i, int) and i + F0[p] == 0):
                            pe_ada(pe, i + 11 + F0[p] // 2)

                repeat(pe, n, body)
                last_ci = c0 + n - 1
                for j in range(2):
                    for s in range(4):
                        def free():
                            if j == 0:
                                pe.wait_ge(sem("ffn_silu" if s < 2 else "ffn_mul"), 2 * last_ci + s % 2 + 1)
                            else:
                                pe.wait_ge(y_out, y0 + s + 1)

                        def ready(k):
                            if j == 0 and s == 0:
                                pe.wait_ge(sem("ffn_lo"), 2 * c0 + k + 1)

                        pe_tile(pe, q + n + j, s, g_hi, g_lo, PARTS[p], before=free, ready=ready)
                        if p == 2:
                            pe_stat_behind(pe, (3, 9)[layer], sq_ffn, 4 * j + s)
                    if layer == 0 and p == 2:
                        pe_ada(pe, 22 + j)

        def raw_half(s):
            return flat(raw[s // 2][:, :, :])[:, (s % 2) * 1024:(s % 2 + 1) * 1024]

        def dsa_views(quad, s):
            if quad == 1 and s == 0:
                n = DC * SMALL
                return raw_half(0)[:, 0:n], lambda w: w[:, 0, 0:n]
            return raw_half(s), lambda w: w[:, s, :]

        def dsa_sp(sp):
            w_in = rows(dsa_w_in[0])
            load_quad(sp, Q_DSA, w_in[:, :, 0:LAT], w_in[:, :, LAT:2 * LAT])
            small = raw_half(0)[:, 0:DC * SMALL].rearrange("p (k n) -> p k n", k=DC)
            qi = raw_half(1).rearrange("p (k n) -> p k n", k=LC)
            uq = flat(raw[1][:, :, :]).rearrange("p (k n) -> p k n", k=LC)
            load_quad(sp, Q_DSA + 1,
                      [(small, w_in[:, :, 2 * LAT:], raw_in[0]), (qi, rows(dsa_w_qidx[0]), x_in)],
                      [(uq, rows(dsa_w_uq[0]), raw_in[1])])
            uk = flat(raw[0][:, :, :]).rearrange("p (h n) -> p h n", n=LAT)
            uv = flat(raw[1][:, :, :]).rearrange("p (k h v) -> p k h v", k=LC, v=DH)
            uv_src = dsa_w_uv[0].rearrange("h (k p) v -> p k h v", p=P)
            load_quad(sp, Q_DSA + 2, [(uk, dsa_w_uk[0].rearrange("(g a) d n -> (a d) g n", a=2), raw_in[0])],
                      [(uv[:, 0, :, :], uv_src[:, 0, :, :], raw_in[1]),
                       (uv[:, 1, :, :], uv_src[:, 1, :, :], x_in)])
            w_out = rows(dsa_w_out[0])
            for j in range(2):
                load_quad(sp, Q_DSA_OUT + j, w_out[:, :, j * 512:j * 512 + 256],
                          w_out[:, :, j * 512 + 256:j * 512 + 512])

        def dsa_split_act(act, quad, s):
            src, dst = dsa_views(quad, s)
            if (quad, s) == (1, 1):
                act.wait_ge(x_in, 32)
            if (quad, s) == (2, 3):
                act.wait_ge(x_in, 48)
            act_split(act, Q_DSA + quad, s, src=src, dst=dst)

        def dsa_split_dve(dve, quad, s):
            src, dst = dsa_views(quad, s)
            dve_split(dve, Q_DSA + quad, s, src=src, dst=dst)

        def dsa_split_pool(pool, quad, s):
            src, dst = dsa_views(quad, s)
            split(pool, nc.gpsimd, Q_DSA + quad, s, src=src, dst=dst)

        def mm3(out, l_hi, l_lo, r_hi, r_lo, first, last):
            nc.tensor.matmul(out, l_hi, r_hi, start=first, stop=False)
            nc.tensor.matmul(out, l_hi, r_lo, start=False, stop=False)
            return nc.tensor.matmul(out, l_lo, r_hi, start=False, stop=last)

        AT_QI, AT_Q, AT_UK, AT_K, AT_V = 0, 4, 12, 20, 28
        LAST = {3: 4 * Q_DSA + 6, 11: 4 * Q_DSA + 8, 18: 4 * Q_DSA + 9, 19: 4 * Q_DSA + 10, 35: 4 * Q_DSA + 12}

        def proj_ready(act, t):
            if t in LAST:
                act.wait_ge(tile_done, LAST[t])
            else:
                act.wait_ge(sem("proj_mm"), t + 1 - sum(x < t for x in LAST))

        def dsa_in_pe(pe, m):
            pe_first_quad(pe, Q_DSA, h_hi, h_lo, lambda k: h_here(pe, m, k),
                          lambda s: pe.wait_ge(y_out, Y_FFN[0] + 20 + s + 1),
                          lambda s: pe_stats(pe, 5, sq_lat[:, 0, :, :], LC) if s == 2 else None)
            pe.wait_ge(lo_done, 4 * Q_DSA + 5)
            w = [t[:, 0, 0:DC * SMALL].rearrange("p (k n) -> p k n", n=SMALL) for t in (w_hi, w_lo)]
            for k in range(DC):
                last = mm3(ps[0:SMALL, 6, :], w[0][:, k, :], w[1][:, k, :], h_hi[:, k, :], h_lo[:, k, :],
                           k == 0, k == DC - 1)
            last.then_inc(tile_done, 1)
            pe_bcast(pe, 5)
            pe.wait_ge(sem("small_out"), 2)
            for b in range(NB):
                last = nc.tensor.transpose(ps[:, 7, b * SMALL:(b + 1) * SMALL], kx_t[0:SMALL, b * P:(b + 1) * P],
                                           ident[0:SMALL, 0:SMALL])
            last.then_inc(sem("small_turned"), 1)
            pe.wait_ge(sem("lat_made"), LC)
            pe.wait_ge(lo_done, 4 * Q_DSA + 6)
            wq = [t[:, 1, :].rearrange("p (k n) -> p k n", k=LC) for t in (w_hi, w_lo)]
            for j in range(4):
                pe.wait_ge(sem("sq_made"), SQ_BASE[5] + j + 1)
                for k in range(LC):
                    last = mm3(ps[:, j, :], wq[0][:, k, j * P:(j + 1) * P], wq[1][:, k, j * P:(j + 1) * P],
                               cq_hi[:, k, :], cq_lo[:, k, :], k == 0, k == LC - 1)
                last.then_inc(tile_done if j == 3 else sem("proj_mm"), 1)
            pe_stats(pe, 6, sq_lat[:, 1, :, :], LC)
            pe.wait_ge(sem("kn_made"), 1)
            for b in range(NB):
                last = nc.tensor.transpose(ps[:, 7, b * P:(b + 1) * P], kn[:, b, :], ident[:, :])
            last.then_inc(sem("knt_mm"), 1)
            pe_bcast(pe, 6)

        def indexer_pe(pe, b):
            n = (b + 1) * P
            if b == 1:
                pe.wait_ge(sem("lat_made"), 2 * LC)
                pe.wait_ge(sem("knt_out"), 1)
                pe.wait_ge(sem("proj_out"), AT_QI + 4)
            for j in range(IH):
                t = (b - 1) * IH + j
                if t >= 4:
                    pe.wait_ge(sem("relu_made"), t - 3)
                lanes = slice(64 * (j % 2), 64 * (j % 2) + 64)
                nc.tensor.matmul(ps[:, 4 + t % 4, 0:n], qi_t[lanes, j // 2, b * P:(b + 1) * P],
                                 kn_t[lanes, 0:n], start=True, stop=True).then_inc(sem("logit_mm"), 1)

        def dsa_q_pe(pe):
            for j in range(8):
                if j < 4:
                    pe.wait_ge(sem("proj_out"), AT_QI + j + 1)
                if j >= 4:
                    pe.wait_ge(sem("proj_out"), AT_Q + j - 3)
                if j == 0:
                    pe.wait_ge(lo_done, 4 * Q_DSA + 8)
                cols = slice(j * P, (j + 1) * P)
                for k in range(LC):
                    last = mm3(ps[:, j % 4, :], w_hi[:, 2 + k, cols], w_lo[:, 2 + k, cols],
                               cq_hi[:, k, :], cq_lo[:, k, :], k == 0, k == LC - 1)
                    if j == 7:
                        last.then_inc(tile_done, 1)
                if j < 7:
                    last.then_inc(sem("proj_mm"), 1)

        def dsa_uk_pe(pe):
            pe.wait_ge(lo_done, 4 * Q_DSA + 10)
            t = 0
            for w in (w_hi, w_lo):
                for k in range(LC):
                    for s in (0, 1):
                        if t < 4:
                            pe.wait_ge(sem("proj_out"), AT_Q + t + 5)
                        else:
                            pe.wait_ge(sem("proj_out"), AT_UK + t - 3)
                        for r in range(4):
                            last = nc.tensor.transpose(ps[:, t % 4, r * P:(r + 1) * P],
                                                       f32(w[:, s, r * LAT + k * P:r * LAT + (k + 1) * P]),
                                                       ident[:, :])
                        last.then_inc(sem("proj_mm") if t < 6 else tile_done, 1)
                        t += 1

        def dsa_keys_pe(pe):
            for j in range(8):
                pe.wait_ge(sem("proj_out"), AT_UK + 8)
                if j >= 4:
                    pe.wait_ge(sem("proj_out"), AT_K + j - 3)
                for k in range(LC):
                    cols = slice(j * P, (j + 1) * P)
                    last = mm3(ps[:, j % 4, :], uk_hi[:, k, cols], uk_lo[:, k, cols],
                               ckv_hi[:, k, :], ckv_lo[:, k, :], k == 0, k == LC - 1)
                last.then_inc(sem("proj_mm"), 1)

        def dsa_v_pe(pe):
            for j in range(8):
                b, cols = j // 2, slice(j % 2 * 512, j % 2 * 512 + 512)
                blk = slice(b * P, (b + 1) * P)
                if j < 4:
                    pe.wait_ge(sem("proj_out"), AT_K + j + 5)
                else:
                    pe.wait_ge(sem("proj_out"), AT_V + j - 3)
                if j == 0:
                    pe.wait_ge(lo_done, 4 * Q_DSA + 12)
                for k in range(LC):
                    last = mm3(ps[:, j % 4, :], ckv_hi[:, k, blk], ckv_lo[:, k, blk],
                               w_hi[:, 2 + k, cols], w_lo[:, 2 + k, cols], k == 0, k == LC - 1)
                    if j == 7:
                        last.then_inc(tile_done, 1)
                if j < 7:
                    last.then_inc(sem("proj_mm"), 1)

        def dsa_in_act(act):
            for s in range(4):
                act.wait_ge(tile_done, 4 * Q_DSA + s + 1)
                nc.scalar.activation(latent[:, s // 2, s % 2, :], ps[:, s, :], ACT.Copy).then_inc(sem("lat_here"), 1)
                nc.scalar.activation(sq_lat[:, s // 2, s % 2, :], ps[:, s, :], ACT.Square).then_inc(sem("sq_made"), 1)
                dsa_split_act(act, 1, s)
            act.wait_ge(tile_done, 4 * Q_DSA + 5)
            nc.scalar.activation(kx_t[0:SMALL, :], ps[0:SMALL, 6, :], ACT.Copy).then_inc(sem("small_out"), 1)
            latent_hi_act(act, 0)
            for j in range(4):
                proj_ready(act, AT_QI + j)
                nc.scalar.activation(qi_t[:, j, :], ps[:, j, :], ACT.Copy).then_inc(sem("proj_out"), 1)
            act.wait_ge(sem("knt_mm"), 1)
            nc.scalar.activation(kn_t[:, :], ps[:, 7, :], ACT.Copy).then_inc(sem("knt_out"), 1)
            latent_hi_act(act, 1)

        def latent_hi_act(act, half_):
            for k in range(LC):
                act.wait_ge(sem("lat_scaled"), half_ * LC + k + 1)
                dst = (cq_hi, ckv_hi)[half_]
                nc.scalar.activation(dst[:, k, :], tmp[:, k, :], ACT.Copy).then_inc(sem("lat_hi"), 1)

        def relu_act(act, b):
            n = (b + 1) * P
            if b > 1:
                act.wait_ge(sem("relu_used"), (b - 1) * IH)
            for j in range(IH):
                t = (b - 1) * IH + j
                act.wait_ge(sem("logit_mm"), t + 1)
                nc.scalar.activation(relu[:, j, 0:n], ps[:, 4 + t % 4, 0:n], ACT.Relu).then_inc(sem("relu_made"), 1)

        def dsa_qkv_act(act, nxt):
            relu_act(act, 1)
            for s in (0, 1):
                dsa_split_act(act, 2, s)
            relu_act(act, 2)
            for j in range(8):
                proj_ready(act, AT_Q + j)
                nc.scalar.activation(q_t[:, j, :], ps[:, j % 4, :], ACT.Copy, scale=DH ** -0.5)\
                    .then_inc(sem("proj_out"), 1)
            relu_act(act, 3)
            for s in (2, 3):
                dsa_split_act(act, 2, s)
            for t in range(8):
                proj_ready(act, AT_UK + t)
                dst = (uk_hi, uk_lo)[t // 4]
                nc.scalar.activation(dst[:, t // 2 % 2, (t % 2) * 512:(t % 2) * 512 + 512], ps[:, t % 4, :],
                                     ACT.Copy).then_inc(sem("proj_out"), 1)
            for j in range(8):
                proj_ready(act, AT_K + j)
                nc.scalar.activation(k_t[:, j, :], ps[:, j % 4, :], ACT.Copy).then_inc(sem("proj_out"), 1)
            for j in range(8):
                proj_ready(act, AT_V + j)
                nc.scalar.activation(v_tok[:, j // 2, j % 2 * 512:j % 2 * 512 + 512], ps[:, j % 4, :],
                                     ACT.Copy).then_inc(sem("proj_out"), 1)
            for s in range(4):
                nxt(s)

        def latent_dve(dve, half_):
            dve.wait_ge(sem("root_out"), 6 + half_)
            dve.wait_ge(sem("lat_here"), 2 + 2 * half_)
            for k in range(LC):
                nc.vector.scalar_tensor_tensor(tmp[:, k, :], ps[:, 5, :], qn_g[:, half_, k:k + 1],
                                               latent[:, half_, k, :], ALU.mult, ALU.mult)\
                    .then_inc(sem("lat_scaled"), 1)
            for k in range(LC):
                dve.wait_ge(sem("lat_hi"), half_ * LC + k + 1)
                hi, lo = ((cq_hi, cq_lo), (ckv_hi, ckv_lo))[half_]
                nc.vector.tensor_tensor(lo[:, k, :], tmp[:, k, :], f32(hi[:, k, :]), ALU.subtract)\
                    .then_inc(sem("lat_made"), 1)
            dve.wait_ge(sem("lat_made"), half_ * LC + LC)

        def dsa_in_dve(dve, ch):
            for s in range(4):
                dsa_split_dve(dve, 1, s)
                if s == 2:
                    dve_var(dve, 5, LAT)
            latent_dve(dve, 0)
            dve.wait_ge(sem("small_turned"), 2)
            ch(nc.vector.tensor_copy(kx[:, :, :], ps[:, 7, 0:NB * SMALL].rearrange("p (b n) -> p b n", b=NB)))
            k_x, w_x, k_1 = kx[:, :, 0:DH], kx[:, :, DH:SMALL], kn[:, :, 0:DH]
            ch(nc.vector.tensor_reduce(mean[:, :], k_x, AX_X, ALU.add))
            ch(nc.vector.tensor_scalar(mean[:, :], mean[:, :], 1.0 / DH, None, ALU.mult))
            ch(nc.vector.tensor_tensor(k_x, k_x, along(mean[:, :], DH), ALU.subtract))
            ch(nc.vector.tensor_tensor(k_1, k_x, k_x, ALU.mult))
            ch(nc.vector.tensor_reduce(mean[:, :], k_1, AX_X, ALU.add))
            nc.vector.tensor_scalar(mean[:, :], mean[:, :], 1.0 / DH, EPS, ALU.mult, ALU.add)\
                .then_inc(sem("small_sum"), 1)
            ch(nc.vector.tensor_scalar(w_x, w_x, IH ** -0.5 * DH ** -0.5, None, ALU.mult))
            dve.wait_ge(sem("small_root"), 2)
            ch(nc.vector.tensor_tensor(k_x, k_x, along(mean[:, :], DH), ALU.mult))
            ch(nc.vector.tensor_tensor(k_x, k_x, ln_gb[:, 0, :].unsqueeze(1).to_broadcast([P, NB, DH]), ALU.mult))
            for a in range(2):
                ch(nc.vector.tensor_tensor(kn[:, :, a * DH:(a + 1) * DH], k_x,
                                           ln_gb[:, 1, :].unsqueeze(1).to_broadcast([P, NB, DH]), ALU.add))
            nc.vector.tensor_copy(mask[:, 0, 0:P], causal[:, :]).then_inc(sem("kn_made"), 1)
            dve_var(dve, 6, LAT)
            latent_dve(dve, 1)

        def score_dve(dve, ch, b):
            n, sc = (b + 1) * P, score[b % 2]
            for j in range(IH):
                t = (b - 1) * IH + j
                dve.wait_ge(sem("relu_made"), t + 1)
                w = kx[:, b, DH + j:DH + j + 1]
                if j == 0:
                    ins = nc.vector.tensor_scalar(sc[:, 0:n], relu[:, j, 0:n], w, None, ALU.mult)
                else:
                    ins = nc.vector.scalar_tensor_tensor(sc[:, 0:n], relu[:, j, 0:n], w, sc[:, 0:n],
                                                         ALU.mult, ALU.add)
                ins.then_inc(sem("relu_used"), 1)
                dve.wait_ge(sem("relu_used"), t + 1)
            ch(nc.vector.tensor_tensor(sc[:, b * P:n], sc[:, b * P:n], causal[:, :], ALU.add))

        def top_dve(dve, ch, blocks):
            step = ch.behind if len(blocks) == 2 else ch
            for _ in range(TOPK // 8):
                for b in blocks:
                    step(nc.vector.max(best[:, b % 2, :], score[b % 2][:, 0:(b + 1) * P]))
                for b in blocks:
                    sc = score[b % 2][:, 0:(b + 1) * P]
                    step(nc.vector.match_replace(sc, best[:, b % 2, :], sc, TAKEN))
            for b in blocks:
                step(nc.vector.tensor_scalar(mask[:, b, 0:(b + 1) * P], score[b % 2][:, 0:(b + 1) * P],
                                             2.0 / 3.0 * TAKEN, -BIG, ALU.is_gt, ALU.mult))
            ch.wait()

        UNITS = [(a, b) for a in range(2) for b in range(NB)]
        U = len(UNITS)

        def unit_behind(i, t, lag):
            u = t - lag
            if u < 0:
                if isinstance(i, int) and i == 0:
                    return None
                return i - 1, u + U, i * U + u
            return i, u, i * U + u

        def early(i, u, n):
            return isinstance(i, int) and i * U + u < n

        def att_pe(pe, i, steps=range(U)):
            def scores(i, u, at):
                a, b = UNITS[u]
                lanes, n = slice(64 * a, 64 * a + 64), (b + 1) * P
                if b == 0:
                    pe.wait_ge(sem("qk_staged"), i * 4 + 2 * a + 2)
                if not early(i, u, 4):
                    pe.wait_ge(sem("s_out"), at - 3)
                nc.tensor.matmul(s_bank(u)[:, 0:n],
                                 q_st[lanes, b * P:(b + 1) * P], k_st[lanes, 0:n],
                                 start=True, stop=True).then_inc(sem("s_mm"), 1)

            def turn(i, u, at):
                a, b = UNITS[u]
                pe.wait_ge(sem("p_made"), at + 1)
                if not early(i, u, 2):
                    pe.wait_ge(sem("pt_out"), at - 1)
                for k in range(b + 1):
                    last = nc.tensor.transpose(ps[:, 4 + u % 2, k * P:(k + 1) * P], p_s[:, u % 2, k * P:(k + 1) * P],
                                               ident[:, :])
                last.then_inc(sem("pt_mm"), 1)

            def values(i, u, at):
                a, b = UNITS[u]
                pe.wait_ge(sem("pt_out"), at + 1)
                if not early(i, u, 2):
                    pe.wait_ge(sem("o_ready"), at - 1)
                for k in range(b + 1):
                    v = v_tok[:, k, bass.ds(i * 128, 128)]
                    last = nc.tensor.matmul(ps[:, 6 + u % 2, 0:2 * DH], p_t[:, u % 2, k * P:(k + 1) * P], v,
                                            start=k == 0, stop=k == b)
                last.then_inc(sem("o_mm"), 1)

            for t in steps:
                if t < U:
                    scores(i, t, i * U + t)
                for stage, lag in ((turn, 2), (values, 3)):
                    unit = unit_behind(i, t, lag)
                    if unit and unit[1] < U:
                        stage(*unit)

        def s_bank(u):
            return ps[:, u % 4, :]

        def att_pool(pool, i):
            for a in range(2):
                if isinstance(i, int) and i == 0:
                    pool.wait_ge(sem("proj_out"), AT_V + 8)
                else:
                    pool.wait_ge(sem("s_mm"), i * U - 4 + 4 * a)
                lanes = slice(64 * a, 64 * a + 64)
                for dst, src in ((q_st, q_t), (k_st, k_t)):
                    part = flat(src[lanes, bass.ds(i, 1), :]).rearrange("p (b n) -> p b n", n=P)
                    nc.gpsimd.tensor_tensor(dst[lanes, :].rearrange("p (b n) -> p b n", n=P), part,
                                            ones[lanes, :].unsqueeze(1).to_broadcast([64, NB, P]), ALU.mult)\
                        .then_inc(sem("qk_staged"), 1)

        def att_act(act, i, steps=range(U)):
            for t in steps:
                if t < U:
                    a, b = UNITS[t]
                    n = (b + 1) * P
                    act.wait_ge(sem("nmax_made"), i * U + t + 1)
                    if not early(i, t, 2):
                        act.wait_ge(sem("pt_mm"), i * U + t - 1)
                    nc.scalar.activation(p_s[:, t % 2, 0:n], s_m[:, t % 2, 0:n], ACT.Exp, bias=nmax[:, t:t + 1],
                                         accum_out=psum_p[:, t:t + 1]).then_inc(sem("p_made"), 1)
                unit = unit_behind(i, t, 1)
                if unit and unit[1] < U:
                    j, u, at = unit
                    n = (UNITS[u][1] + 1) * P
                    act.wait_ge(sem("pt_mm"), at + 1)
                    if not early(j, u, 2):
                        act.wait_ge(sem("o_mm"), at - 1)
                    nc.scalar.activation(p_t[:, u % 2, 0:n], ps[:, 4 + u % 2, 0:n], ACT.Copy)\
                        .then_inc(sem("pt_out"), 1)

        def att_dve(dve, ch, i, steps=range(U)):
            for t in steps:
                if t < U:
                    a, b = UNITS[t]
                    n = (b + 1) * P
                    dve.wait_ge(sem("s_mm"), i * U + t + 1)
                    if not early(i, t, 2):
                        dve.wait_ge(sem("p_made"), i * U + t - 1)
                    nc.vector.tensor_tensor(s_m[:, t % 2, 0:n], s_bank(t)[:, 0:n], mask[:, b, 0:n], ALU.add)\
                        .then_inc(sem("s_out"), 1)
                    dve.wait_ge(sem("s_out"), i * U + t + 1)
                    nc.vector.tensor_reduce(nmax[:, t:t + 1], s_m[:, t % 2, 0:n], AX_X, ALU.max, negate=True)\
                        .then_inc(sem("nmax_made"), 1)
                unit = unit_behind(i, t, 3)
                if unit and unit[1] < U:
                    j, u, at = unit
                    a, b = UNITS[u]
                    dve.wait_ge(sem("p_made"), at + 1)
                    nc.vector.reciprocal(rsum[:, u:u + 1], psum_p[:, u:u + 1]).then_inc(sem("rsum_made"), 1)
                    dve.wait_ge(sem("rsum_made"), at + 1)
                    dve.wait_ge(sem("o_mm"), at + 1)
                    nc.vector.tensor_scalar(o_tok[:, b, bass.ds(j * 128 + a * 64, 64)],
                                            ps[:, 6 + u % 2, a * DH:(a + 1) * DH],
                                            rsum[:, u:u + 1], None, ALU.mult).then_inc(sem("o_ready"), 1)

        def o_turn_pe(pe, m, d):
            if d >= 4:
                h_here(pe, m, d - 4)
            for b in range(NB):
                last = nc.tensor.transpose(ps[:, 4 + d % 4, b * P:(b + 1) * P], o_tok[:, b, d * P:(d + 1) * P],
                                           ident[:, :])
            last.then_inc(sem("att_turned"), 1)

        def o_turn_act(act):
            for d in range(8):
                act.wait_ge(sem("att_turned"), d + 1)
                nc.scalar.activation(h_hi[:, d, :], ps[:, 4 + d % 4, :], ACT.Copy).then_inc(sem("h_rounded"), 1)

        def o_turn_dve(dve, m):
            for d in range(8):
                dve.wait_ge(sem("h_rounded"), 8 * m + d + 1)
                nc.vector.tensor_tensor(h_lo[:, d, :], ps[:, 4 + d % 4, :], f32(h_hi[:, d, :]), ALU.subtract)\
                    .then_inc(sem("h_made"), 1)
            h_here(dve, m, DC - 1)

        block = ctx.enter_context(nc.Block())
        N_MISC = 5

        @block.sync
        def _(sp):
            sp.dma_start(row_vec[0:DC, :], c.rearrange("a (k p) -> (a k) p", p=P)).then_inc(vec_in, 16)
            sp.dma_start(row_vec[DC:9 * DC, :], norm_g.rearrange("a b (k p) -> (a b k) p", p=P)).then_inc(vec_in, 16)
            sp.dma_start(row_bias[:, :], ada_b.rearrange("a (k p) -> (a k) p", p=P)).then_inc(vec_in, 16)
            sp.dma_start(row_conv[:, :], gdn_conv_w[0].rearrange("j (k p) -> (j k) p", p=P)).then_inc(vec_in, 16)
            sp.dma_start(row_vec[9 * DC:9 * DC + 1, :], gdn_norm_g).then_inc(vec_in, 16)
            sp.dma_start(row_vec[9 * DC + 1:9 * DC + 1 + LC, :], dsa_q_norm_g[0].rearrange("(k p) -> k p", p=P))\
                .then_inc(vec_in, 16)
            sp.dma_start(row_vec[9 * DC + 1 + LC:VEC, :], dsa_kv_norm_g[0].rearrange("(k p) -> k p", p=P))\
                .then_inc(vec_in, 16)
            load_ada(sp, 0, 0)
            sp.dma_start(x_tok[:, :, :], x[0].rearrange("(b p) d -> p b d", p=P)).then_inc(x_in, 16)
            for jj in range(1, 4):
                load_ada(sp, 0, jj)
            w_in = rows(gdn_w_in[0])

            def gdn_quad(i):
                at = i * 512
                load_quad(sp, i, w_in[:, :, bass.ds(at, 256)], w_in[:, :, bass.ds(at + 256, 256)])

            gdn_quad(0)
            misc = [(ba_raw[:, :, :], w_in[:, :, (QKV + H) * P:]),
                    (dt_b[:, 0, :], gdn_dt_bias[0].partition_broadcast(P)),
                    (dt_b[:, 1, :], gdn_a_log[0].partition_broadcast(P)),
                    (ln_gb[:, 0, :], dsa_kidx_ln_g[0].partition_broadcast(P)),
                    (ln_gb[:, 1, :], dsa_kidx_ln_b[0].partition_broadcast(P))]
            assert len(misc) == N_MISC
            for dst, src in misc:
                sp.dma_start(dst, src).then_inc(sem("misc_in"), 16)

            def gdn_turn(i):
                gdn_quad(i)

            repeat(sp, N_GDN_IN, gdn_turn, first=1)
            w_out = rows(gdn_w_out[0])
            for j in range(2):
                load_quad(sp, Q_GDN_OUT + j, w_out[:, :, j * 512:j * 512 + 256],
                          w_out[:, :, j * 512 + 256:j * 512 + 512])
            ffn_sp(sp, 0)
            dsa_sp(sp)
            ffn_sp(sp, 1)
            for t in range(2 * NB):
                sp.wait_ge(sem("x_out"), t + 1)
                b, cols = t % NB, slice(t // NB * 512, t // NB * 512 + 512)
                sp.dma_start(out[0, b * P:(b + 1) * P, cols], o_out[:, b, cols]).then_inc(sem("stored"), 16)
            sp.wait_ge(sem("stored"), 16 * 2 * NB)

        @block.gpsimd
        def _(pool):
            ch = Chain(pool, sem("pool_chain"))

            def fill(t, value, *cuts):
                ch(nc.gpsimd.memset(t, value))
                for compare, other, base, pattern, channel in cuts:
                    ch(nc.gpsimd.affine_select(out=t, in_=t, compare_op=compare, fill=other, base=base,
                                               pattern=pattern, channel_multiplier=channel))

            fill(ident[:, :], 0.0, (ALU.not_equal, 1.0, 0, [[-1, P]], 1))
            ch(nc.gpsimd.memset(ones[:, :], 1.0))
            nc.gpsimd.memset(half[:, :], -0.5).then_inc(sem("consts"), 1)
            for u in conv_u:
                ch(nc.gpsimd.memset(u[:, 0:3], 0.0))
            fill(upto[:, :], 1.0, (ALU.is_ge, 0.0, 0, [[1, P]], -1))
            fill(mask_l[:, :], 0.0, (ALU.is_gt, BIG, 0, [[-1, P]], 1))
            fill(mask_t[:, :], 0.0, (ALU.is_ge, BIG, 0, [[1, P]], -1))
            fill(causal[:, :], 0.0, (ALU.is_ge, -BIG, 0, [[-1, P]], 1))
            fill(first_l[:, :], -1.0, (ALU.is_equal, 0.0, -1, [[-2, P // 2], [0, 2]], 1),
                 (ALU.is_ge, 0.0, 0, [[0, P // 2], [-1, 2]], 0))
            for lv in range(LEVELS):
                n = 1 << lv
                pairs = P // (2 * n)
                cuts = [(ALU.is_ge, 0.0, 0, [[-2 * n, pairs], [0, 2], [0, n]], 1),
                        (ALU.is_ge, 0.0, n - 1, [[2 * n, pairs], [0, 2], [0, n]], -1),
                        (ALU.is_gt, 0.0, 0, [[0, pairs], [1, 2], [0, n]], 0)]
                fill(first_t[:, :] if lv == 0 else level_t[:, lv, :], -1.0 if lv == 0 else 1.0, *cuts)
            nc.gpsimd.memset(state[:, :, :], 0.0).then_inc(sem("consts"), 1)
            pool_root(pool, 0)
            for s in range(4):
                split(pool, nc.gpsimd, 0, s)
            repeat(pool, 12, lambda j: load_ada(pool, 0, j), first=4)
            pool.wait_ge(sem("qkv_made"), QKV)
            pool_qk_root(pool)
            pool.wait_ge(sem("gate_made"), 1)
            free_for_core(pool)
            core_loop(lambda *a: core_pool(pool, *a), lambda *a: core_start_pool(pool, *a), None, pool)
            for g in range(NG):
                norm_root_pool(pool, g)
            pool_root(pool, 1)
            pool_residual(pool, 0)
            pool_root(pool, 2)
            repeat(pool, 12, lambda j: load_ada(pool, 1, j))
            pool_root(pool, 3)
            pool_residual(pool, 1)
            pool_root(pool, 4)
            pool_root(pool, 5)
            pool.wait_ge(sem("small_sum"), 2)
            nc.gpsimd.tensor_tensor(mean[:, :], mean[:, :], half[:, 0:NB], ALU.pow).then_inc(sem("small_root"), 1)
            pool_root(pool, 6)
            for s in range(4):
                dsa_split_pool(pool, 2, s)
            att_pool(pool, 0)
            pool.wait_ge(sem("qk_staged"), 4)
            for s in range(4):
                split(pool, nc.gpsimd, Q_DSA_OUT, s)
            pool.wait_ge(lo_done, 4 * Q_DSA_OUT + 4)
            repeat(pool, AH // 2, lambda i: att_pool(pool, i), first=1)
            pool_root(pool, 7)
            pool_residual(pool, 2)
            pool_root(pool, 8)
            pool_root(pool, 9)
            pool_residual(pool, 3)

        @block.scalar
        def _(act):
            act.wait_ge(sem("vec_out"), 1)
            nc.scalar.activation(c_act[:, :], vec_t[:, 0:DC], ACT.Silu).then_inc(sem("c_made"), 1)
            for d in range(DC):
                act.wait_ge(sem("x_turned"), d + 1)
                nc.scalar.activation(x_t[:, d, :], ps[:, d % 4, :], ACT.Copy).then_inc(sem("x_here"), 1)
            act_squares(act, 0, x_t, sq_first, wait=lambda d: act.wait_ge(sem("x_here"), d + 1))
            for s in range(4):
                act_split(act, 0, s)
            act_h(act, 0, 0, 0)
            act.wait_ge(sem("misc_in"), 16 * N_MISC)
            nc.scalar.activation(ba_hi[:, :, :], ba_raw[:, :, :], ACT.Copy).then_inc(sem("ba_rounded"), 1)

            def gdn_turn(i):
                for s in range(4):
                    gdn_in_act(act, i, s, True)
                    act_split(act, i + 1, s)
                    gdn_conv_act(act, i, s)

            repeat(act, N_CONV, gdn_turn)
            for i in range(N_CONV, N_GDN_IN):
                for s in range(4):
                    gdn_in_act(act, i, s, False)
                    act_split(act, i + 1, s)
                    if i == N_CONV:
                        if s == 1:
                            act_gates_out(act)
                        act_qk_squares(act, s)
                if i == N_CONV:
                    act_gates(act)
                    act_g_exp(act)
            free_for_core(act)
            core_loop(lambda *a: core_act(act, *a), lambda *a: core_start_act(act, *a),
                      lambda *a: core_end_act(act, *a), act)
            gdn_norm_act(act)
            plain_out(act, "act", Q_GDN_OUT, y_gdn, 0, lambda s: act_split(act, Q_FFN[0], s), sq_gdn)
            act_squares(act, 2, x_t, sq_gdn, wait=lambda d: x_ready(act, 0, d))
            act_h(act, 0, 2, 2)
            ffn_act(act, 0, lambda s: act_split(act, Q_DSA, s))
            act_squares(act, 4, x_t, sq_ffn, wait=lambda d: x_ready(act, 1, d))
            act_h(act, 1, 0, 3)
            dsa_in_act(act)
            dsa_qkv_act(act, lambda s: act_split(act, Q_DSA_OUT, s))
            repeat(act, AH // 2, lambda i: att_act(act, i))
            att_act(act, AH // 2 - 1, range(U, U + 3))
            o_turn_act(act)
            plain_out(act, "act", Q_DSA_OUT, y_dsa, 32, lambda s: act_split(act, Q_FFN[1], s), sq_dsa)
            act_squares(act, 8, x_t, sq_dsa, wait=lambda d: x_ready(act, 2, d))
            act_h(act, 1, 2, 5)
            ffn_act(act, 1, None)
            for t in range(2 * NB):
                act.wait_ge(sem("x_back"), t + 1)
                nc.scalar.activation(o_out[:, t % NB, t // NB * 512:t // NB * 512 + 512], ps[:, t % 4, :], ACT.Copy)\
                    .then_inc(sem("x_out"), 1)

        @block.vector
        def _(dve):
            ch = Chain(dve, sem("dve_chain"))
            dve.wait_ge(sem("vec_turned"), 1)
            nc.vector.tensor_copy(vec_t[:, :], ps[:, 6, 0:VEC]).then_inc(sem("vec_out"), 1)
            dve.wait_ge(sem("vec_out"), 1)
            ch.inc(nc.vector.tensor_copy(bias_t[:, :], ps[:, 6, 128:224]))
            ch(nc.vector.tensor_copy(conv_t[:, :, :], ps[:, 6, 256:352].rearrange("p (j k) -> p j k", j=CONV)))
            dve.wait_ge(sem("c_made"), 1)
            for j in range(4):
                for part in range(4):
                    dve_ada(dve, ch, j, part)
                if j == 2:
                    dve_var(dve, 0)
                dve_ada_out(dve, ch, j)
            dve_coef(dve, ch, 0, [0])
            dve_h(dve, 0, 0, 0, 0)
            dve.wait_ge(sem("ba_rounded"), 1)
            nc.vector.tensor_tensor(ba_lo[:, :, :], ba_raw[:, :, :], f32(ba_hi[:, :, :]), ALU.subtract)\
                .then_inc(sem("ba_split"), 1)
            dve.wait_ge(lo_done, 4)

            def gdn_turn(i):
                for s in range(4):
                    dve_ada_beside(dve, ch, i + 4, s)
                    gdn_conv_dve(dve, ch, i, s)
                    dve_split(dve, i + 1, s)

            repeat(dve, N_CONV, gdn_turn, ch)
            for i in range(N_CONV, N_GDN_IN):
                for s in range(4):
                    dve_ada_beside(dve, ch, i + 4, s)
                    dve_split(dve, i + 1, s)
                if i == N_CONV:
                    dve_gates(dve, ch)
                    dve_sums(dve, ch)
            dve_factors(dve, ch)
            dve_ada_out(dve, ch, 11)
            dve_coef(dve, ch, 0, [1, 2, 3])
            dve.wait_ge(sem("consts"), 2)
            free_for_core(dve)
            core_loop(lambda *a: core_dve(dve, ch, *a), lambda *a: core_start_dve(dve, ch, *a), None, dve, ch)
            gdn_norm_dve(dve)
            plain_out(dve, "dve", Q_GDN_OUT, y_gdn, 0, lambda s: dve_split(dve, Q_FFN[0], s))
            dve.wait_ge(y_out, 8)
            dve_var(dve, 1)
            dve_residual(dve, 1, 0, 1, y_gdn, 0)
            dve_var(dve, 2)
            dve_h(dve, 2, 0, 2, 2)
            ffn_dve(dve, ch, 0, lambda s: dve_split(dve, Q_DSA, s))
            dve_coef(dve, ch, 1, [0, 1, 2, 3])
            dve.wait_ge(y_out, Y_FFN[0] + 24)
            dve_var(dve, 3)
            dve_residual(dve, 3, 0, 3, y_ffn, 1)
            dve_var(dve, 4)
            dve_h(dve, 4, 1, 0, 3)
            dsa_in_dve(dve, ch)
            score_dve(dve, ch, 1)
            top_dve(dve, ch, [1])
            score_dve(dve, ch, 2)
            score_dve(dve, ch, 3)
            top_dve(dve, ch, [2, 3])
            dve.wait_ge(lo_done, 4 * Q_DSA + 12)
            repeat(dve, AH // 2, lambda i: att_dve(dve, ch, i), ch)
            att_dve(dve, ch, AH // 2 - 1, range(U, U + 3))
            dve.wait_ge(lo_done, 4 * Q_DSA_OUT + 4)
            o_turn_dve(dve, 4)
            plain_out(dve, "dve", Q_DSA_OUT, y_dsa, 32, lambda s: dve_split(dve, Q_FFN[1], s))
            dve.wait_ge(y_out, 40)
            dve_var(dve, 7)
            dve_residual(dve, 7, 1, 1, y_dsa, 2)
            dve_var(dve, 8)
            dve_h(dve, 8, 1, 2, 5)
            ffn_dve(dve, ch, 1, None)
            dve.wait_ge(y_out, Y_FFN[1] + 24)
            dve_var(dve, 9)
            dve_residual(dve, 9, 1, 3, y_ffn, 3)

        @block.tensor
        def _(pe):
            pe.wait_ge(sem("consts"), 1)
            pe.wait_ge(vec_in, 16 * 7)
            for at, t, n in ((0, row_vec, VEC), (128, row_bias, 96), (256, row_conv, 96)):
                last = nc.tensor.transpose(ps[:, 6, at:at + n], t[:, :], ident[0:n, 0:n])
            last.then_inc(sem("vec_turned"), 1)
            pe.wait_ge(x_in, 16)
            for d in range(DC):
                if d >= 4:
                    pe.wait_ge(sem("x_here"), d - 3)
                for b in range(NB):
                    last = nc.tensor.transpose(ps[:, d % 4, b * P:(b + 1) * P], x_tok[:, b, d * P:(d + 1) * P],
                                               ident[:, :])
                last.then_inc(sem("x_turned"), 1)
            pe_ada(pe, 0)
            pe_stats(pe, 0, sq_first)
            for j in range(1, 3):
                pe_ada(pe, j)
            pe_bcast(pe, 0)
            pe_ada(pe, 3)

            def gdn_turn(i, sums=False):
                if isinstance(i, int) and i == 0:
                    pe_first_quad(pe, 0, h_hi, h_lo, lambda k: h_here(pe, 0, k))
                    return
                for s in range(4):
                    pe_tile(pe, i, s, h_hi, h_lo, before=lambda: pe.wait_ge(sem("gdn_out_of_ps"), i * 4 - 3 + s))
                    if s == 0:
                        pe_ada(pe, i + 3)
                    if sums and QKV < i * 4 + s <= QKV + 4:
                        pe_qk_sums(pe, i * 4 + s - QKV - 1)
                    if sums and i * 4 + s == QKV + 4:
                        pe_g_sums(pe)
                    if sums and i * 4 + s == QKV:
                        pe_gates(pe)
                    if sums and i * 4 + s == QKV + 1:
                        pe_gates_turn(pe)

            repeat(pe, N_CONV, gdn_turn)
            for i in range(N_CONV, N_GDN_IN):
                gdn_turn(i, sums=True)
            pe_ada(pe, 11)
            pe.wait_ge(sem("consts"), 2)
            pe.wait_ge(sem("gdn_out_of_ps"), 4 * N_GDN_IN)
            core_loop(lambda *a: core_pe(pe, *a), lambda *a: core_start_pe(pe, *a),
                      lambda *a: core_end_pe(pe, *a), pe)
            gdn_norm_pe(pe)
            pe_first_quad(pe, Q_GDN_OUT, h_hi, h_lo, lambda k: h_here(pe, 1, k),
                          after=lambda s: pe_stat_behind(pe, 1, sq_gdn, s))
            for s in range(4):
                pe_tile(pe, Q_GDN_OUT + 1, s, h_hi, h_lo, before=lambda: pe.wait_ge(y_out, s + 1))
                pe_stat_behind(pe, 1, sq_gdn, 4 + s)
            pe_bcast(pe, 1)
            pe_stats(pe, 2, sq_gdn)
            pe_bcast(pe, 2)
            ffn_pe(pe, 0, 2)
            pe_bcast(pe, 3)
            pe_stats(pe, 4, sq_ffn)
            pe_bcast(pe, 4)
            dsa_in_pe(pe, 3)
            indexer_pe(pe, 1)
            indexer_pe(pe, 2)
            dsa_q_pe(pe)
            indexer_pe(pe, 3)
            dsa_uk_pe(pe)
            dsa_keys_pe(pe)
            dsa_v_pe(pe)
            repeat(pe, AH // 2, lambda i: att_pe(pe, i))
            att_pe(pe, AH // 2 - 1, range(U, U + 3))
            pe.wait_ge(sem("o_ready"), 8 * U)
            for d in range(4):
                o_turn_pe(pe, 4, d)
            pe_first_quad(pe, Q_DSA_OUT, h_hi, h_lo, lambda k: h_here(pe, 4, k),
                          after=lambda s: pe_stat_behind(pe, 7, sq_dsa, s),
                          between=lambda k: o_turn_pe(pe, 4, 4 + k))
            for s in range(4):
                pe_tile(pe, Q_DSA_OUT + 1, s, h_hi, h_lo, before=lambda: pe.wait_ge(y_out, 32 + s + 1))
                pe_stat_behind(pe, 7, sq_dsa, 4 + s)
            pe_bcast(pe, 7)
            pe_stats(pe, 8, sq_dsa)
            pe_bcast(pe, 8)
            ffn_pe(pe, 1, 5)
            pe_bcast(pe, 9)
            for t in range(2 * NB):
                if t % NB == 0:
                    for d in range(t, t + 4):
                        x_ready(pe, 3, d)
                if t >= 4:
                    pe.wait_ge(sem("x_out"), t - 3)
                b = t % NB
                for r in range(4):
                    last = nc.tensor.transpose(ps[:, t % 4, r * P:(r + 1) * P],
                                               x_t[:, t // NB * 4 + r, b * P:(b + 1) * P], ident[:, :])
                last.then_inc(sem("x_back"), 1)


_INS = ["x", "c", "ada_w", "ada_b", "norm_g", "ffn_w_in", "ffn_w_out", "gdn_w_in", "gdn_conv_w", "gdn_a_log",
        "gdn_dt_bias", "gdn_norm_g", "gdn_w_out", "dsa_w_in", "dsa_q_norm_g", "dsa_kv_norm_g", "dsa_w_uq",
        "dsa_w_uk", "dsa_w_uv", "dsa_w_qidx", "dsa_kidx_ln_g", "dsa_kidx_ln_b", "dsa_w_out"]
_OUTS = [((1, 512, 1024), "float32")]


def kernel(**inputs):
    import numpy as _np
    import concourse.bacc as _bacc
    from concourse import mybir as _mybir
    from concourse.bass_utils import run_bass_kernel_spmd as _run

    nc = _bacc.Bacc("TRN2", target_bir_lowering=False, num_devices=1)
    arrays, args = {}, []
    for name in _INS:
        a = _np.ascontiguousarray(inputs[name])
        arrays[f"in_{name}_dram"] = a
        args.append(nc.dram_tensor(f"in_{name}_dram", a.shape, _mybir.dt.from_np(a.dtype), kind="ExternalInput").ap())
    for i, (shape, dtype) in enumerate(_OUTS):
        dt = _mybir.dt.from_np(_np.dtype(dtype))
        args.append(nc.dram_tensor(f"out_{i}_dram", shape, dt, kind="ExternalOutput").ap())
    build_trunk(nc, *args)
    r = _run(nc, [arrays], core_ids=[0])
    return r.results[0]["out_0_dram"]
```
